# Optimizing a Trainium2 kernel written in Bass

```python
import numpy as np
import jax
import jax.numpy as jnp
from jax import lax

D_MODEL = 1024
BATCH = 1
SEQ = 512
DEPTH = 1

NSA_HEADS = 8
NSA_KV_GROUPS = 2
NSA_HPG = NSA_HEADS // NSA_KV_GROUPS
NSA_HEAD_DIM = 64
N_NSA_BRANCH = 3
CMP_LEN = 32
CMP_STRIDE = 16
CMP_HIDDEN = 128
SLC_LEN = 64
SLC_TOPK = 16
WINDOW = 512
Q_BLOCK = 128
FORCE_SCORE = 1.0e4

GLA_HEADS = 4
GLA_DK = 64
GLA_DV = 128
GLA_GATE_RANK = 16
GLA_GATE_TAU = 16.0
GLA_CHUNK = 64

ROPE_THETA = 500000.0
ROPE_DIM = NSA_HEAD_DIM // 4

D_FF = (8 * D_MODEL + 3 * 256 - 1) // (3 * 256) * 256

EPS = 1e-6
NEG_INF = -1e30

NSA_Q_COLS = NSA_HEADS * NSA_HEAD_DIM
NSA_KV_COLS = N_NSA_BRANCH * 2 * NSA_KV_GROUPS * NSA_HEAD_DIM
NSA_GATE_COLS = NSA_HEADS * N_NSA_BRANCH
GLA_QK_COLS = GLA_HEADS * GLA_DK
GLA_V_COLS = GLA_HEADS * GLA_DV
MERGE_COLS = 2 * D_MODEL
IN_COLS = NSA_Q_COLS + NSA_KV_COLS + NSA_GATE_COLS + 2 * GLA_QK_COLS + 2 * GLA_V_COLS + GLA_GATE_RANK + MERGE_COLS


def rmsnorm(x, gain):
    xf = x.astype(jnp.float32)
    y = xf * lax.rsqrt(jnp.mean(xf * xf, axis=-1, keepdims=True) + EPS)
    return (y * gain.astype(jnp.float32)).astype(x.dtype)

def partial_rope(x, pos):
    half = ROPE_DIM // 2
    inv_freq = ROPE_THETA ** (-jnp.arange(half, dtype=jnp.float32) / half)
    ang = pos.astype(jnp.float32)[:, None] * inv_freq[None, :]
    cos = jnp.cos(ang).astype(x.dtype)
    sin = jnp.sin(ang).astype(x.dtype)
    x1 = x[..., :half]
    x2 = x[..., half:ROPE_DIM]
    return jnp.concatenate([x1 * cos - x2 * sin, x2 * cos + x1 * sin, x[..., ROPE_DIM:]], axis=-1)

def masked_softmax(scores, mask):
    p = jax.nn.softmax(jnp.where(mask, scores, NEG_INF), axis=-1)
    return p * mask

def compress_blocks(kv, pe, w1, w2):
    b, g, t, d = kv.shape
    ratio = CMP_LEN // CMP_STRIDE
    n_sub = t // CMP_STRIDE
    n_cmp = n_sub - ratio + 1
    sub = kv.reshape(b, g, n_sub, CMP_STRIDE, d)
    blocks = jnp.concatenate([sub[:, :, r:r + n_cmp] for r in range(ratio)], axis=3)
    blocks = (blocks + pe).reshape(b, g, n_cmp, CMP_LEN * d)
    return jax.nn.silu(blocks @ w1) @ w2

def selection_overlap(n_cmp, n_slc):
    c_start = np.arange(n_cmp)[:, None] * CMP_STRIDE
    s_start = np.arange(n_slc)[None, :] * SLC_LEN
    ov = (c_start < s_start + SLC_LEN) & (c_start + CMP_LEN > s_start)
    return jnp.asarray(ov, dtype=jnp.float32)

def nsa_attention(q, k_cmp, v_cmp, k_slc, v_slc, k_win, v_win, gates):
    b, g, hg, t_len, d = q.shape
    pos = jnp.arange(t_len)
    scale = NSA_HEAD_DIM ** -0.5
    q_rot = partial_rope(q, pos)
    k_slc = partial_rope(k_slc, pos)
    k_win = partial_rope(k_win, pos)
    n_cmp = k_cmp.shape[2]
    cmp_end = jnp.arange(n_cmp) * CMP_STRIDE + CMP_LEN - 1
    n_slc = t_len // SLC_LEN
    topk = min(SLC_TOPK, n_slc)
    overlap = selection_overlap(n_cmp, n_slc)
    kb = k_slc.reshape(b, g, n_slc, SLC_LEN, d)
    vb = v_slc.reshape(b, g, n_slc, SLC_LEN, d)
    kw = jnp.pad(k_win, ((0, 0), (0, 0), (WINDOW, 0), (0, 0)))
    vw = jnp.pad(v_win, ((0, 0), (0, 0), (WINDOW, 0), (0, 0)))
    bi = jnp.arange(b)[:, None, None, None]
    gi = jnp.arange(g)[None, :, None, None]
    blk_ids = jnp.arange(n_slc)

    def query_block(i):
        s = i * Q_BLOCK
        t = s + jnp.arange(Q_BLOCK)
        q_raw = lax.dynamic_slice_in_dim(q, s, Q_BLOCK, axis=3) * scale
        q_pos = lax.dynamic_slice_in_dim(q_rot, s, Q_BLOCK, axis=3) * scale
        sc = jnp.einsum('bghqd,bgnd->bghqn', q_raw, k_cmp, preferred_element_type=jnp.float32)
        p_c = masked_softmax(sc, cmp_end[None, :] <= t[:, None])
        o_c = jnp.einsum('bghqn,bgnd->bghqd', p_c.astype(v_cmp.dtype), v_cmp)
        imp = jnp.einsum('bgqn,nj->bgqj', p_c.sum(axis=2), overlap)
        cur = t[:, None] // SLC_LEN
        valid = blk_ids[None, :] * SLC_LEN <= t[:, None]
        forced = (blk_ids[None, :] == 0) | (blk_ids[None, :] == cur) | (blk_ids[None, :] == cur - 1)
        score = jnp.where(valid, jnp.where(forced, FORCE_SCORE, imp), -jnp.inf)
        top_v, idx = lax.top_k(score, topk)
        ks = kb[bi, gi, idx]
        vs = vb[bi, gi, idx].reshape(b, g, Q_BLOCK, topk * SLC_LEN, d)
        ss = jnp.einsum('bghqd,bgqnld->bghqnl', q_pos, ks, preferred_element_type=jnp.float32)
        ss = ss.reshape(b, g, hg, Q_BLOCK, topk * SLC_LEN)
        tok = idx[..., None] * SLC_LEN + jnp.arange(SLC_LEN)
        m_s = (jnp.isfinite(top_v)[..., None] & (tok <= t[None, None, :, None, None]))
        m_s = m_s.reshape(b, g, 1, Q_BLOCK, topk * SLC_LEN)
        p_s = masked_softmax(ss, m_s)
        o_s = jnp.einsum('bghqm,bgqmd->bghqd', p_s.astype(vs.dtype), vs)
        kwin = lax.dynamic_slice_in_dim(kw, s, WINDOW + Q_BLOCK, axis=2)
        vwin = lax.dynamic_slice_in_dim(vw, s, WINDOW + Q_BLOCK, axis=2)
        kpos = s - WINDOW + jnp.arange(WINDOW + Q_BLOCK)
        dist = t[:, None] - kpos[None, :]
        m_w = (kpos[None, :] >= 0) & (dist >= 0) & (dist < WINDOW)
        sw = jnp.einsum('bghqd,bgkd->bghqk', q_pos, kwin, preferred_element_type=jnp.float32)
        p_w = masked_softmax(sw, m_w)
        o_w = jnp.einsum('bghqk,bgkd->bghqd', p_w.astype(vwin.dtype), vwin)
        gt = lax.dynamic_slice_in_dim(gates, s, Q_BLOCK, axis=3)
        return gt[..., 0:1] * o_c + gt[..., 1:2] * o_s + gt[..., 2:3] * o_w

    out = lax.map(query_block, jnp.arange(t_len // Q_BLOCK))
    return out.transpose(1, 0, 4, 2, 3, 5).reshape(b, t_len, g * hg * d)

def gla_chunked(q, k, v, log_a):
    b, h, t_len, dk = q.shape
    dv = v.shape[-1]
    n_chunk = t_len // GLA_CHUNK

    def to_chunks(a):
        return jnp.moveaxis(a.astype(jnp.float32).reshape(b, h, n_chunk, GLA_CHUNK, a.shape[-1]), 2, 0)

    causal = jnp.tril(jnp.ones((GLA_CHUNK, GLA_CHUNK), dtype=bool))

    def step(state, inp):
        qc, kc, vc, gc = inp
        cum = jnp.cumsum(gc, axis=2)
        last = cum[:, :, -1:, :]
        inter = jnp.einsum('bhtd,bhdv->bhtv', qc * jnp.exp(cum), state)
        diff = jnp.where(causal[:, :, None], cum[:, :, :, None, :] - cum[:, :, None, :, :], -jnp.inf)
        attn = jnp.einsum('bhtd,bhsd,bhtsd->bhts', qc, kc, jnp.exp(diff))
        out = inter + jnp.einsum('bhts,bhsv->bhtv', attn, vc)
        state = jnp.exp(last)[:, :, 0, :, None] * state + jnp.einsum('bhsd,bhsv->bhdv', kc * jnp.exp(last - cum), vc)
        return state, out

    s0 = jnp.zeros((b, h, dk, dv), jnp.float32)
    _, o = lax.scan(step, s0, (to_chunks(q), to_chunks(k), to_chunks(v), to_chunks(log_a)))
    return jnp.moveaxis(o, 0, 2).reshape(b, h, t_len, dv)

def split_in_proj(proj):
    widths = [NSA_Q_COLS, NSA_KV_COLS, NSA_GATE_COLS, GLA_QK_COLS, GLA_QK_COLS, GLA_V_COLS,
              GLA_GATE_RANK, GLA_V_COLS, MERGE_COLS]
    cuts = [int(c) for c in np.cumsum(widths)[:-1]]
    return jnp.split(proj, cuts, axis=-1)

def first_inputs(seed: int = 0) -> dict:
    key = jax.random.key(seed)
    ks = jax.random.split(key, 20)
    L = DEPTH

    def nrm(k, shape, scale):
        return jax.random.normal(k, shape, jnp.float32) * scale

    flat_blk = CMP_LEN * NSA_HEAD_DIM
    return {
        'x': nrm(ks[0], (BATCH, SEQ, D_MODEL), 1.0),
        'norm_mix': 1.0 + nrm(ks[1], (L, D_MODEL), 0.02),
        'w_in': nrm(ks[2], (L, D_MODEL, IN_COLS), D_MODEL ** -0.5),
        'cmp_pe_k': nrm(ks[3], (L, CMP_LEN, NSA_HEAD_DIM), 0.1),
        'cmp_pe_v': nrm(ks[4], (L, CMP_LEN, NSA_HEAD_DIM), 0.1),
        'cmp_k_w1': nrm(ks[5], (L, flat_blk, CMP_HIDDEN), flat_blk ** -0.5),
        'cmp_k_w2': nrm(ks[6], (L, CMP_HIDDEN, NSA_HEAD_DIM), CMP_HIDDEN ** -0.5),
        'cmp_v_w1': nrm(ks[7], (L, flat_blk, CMP_HIDDEN), flat_blk ** -0.5),
        'cmp_v_w2': nrm(ks[8], (L, CMP_HIDDEN, NSA_HEAD_DIM), CMP_HIDDEN ** -0.5),
        'gla_gate_w2': nrm(ks[9], (L, GLA_GATE_RANK, GLA_QK_COLS), GLA_GATE_RANK ** -0.5),
        'gla_gate_b': nrm(ks[10], (L, GLA_QK_COLS), 0.1),
        'gla_norm': 1.0 + nrm(ks[11], (L, GLA_DV), 0.02),
        'w_up_nsa': nrm(ks[12], (L, NSA_Q_COLS, D_MODEL), NSA_Q_COLS ** -0.5),
        'w_up_gla': nrm(ks[13], (L, GLA_V_COLS, D_MODEL), GLA_V_COLS ** -0.5),
        'w_out': nrm(ks[14], (L, D_MODEL, D_MODEL), D_MODEL ** -0.5),
        'norm_ffn': 1.0 + nrm(ks[15], (L, D_MODEL), 0.02),
        'w_ffn_gate': nrm(ks[16], (L, D_MODEL, D_FF), D_MODEL ** -0.5),
        'w_ffn_up': nrm(ks[17], (L, D_MODEL, D_FF), D_MODEL ** -0.5),
        'w_ffn_down': nrm(ks[18], (L, D_FF, D_MODEL), D_FF ** -0.5),
        'norm_final': 1.0 + nrm(ks[19], (D_MODEL,), 0.02),
    }

def first_block(x, norm_mix, w_in, cmp_pe_k, cmp_pe_v, cmp_k_w1, cmp_k_w2, cmp_v_w1, cmp_v_w2,
              gla_gate_w2, gla_gate_b, gla_norm, w_up_nsa, w_up_gla, w_out, norm_ffn,
              w_ffn_gate, w_ffn_up, w_ffn_down, norm_final):
    b, t_len, _ = x.shape
    for layer in range(DEPTH):
        h = rmsnorm(x, norm_mix[layer])
        proj = h @ w_in[layer]
        q_nsa, kv_nsa, g_nsa, q_gla, k_gla, v_gla, lr_gla, r_gla, g_merge = split_in_proj(proj)
        q_a = q_nsa.reshape(b, t_len, NSA_KV_GROUPS, NSA_HPG, NSA_HEAD_DIM).transpose(0, 2, 3, 1, 4)
        kv = kv_nsa.reshape(b, t_len, 2 * N_NSA_BRANCH, NSA_KV_GROUPS, NSA_HEAD_DIM).transpose(2, 0, 3, 1, 4)
        k_cmp = compress_blocks(kv[0], cmp_pe_k[layer], cmp_k_w1[layer], cmp_k_w2[layer])
        v_cmp = compress_blocks(kv[1], cmp_pe_v[layer], cmp_v_w1[layer], cmp_v_w2[layer])
        gates_a = jax.nn.sigmoid(g_nsa).reshape(b, t_len, NSA_KV_GROUPS, NSA_HPG, N_NSA_BRANCH).transpose(0, 2, 3, 1, 4)
        o_a = nsa_attention(q_a, k_cmp, v_cmp, kv[2], kv[3], kv[4], kv[5], gates_a)
        log_a = jax.nn.log_sigmoid((lr_gla @ gla_gate_w2[layer] + gla_gate_b[layer]).astype(jnp.float32)) / GLA_GATE_TAU
        heads = lambda a, dh: a.reshape(b, t_len, GLA_HEADS, dh).transpose(0, 2, 1, 3)
        o_b = gla_chunked(heads(q_gla * GLA_DK ** -0.5, GLA_DK), heads(k_gla, GLA_DK),
                          heads(v_gla, GLA_DV), heads(log_a, GLA_DK))
        o_b = rmsnorm(o_b.transpose(0, 2, 1, 3).astype(x.dtype), gla_norm[layer])
        o_b = (o_b * jax.nn.silu(r_gla.reshape(b, t_len, GLA_HEADS, GLA_DV))).reshape(b, t_len, GLA_V_COLS)
        gate_a, gate_b = jnp.split(jax.nn.sigmoid(g_merge), 2, axis=-1)
        merged = gate_a * (o_a @ w_up_nsa[layer]) + gate_b * (o_b @ w_up_gla[layer])
        x = x + merged @ w_out[layer]
        h = rmsnorm(x, norm_ffn[layer])
        x = x + (jax.nn.silu(h @ w_ffn_gate[layer]) * (h @ w_ffn_up[layer])) @ w_ffn_down[layer]
    return rmsnorm(x, norm_final)


DEPTH_2 = 4

N_MIXERS = 3
N_MLA_LAYERS = (DEPTH_2 + 2) // 3
N_SWA_LAYERS = (DEPTH_2 + 1) // 3
N_FOX_LAYERS = DEPTH_2 // 3
BLOCK = 128
NEG_INF_2 = -1e30
RMS_EPS = 1e-6
LN_EPS = 1e-5
DEEPNORM_ALPHA = (2 * DEPTH_2) ** 0.25
DEEPNORM_BETA = (8 * DEPTH_2) ** -0.25

MLA_HEADS = 16
MLA_NOPE_DIM = 64
MLA_ROPE_DIM = 32
MLA_V_DIM = 64
MLA_Q_RANK = 384
MLA_KV_RANK = 256
ROPE_THETA_2 = 10000.0
MLA_WIDTH = MLA_HEADS * MLA_V_DIM
MLA_IN = MLA_Q_RANK + MLA_KV_RANK + MLA_ROPE_DIM + MLA_WIDTH

SWA_Q_HEADS = 16
SWA_KV_HEADS = 4
SWA_GROUP = SWA_Q_HEADS // SWA_KV_HEADS
SWA_HEAD_DIM = 64
WINDOW_2 = 128
SWA_WIDTH = SWA_Q_HEADS * SWA_HEAD_DIM
SWA_KV_WIDTH = SWA_KV_HEADS * SWA_HEAD_DIM
SWA_IN = 2 * SWA_WIDTH + 2 * SWA_KV_WIDTH

FOX_HEADS = 16
FOX_HEAD_DIM = 64
FOX_WIDTH = FOX_HEADS * FOX_HEAD_DIM
FOX_IN = 4 * FOX_WIDTH + FOX_HEADS


def _rmsnorm(x, g):
    xf = x.astype(jnp.float32)
    y = xf * lax.rsqrt(jnp.mean(xf * xf, axis=-1, keepdims=True) + RMS_EPS)
    return (y * g.astype(jnp.float32)).astype(x.dtype)

def _layernorm(x, g, b):
    xf = x.astype(jnp.float32)
    mu = jnp.mean(xf, axis=-1, keepdims=True)
    var = jnp.mean(jnp.square(xf - mu), axis=-1, keepdims=True)
    y = (xf - mu) * lax.rsqrt(var + LN_EPS) * g.astype(jnp.float32) + b.astype(jnp.float32)
    return y.astype(x.dtype)

def _rope_tables(seq, dim):
    inv = ROPE_THETA_2 ** (-jnp.arange(0, dim, 2, dtype=jnp.float32) / dim)
    ang = jnp.arange(seq, dtype=jnp.float32)[:, None] * inv[None, :]
    return jnp.cos(ang), jnp.sin(ang)

def _apply_rope(x, cos, sin):
    x1, x2 = jnp.split(x.astype(jnp.float32), 2, axis=-1)
    return jnp.concatenate([x1 * cos - x2 * sin, x2 * cos + x1 * sin], axis=-1).astype(x.dtype)

def _alibi_slopes(n_heads):
    return 2.0 ** (-8.0 * jnp.arange(1, n_heads + 1, dtype=jnp.float32) / n_heads)

def _dense_causal(q, k, v, scale, cum=None):
    B, S, H, _ = q.shape
    dv = v.shape[-1]
    nb = S // BLOCK
    k_pos = jnp.arange(S)
    cum_t = None if cum is None else jnp.transpose(cum, (0, 2, 1))

    def one_block(n):
        start = n * BLOCK
        q_blk = lax.dynamic_slice_in_dim(q, start, BLOCK, axis=1)
        q_pos = start + jnp.arange(BLOCK)
        s = jnp.einsum('bqhd,bkhd->bhqk', q_blk, k, preferred_element_type=jnp.float32) * scale
        if cum_t is not None:
            c_q = lax.dynamic_slice_in_dim(cum_t, start, BLOCK, axis=2)
            s = s + c_q[..., :, None] - cum_t[:, :, None, :]
        s = jnp.where(k_pos[None, :] <= q_pos[:, None], s, NEG_INF_2)
        p = jax.nn.softmax(s, axis=-1).astype(v.dtype)
        return jnp.einsum('bhqk,bkhd->bqhd', p, v)

    out = lax.map(one_block, jnp.arange(nb))
    return jnp.transpose(out, (1, 0, 2, 3, 4)).reshape(B, S, H, dv)

def _mla_branch(x, w_in, q_norm, w_q_up, kv_norm, w_kv_up, w_out):
    B, S, _ = x.shape
    h = x @ w_in
    c1 = MLA_Q_RANK
    c2 = c1 + MLA_KV_RANK
    c3 = c2 + MLA_ROPE_DIM
    cq, ckv, k_rope, gate = h[..., :c1], h[..., c1:c2], h[..., c2:c3], h[..., c3:]
    q = (_rmsnorm(cq, q_norm) @ w_q_up).reshape(B, S, MLA_HEADS, MLA_NOPE_DIM + MLA_ROPE_DIM)
    kv = (_rmsnorm(ckv, kv_norm) @ w_kv_up).reshape(B, S, MLA_HEADS, MLA_NOPE_DIM + MLA_V_DIM)
    cos, sin = _rope_tables(S, MLA_ROPE_DIM)
    q_rope = _apply_rope(q[..., MLA_NOPE_DIM:], cos[:, None, :], sin[:, None, :])
    k_rope = _apply_rope(k_rope, cos, sin)
    q_full = jnp.concatenate([q[..., :MLA_NOPE_DIM], q_rope], axis=-1)
    k_full = jnp.concatenate(
        [kv[..., :MLA_NOPE_DIM],
         jnp.broadcast_to(k_rope[:, :, None, :], (B, S, MLA_HEADS, MLA_ROPE_DIM))], axis=-1)
    v = kv[..., MLA_NOPE_DIM:]
    scale = (MLA_NOPE_DIM + MLA_ROPE_DIM) ** -0.5
    o = _dense_causal(q_full, k_full, v, scale).reshape(B, S, MLA_WIDTH)
    return (o * jax.nn.silu(gate)) @ w_out

def _swa_branch(x, w_in, sinks, w_out):
    B, S, _ = x.shape
    nb = S // BLOCK
    h = x @ w_in
    c1 = SWA_WIDTH
    c2 = c1 + SWA_KV_WIDTH
    c3 = c2 + SWA_KV_WIDTH
    q = h[..., :c1].reshape(B, nb, BLOCK, SWA_KV_HEADS, SWA_GROUP, SWA_HEAD_DIM)
    k = h[..., c1:c2].reshape(B, nb, BLOCK, SWA_KV_HEADS, SWA_HEAD_DIM)
    v = h[..., c2:c3].reshape(B, nb, BLOCK, SWA_KV_HEADS, SWA_HEAD_DIM)
    gate = h[..., c3:]

    def band(t):
        prev = jnp.concatenate([jnp.zeros_like(t[:, :1]), t[:, :-1]], axis=1)
        return jnp.concatenate([prev, t], axis=2)

    kb, vb = band(k), band(v)
    scale = SWA_HEAD_DIM ** -0.5
    s = jnp.einsum('bnqkgd,bnskd->bnkgqs', q, kb, preferred_element_type=jnp.float32) * scale
    qi = jnp.arange(BLOCK)[:, None]
    kj = jnp.arange(2 * BLOCK)[None, :]
    dist = qi + BLOCK - kj
    key_pos = jnp.arange(nb)[:, None, None] * BLOCK - BLOCK + kj[None]
    valid = (dist >= 0) & (dist < WINDOW_2) & (key_pos >= 0)
    slopes = _alibi_slopes(SWA_Q_HEADS).reshape(SWA_KV_HEADS, SWA_GROUP)
    s = s - slopes[:, :, None, None] * dist.astype(jnp.float32)
    s = jnp.where(valid[None, :, None, None], s, NEG_INF_2)
    sink = sinks.astype(jnp.float32).reshape(SWA_KV_HEADS, SWA_GROUP)[:, :, None, None]
    m = jnp.maximum(jnp.max(s, axis=-1, keepdims=True), sink)
    p = jnp.exp(s - m)
    p = (p / (jnp.sum(p, axis=-1, keepdims=True) + jnp.exp(sink - m))).astype(vb.dtype)
    o = jnp.einsum('bnkgqs,bnskd->bnqkgd', p, vb).reshape(B, S, SWA_WIDTH)
    return (o * jax.nn.silu(gate)) @ w_out

def _fox_branch(x, w_in, b_f, w_out):
    B, S, _ = x.shape
    h = x @ w_in
    W = FOX_WIDTH
    q = h[..., :W].reshape(B, S, FOX_HEADS, FOX_HEAD_DIM)
    k = h[..., W:2 * W].reshape(B, S, FOX_HEADS, FOX_HEAD_DIM)
    v = h[..., 2 * W:3 * W].reshape(B, S, FOX_HEADS, FOX_HEAD_DIM)
    f_logit = h[..., 3 * W:3 * W + FOX_HEADS]
    gate = h[..., 3 * W + FOX_HEADS:]
    log_f = jax.nn.log_sigmoid(f_logit.astype(jnp.float32) + b_f.astype(jnp.float32))
    cum = jnp.cumsum(log_f, axis=1)
    o = _dense_causal(q, k, v, FOX_HEAD_DIM ** -0.5, cum).reshape(B, S, W)
    return (o * jax.nn.silu(gate)) @ w_out

def second_inputs(seed: int = 0) -> dict:
    key = jax.random.key(seed)
    ks = jax.random.split(key, 16)

    def nrm(k, shape, scale):
        return jax.random.normal(k, shape, jnp.float32) * scale

    return {
        "x": nrm(ks[0], (BATCH, SEQ, D_MODEL), 1.0),
        "ln_g": 1.0 + nrm(ks[1], (DEPTH_2, D_MODEL), 0.02),
        "ln_b": nrm(ks[2], (DEPTH_2, D_MODEL), 0.02),
        "mla_w_in": nrm(ks[3], (N_MLA_LAYERS, D_MODEL, MLA_IN), D_MODEL ** -0.5),
        "mla_q_norm": 1.0 + nrm(ks[4], (N_MLA_LAYERS, MLA_Q_RANK), 0.02),
        "mla_w_q_up": nrm(ks[5], (N_MLA_LAYERS, MLA_Q_RANK, MLA_HEADS * (MLA_NOPE_DIM + MLA_ROPE_DIM)), MLA_Q_RANK ** -0.5),
        "mla_kv_norm": 1.0 + nrm(ks[6], (N_MLA_LAYERS, MLA_KV_RANK), 0.02),
        "mla_w_kv_up": nrm(ks[7], (N_MLA_LAYERS, MLA_KV_RANK, MLA_HEADS * (MLA_NOPE_DIM + MLA_V_DIM)), MLA_KV_RANK ** -0.5),
        "mla_w_out": nrm(ks[8], (N_MLA_LAYERS, MLA_WIDTH, D_MODEL), DEEPNORM_BETA * MLA_WIDTH ** -0.5),
        "swa_w_in": nrm(ks[9], (N_SWA_LAYERS, D_MODEL, SWA_IN), D_MODEL ** -0.5),
        "swa_sinks": nrm(ks[10], (N_SWA_LAYERS, SWA_Q_HEADS), 0.5),
        "swa_w_out": nrm(ks[11], (N_SWA_LAYERS, SWA_WIDTH, D_MODEL), DEEPNORM_BETA * SWA_WIDTH ** -0.5),
        "fox_w_in": nrm(ks[12], (N_FOX_LAYERS, D_MODEL, FOX_IN), D_MODEL ** -0.5),
        "fox_b_f": jax.random.uniform(ks[13], (N_FOX_LAYERS, FOX_HEADS), jnp.float32, 1.0, 4.0),
        "fox_w_out": nrm(ks[14], (N_FOX_LAYERS, FOX_WIDTH, D_MODEL), DEEPNORM_BETA * FOX_WIDTH ** -0.5),
    }

def second_block(x, ln_g, ln_b, mla_w_in, mla_q_norm, mla_w_q_up, mla_kv_norm, mla_w_kv_up, mla_w_out,
              swa_w_in, swa_sinks, swa_w_out, fox_w_in, fox_b_f, fox_w_out):
    for i in range(DEPTH_2):
        j = i // N_MIXERS
        kind = i % N_MIXERS
        if kind == 0:
            y = _mla_branch(x, mla_w_in[j], mla_q_norm[j], mla_w_q_up[j], mla_kv_norm[j],
                            mla_w_kv_up[j], mla_w_out[j])
        elif kind == 1:
            y = _swa_branch(x, swa_w_in[j], swa_sinks[j], swa_w_out[j])
        else:
            y = _fox_branch(x, fox_w_in[j], fox_b_f[j], fox_w_out[j])
        x = _layernorm(DEEPNORM_ALPHA * x + y, ln_g[i], ln_b[i])
    return x


def setup_inputs(seed=0):
    out = dict(first_inputs(seed))
    for name, value in second_inputs(seed + 1).items():
        if name != "x":
            out[name + "_2"] = value
    return out


def reference(
    x, norm_mix, w_in, cmp_pe_k, cmp_pe_v, cmp_k_w1, cmp_k_w2, cmp_v_w1, cmp_v_w2, gla_gate_w2,
    gla_gate_b, gla_norm, w_up_nsa, w_up_gla, w_out, norm_ffn, w_ffn_gate, w_ffn_up, w_ffn_down,
    norm_final, ln_g_2, ln_b_2, mla_w_in_2, mla_q_norm_2, mla_w_q_up_2, mla_kv_norm_2,
    mla_w_kv_up_2, mla_w_out_2, swa_w_in_2, swa_sinks_2, swa_w_out_2, fox_w_in_2, fox_b_f_2,
    fox_w_out_2,
):
    x = first_block(
        x, norm_mix, w_in, cmp_pe_k, cmp_pe_v, cmp_k_w1, cmp_k_w2, cmp_v_w1, cmp_v_w2,
        gla_gate_w2, gla_gate_b, gla_norm, w_up_nsa, w_up_gla, w_out, norm_ffn, w_ffn_gate,
        w_ffn_up, w_ffn_down, norm_final,
    )
    return second_block(
        x, ln_g_2, ln_b_2, mla_w_in_2, mla_q_norm_2, mla_w_q_up_2, mla_kv_norm_2, mla_w_kv_up_2,
        mla_w_out_2, swa_w_in_2, swa_sinks_2, swa_w_out_2, fox_w_in_2, fox_b_f_2, fox_w_out_2,
    )


_drawn_inputs = setup_inputs


def setup_inputs(seed=0):
    import zlib

    import numpy as np

    out = dict(_drawn_inputs(seed))
    spreads = {}
    factors = {'norm_mix': 3.541,
     'cmp_pe_k': 8.0,
     'cmp_pe_v': 3.364,
     'gla_gate_b': 3.56,
     'gla_norm': 7.549,
     'norm_ffn': 4.023,
     'norm_final': 2.828,
     'mla_q_norm_2': 8.0,
     'mla_kv_norm_2': 8.0,
     'swa_sinks_2': 8.0}
    for name, (base, spread) in spreads.items():
        noise = np.random.default_rng([zlib.crc32(name.encode()), seed]).standard_normal(out[name].shape)
        drawn = base * np.exp(spread * noise) if base else spread * noise
        out[name] = jnp.asarray(drawn.astype(out[name].dtype))
    for name, factor in factors.items():
        out[name] = (out[name] * factor).astype(out[name].dtype)
    return out
```

```python
import numpy as np
import concourse.bass as bass
from concourse import mybir
from contextlib import ExitStack

F = mybir.dt.float32
R = mybir.dt.float32r
B16 = mybir.dt.bfloat16
I32 = mybir.dt.int32
ALU = mybir.AluOpType
ACT = mybir.ActivationFunctionType
AX = mybir.AxisListType

T = 512
D = 1024
NT = 4
DFF = 2816
RAW_SLOTS = 4
W_SLOTS = 5
LOOK = 3
PIECE = 1024
OFF = (0, 128, 384, 768)
ALPHA = 8.0 ** 0.25
C_ID, C_MASK, C_DIST, C_NROPE, C_MROPE, C_SEL, C_GLA, C_END = 0, 128, 256, 512, 576, 704, 720, 1744


class Queue:

    def __init__(self, sem):
        self.sem, self.n, self.items = sem, 0, []

    def do(self, after, f, *a, **k):
        self.n += 1
        self.items.append((after, f, a, k, (self.sem, 1)))
        return (self.sem, self.n)

    def quiet(self, after, f, *a, **k):
        self.items.append((after, f, a, k, None))

    def wait(self, *after):
        self.items.append((list(after), None, (), {}, None))

    def dma(self, after, lane, f, *a):
        lane[1] += 16
        self.items.append((after, f, a, {}, (lane[0], 16)))
        return (lane[0], lane[1])

    def slot(self):
        own = []
        self.items.append(own)
        return own

    def last(self):
        return (self.sem, self.n)

    def play(self, eng):
        seen, flat = {}, []
        for it in self.items:
            flat += it if isinstance(it, list) else [it]
        for after, f, a, k, inc in flat:
            stack = [after]
            while stack:
                t = stack.pop(0)
                if t is None:
                    continue
                if isinstance(t, list):
                    stack = t + stack
                    continue
                sem, v = t
                if v > seen.get(sem.name, 0):
                    eng.wait_ge(sem, v)
                    seen[sem.name] = v
            if f is not None:
                ins = f(*a, **k)
                if inc is not None:
                    ins.then_inc(inc[0], inc[1])


class Bank:

    def __init__(self, t):
        self.t, self.free, self.tok = t, None, None


def program(nc, A, out, stages=("mix", "ffn", "mla0", "swa", "fox", "mla1")):
    top = ExitStack()
    with top:
        names = {}

        def sem(name):
            return top.enter_context(nc.semaphore(name))

        def alloc(cm, name, shape, dt=F):
            names[name] = names.get(name, 0) + 1
            return cm.enter_context(nc.sbuf_tensor(f"{name}_{names[name]}", shape, dt))

        PE, AC, VE, PO = (Queue(sem(n)) for n in ("s_pe", "s_act", "s_dve", "s_pool"))
        SP = Queue(None)
        pe, act, ve, po = nc.tensor, nc.scalar, nc.vector, nc.gpsimd
        mult, add, sub = ALU.mult, ALU.add, ALU.subtract

        X = alloc(top, "X", [128, NT, D])
        XT = (alloc(top, "XTh", [128, 8, T], R), alloc(top, "XTl", [128, 8, T], R))
        Wr = [alloc(top, "Wr", [128, PIECE]) for i in range(RAW_SLOTS)]
        Wh = [alloc(top, "Wh", [128, PIECE], R) for i in range(W_SLOTS)]
        Wl = [alloc(top, "Wl", [128, PIECE], R) for i in range(W_SLOTS)]
        CST = alloc(top, "CST", [128, C_GLA])
        IDB = alloc(top, "IDB", [128, 128], B16)
        MKB = alloc(top, "MKB", [128, 128], B16)
        SLB = alloc(top, "SLB", [128, 16], B16)
        GB = alloc(top, "GB", [128, 2, D])
        ST = alloc(top, "ST", [128, NT, 24])

        all_banks = [Bank(top.enter_context(nc.psum_tensor(f"PS{i}", [128, 512], F))) for i in range(8)]
        idle = list(all_banks)

        def take():
            return idle.pop(0)

        def give(b, *toks):
            b.free = list(toks)
            idle.append(b)

        IDN = CST[:, C_ID:C_ID + 128]

        def lane(name):
            return [sem(name), 0]

        def tile(i):
            return slice(128 * i, 128 * i + 128)

        k_cst = AC.dma([], lane("l_cst"), act.dma_start, CST[:, :], A["cst"][:, 0:C_GLA])
        k_x = AC.dma([], lane("l_x"), act.dma_start, X[:, :, :], A["x"].rearrange("o (i p) d -> p (o i) d", p=128))
        VE.do([k_cst], ve.tensor_copy, IDB[:, :], IDN)
        VE.do([k_cst], ve.tensor_copy, SLB[:, :], CST[:, C_SEL:C_SEL + 16])
        k_idb = VE.do([k_cst], ve.tensor_copy, MKB[:, :], CST[:, C_MASK:C_MASK + 128])

        l_g = [lane("l_g0"), lane("l_g1")]
        gb_free = [None]

        def gains(*rs):
            return [AC.dma([gb_free[0]], l_g[j], act.dma_start, GB[:, j, :],
                           r.rearrange("(o n) -> o n", o=1).broadcast_to([128, D])) for j, r in enumerate(rs)]

        l_raw = [lane(f"l_raw{i}") for i in range(RAW_SLOTS)]
        s_hi, s_lo = sem("s_hi"), sem("s_lo")
        released, places = {}, []

        class Piece:
            def __init__(self, i, n, p=128):
                self.ready, self.i, self.n, self.p = (s_lo, i + 1), i, n, p
                self.t = (Wh[i % W_SLOTS], Wl[i % W_SLOTS])

            def __call__(self, a, c0, c1, p0=0, p1=128):
                return [t[p0:p1, a * self.n + c0:a * self.n + c1] for t in self.t]

        def weight(srcs, n, rows=None, p=128):
            i = len(places)
            places.append(AC.slot())
            raw, lan = Wr[i % RAW_SLOTS], l_raw[i % RAW_SLOTS]
            a = srcs[0][0].shape[1]
            for src, c, p0 in srcs:
                pp, m = src.shape[0], src.shape[2]
                dst = raw[p0:p0 + pp, 0:a * n].rearrange("p (a n) -> p a n", n=n)[:, :, c:c + m]
                tok = SP.dma([(s_lo, i - RAW_SLOTS + 1)] if i >= RAW_SLOTS else [], lan, nc.sync.dma_start, dst, src)
            used = a * n
            free = [released[i - W_SLOTS]] if i >= W_SLOTS else []
            h, l = Wh[i % W_SLOTS], Wl[i % W_SLOTS]
            places[max(i - LOOK, 0)].append(([tok] + free, act.copy, (h[0:p, 0:used], raw[0:p, 0:used]), {}, (s_hi, 1)))
            PO.items.append(([tok, (s_hi, i + 1)] + free, po.tensor_tensor,
                             (l[0:p, 0:used], raw[0:p, 0:used], h[0:p, 0:used].bitcast(F), sub), {}, (s_lo, 1)))
            return Piece(i, rows if rows else n)

        def mm3(o, l, r, start, stop, after, sig=False):
            PE.quiet(after, pe.matmul, o, l[0], r[1], start=start, stop=False)
            PE.quiet([], pe.matmul, o, l[1], r[0], start=False, stop=False)
            f = PE.do if stop or sig else PE.quiet
            return f([], pe.matmul, o, l[0], r[0], start=False, stop=stop)

        def pair(p, *ix):
            return [t[ix] for t in p]

        def by_rows(w):
            return w.rearrange("(a p) n -> p a n", p=128)

        ALL = slice(None)

        def proj_T(src, rhs, rdy, kts=None, o=None, start=True, stop=True):
            n = src.shape[2]
            w = weight([(src, 0, 0)], n)
            b = o or take()
            kts = src.shape[1]
            for a in range(kts):
                tok = mm3(b.t[0:n, :], w(a, 0, n), pair(rhs, ALL, a, ALL), start and a == 0, stop and a == kts - 1,
                          [w.ready, b.free, rdy], sig=a == kts - 1)
            released[w.i] = b.tok = tok
            return b

        def proj_N(pieces, n, lhs, rdy):
            bs = [take() for _ in range(NT)]
            kts, a0 = sum(k for _, k in pieces), 0
            for src, k in pieces:
                w = weight([(src, 0, 0)], src.shape[2], rows=n)
                for i in range(NT):
                    for a in range(k):
                        tok = mm3(bs[i].t[:, 0:n], pair(lhs, ALL, a0 + a, tile(i)), w(a, 0, n), a0 + a == 0,
                                  a0 + a == kts - 1, [w.ready, bs[i].free, rdy], sig=i == NT - 1 and a == k - 1)
                        if tok:
                            released[w.i] = bs[i].tok = tok
                a0 += k
            return bs

        def cut(src, n):
            k, per = src.shape[1], max(1, PIECE // n)
            return [(src[:, j:min(j + per, k), :], min(per, k - j)) for j in range(0, k, per)]

        def outproj(src, lhs, rdy, alpha):
            bs = [[take(), take()] for _ in range(NT)]
            kts = src.shape[1]
            for a in range(kts):
                w = weight([(src[:, a:a + 1, :], 0, 0)], D)
                for i in range(NT):
                    for c in range(2):
                        b = bs[i][c]
                        tok = mm3(b.t[:, :], pair(lhs, ALL, a, tile(i)), w(0, 512 * c, 512 * c + 512),
                                  a == 0, a == kts - 1, [w.ready, b.free, rdy], sig=i == NT - 1 and c == 1)
                        if tok:
                            released[w.i] = b.tok = tok
            done = []
            for i in range(NT):
                for c in range(2):
                    b, xs = bs[i][c], X[:, i, 512 * c:512 * c + 512]
                    t = VE.do([b.tok, k_x, VE.last()], ve.scalar_tensor_tensor, xs, xs, alpha, b.t[:, :], mult, add)
                    give(b, t)
                done.append(t)
            return done

        def split(pr, src, *after):
            a = AC.do(list(after), act.copy, pr[0], src)
            return VE.do([a, list(after)], ve.tensor_tensor, pr[1], src, pr[0].bitcast(F), sub)

        def rsqrt(dst, src, scale, eps, v, q, *after):
            a = VE.do(list(after), ve.tensor_scalar, v, src, scale, eps, mult, add)
            a = AC.do([a], act.activation, q, v, ACT.Ln)
            a = AC.do([a], act.activation, dst, q, ACT.Exp, scale=-0.5)
            a = VE.do([a], ve.tensor_tensor, q, dst, dst, mult)
            a = VE.do([a], ve.tensor_tensor, q, q, v, mult)
            a = VE.do([a], ve.tensor_scalar, q, q, -0.5, 1.5, mult, add)
            return VE.do([a], ve.tensor_tensor, dst, dst, q, mult)

        def transposes(blocks, b, after):
            after = [after, b.free, k_cst]
            for s, c in blocks:
                p, m = s.shape[0], int(np.prod(s.shape[1:]))
                f = PE.do if c == blocks[-1][1] else PE.quiet
                tok = f(after, pe.transpose, b.t[0:m, c:c + p], s, IDN[0:p, 0:p])
            return tok

        def to_XT(src, i, *after):
            toks = []
            for c in range(2):
                b = take()
                t = transposes([(src[:, tile(4 * c + j)], 128 * j) for j in range(4)], b, list(after))
                ps = b.t[:, :].rearrange("p (j t) -> p j t", j=4)
                v = split(pair(XT, ALL, slice(4 * c, 4 * c + 4), tile(i)), ps, t)
                give(b, v)
                toks.append(v)
            return toks

        def rms_norm(gt, ready, cm, to_x=False):
            junk = alloc(cm, "junk", [128, D])
            H = alloc(cm, "H", [128, 2, D])
            toks, used = [], [None, None]
            for i in range(NT):
                st = ST[:, i, :]
                a = AC.do([ready[i] if ready else k_x, AC.last()], act.activation, junk[:, :], X[:, i, :], ACT.Square,
                          accum_out=st[:, 0:1])
                r = rsqrt(st[:, 1:2], st[:, 0:1], 1.0 / D, 1e-6, st[:, 2:3], st[:, 3:4], a)
                h = X[:, i, :] if to_x else H[:, i % 2, :]
                v = VE.do([r, gt, used[i % 2]], ve.scalar_tensor_tensor, h, X[:, i, :], st[:, 1:2], GB[:, 0, :], mult, mult)
                toks.append(to_XT(h, i, v))
                used[i % 2] = PE.last()
            gb_free[0] = VE.last()
            return toks

        def layer_norm(gt, ready, transposed=True):
            toks = []
            for i in range(NT):
                st, x = ST[:, i, :], X[:, i, :]
                for c in range(2):
                    v = VE.do([ready[i]], ve.bn_stats, st[:, 6 * c:6 * c + 6], X[:, i, 512 * c:512 * c + 512])
                v = VE.do([v], ve.bn_aggr, st[:, 12:14], st[:, 0:12])
                r = rsqrt(st[:, 14:15], st[:, 13:14], 1.0, 1e-5, st[:, 15:16], st[:, 16:17], v)
                v = VE.do([v, gt], ve.scalar_tensor_tensor, x, x, st[:, 12:13], GB[:, 0, :], sub, mult)
                v = VE.do([v, r], ve.scalar_tensor_tensor, x, x, st[:, 14:15], GB[:, 1, :], mult, add)
                toks.append(to_XT(x, i, v) if transposed else v)
            gb_free[0] = VE.last()
            return toks

        def fence():
            f = [PE.last(), AC.last(), VE.last()]
            for q in (PE, AC, VE):
                q.wait(*f)

        def rope(x1, x2, o1, o2, cos, sin, t1, t2, *after):
            VE.do([list(after), k_cst], ve.tensor_tensor, t1, x2, sin, mult)
            a = VE.do([], ve.tensor_tensor, t2, x1, sin, mult)
            VE.do([a], ve.tensor_tensor, o1, x1, cos, mult)
            a = VE.do([a], ve.tensor_tensor, o2, x2, cos, mult)
            VE.do([a], ve.tensor_tensor, o1, o1, t1, sub)
            return VE.do([a], ve.tensor_tensor, o2, o2, t2, add)

        class Attention:
            def __init__(self, cm):
                self.P = [alloc(cm, "P", [128, 1280]) for i in range(2)]
                self.PT = [alloc(cm, "PT", [128, 1280]) for i in range(2)]
                self.sm = [alloc(cm, "sm", [128, 20]) for i in range(2)]
                self.p_free, self.t_free, self.n, self.m, self.flip = [None, None], [None, None], 0, 0, 0

            def scores(self, q, k, rdy, extra=(), gate=None):
                s = self.n % 2
                self.n += 1
                P, sm = self.P[s], self.sm[s]
                toks = []
                for i in range(NT):
                    n = (i + 1) * 128
                    b = take()
                    PE.quiet([b.free, rdy], pe.matmul, b.t[:, 0:n], q(i), k(n), start=True, stop=False)
                    for l, r in extra:
                        PE.quiet([], pe.matmul, b.t[:, 0:n], l(i), r(n), start=False, stop=False)
                    t = PE.do([k_idb], pe.matmul, b.t[:, n - 128:n], IDB[:, :], MKB[:, :], start=False, stop=True)
                    v = VE.do([t, self.p_free[s]], ve.reduce_max, sm[:, i:i + 1], b.t[:, 0:n], AX.X, negate=True)
                    a = AC.do([v, self.p_free[s]], act.activation, P[:, OFF[i]:OFF[i] + n], b.t[:, 0:n], ACT.Exp,
                              bias=sm[:, i:i + 1], accum_out=sm[:, 4 + i:5 + i])
                    give(b, a)
                    toks.append(a)
                v = VE.do([toks], ve.reciprocal, sm[:, 8:12], sm[:, 4:8])
                if gate is not None:
                    v = VE.do([v], ve.tensor_tensor, sm[:, 8:12], sm[:, 8:12], gate, mult)
                for i in range(NT):
                    n = (i + 1) * 128
                    p = P[:, OFF[i]:OFF[i] + n]
                    v2 = VE.do([v], ve.tensor_scalar, p, p, sm[:, 8 + i:9 + i], None, mult)
                return s, v2

            def evacuate(self, dst, src, after):
                self.flip ^= 1
                if self.flip:
                    return AC.do(after, act.copy, dst, src)
                return VE.do(after, ve.tensor_copy, dst, src)

            def values(self, ps, v, o, rdy, start=True, stop=True):
                s, done = ps
                m = self.m % 2
                self.m += 1
                P, PT = self.P[s], self.PT[m]
                evs = []
                for js, base in (((0,), 0), ((1, 3), 512), ((2,), 1024)):
                    b = take()
                    cols = [(i, j) for j in js for i in range(j, NT)]
                    n = 128 * len(cols)
                    t = transposes([(P[:, OFF[i] + 128 * j:OFF[i] + 128 * j + 128], 128 * c)
                                    for c, (i, j) in enumerate(cols)], b, done)
                    e = self.evacuate(PT[:, base:base + n], b.t[:, 0:n], [t, self.t_free[m]])
                    give(b, e)
                    evs.append(e)
                self.p_free[s] = PE.last()
                src = (0, 512, 1024, 896)
                for j in range(NT):
                    f = PE.quiet if j < NT - 1 else PE.do
                    tok = f([evs, rdy], pe.matmul, o[:, 128 * j:512], v(j), PT[:, src[j]:src[j] + 512 - 128 * j],
                            start=start and j == 0, stop=stop and j == NT - 1)
                self.t_free[m] = tok
                return tok

        def half(h):
            return slice(64 * (h % 2), 64 * (h % 2) + 64)

        def gated(ob, f, GT, after):
            v = VE.do(after, ve.tensor_tensor, GT[:, f, :], ob.t[:, :], GT[:, f, :], mult)
            give(ob, v)
            return split(pair(XT, ALL, f, ALL), GT[:, f, :], v)

        def ffn(ready, cm):
            wg, wu, wd = by_rows(A["w_ffn_gate"][0]), by_rows(A["w_ffn_up"][0]), by_rows(A["w_ffn_down"][0])
            HT = [(alloc(cm, "HTh", [128, 8, T], R), alloc(cm, "HTl", [128, 8, T], R)) for _ in range(2)]
            sg = [alloc(cm, "sg", [128, T]) for _ in range(2)]
            hf = [alloc(cm, "hf", [128, T]) for _ in range(2)]
            f0, n, used = 0, 0, [None, None]
            free = [None, None]
            for g, cnt in enumerate((8, 7, 7)):
                H, toks = HT[g % 2], []
                for f in range(cnt):
                    c = slice(128 * (f0 + f), 128 * (f0 + f) + 128)
                    bg = proj_T(wg[:, :, c], XT, ready)
                    bu = proj_T(wu[:, :, c], XT, ready)
                    s = n % 2
                    n += 1
                    a = AC.do([bg.tok, used[s]], act.activation, sg[s][:, :], bg.t[:, :], ACT.Silu)
                    give(bg, a)
                    v = VE.do([a, bu.tok, used[s]], ve.tensor_tensor, hf[s][:, :], sg[s][:, :], bu.t[:, :], mult)
                    give(bu, v)
                    toks.append(split(pair(H, ALL, f, ALL), hf[s][:, :], v, free[g % 2]))
                    used[s] = toks[-1]
                done = outproj(wd[:, f0:f0 + cnt, :], H, toks, 1.0)
                free[g % 2] = PE.last()
                f0 += cnt
            return done

        def mla(li, ready, cm):
            w_in = by_rows(A["mla_w_in_2"][li])
            CQ = [alloc(cm, "CQ", [128, 3, T], R) for h in "hl"]
            CK = [alloc(cm, "CK", [128, 2, T], R) for h in "hl"]
            GT = alloc(cm, "GT", [128, 8, T])
            QT = [alloc(cm, "QT", [96, T]) for i in range(2)]
            KT = [alloc(cm, "KT", [96, T]) for i in range(2)]
            QRT = alloc(cm, "QRT", [128, NT, T])
            V = alloc(cm, "V", [128, NT, D])
            cos = lambda i: CST[:, C_MROPE + 16 * i:C_MROPE + 16 * i + 16]
            sin = lambda i: CST[:, C_MROPE + 64 + 16 * i:C_MROPE + 64 + 16 * i + 16]
            scale = 96.0 ** -0.5
            with ExitStack() as c1:
                QN, KN = alloc(c1, "QN", [128, 384]), alloc(c1, "KN", [128, 256])
                CN = alloc(c1, "CN", [128, NT, 704])
                scr = alloc(c1, "scr", [128, 384])
                tm = alloc(c1, "tm", [128, 32])
                ln = lane(f"l_n{li}"), lane(f"l_m{li}")
                k_n = [AC.dma([], ln[0], act.dma_start, QN[:, :], A["mla_q_norm_2"][li:li + 1, :].broadcast_to([128, 384])),
                       AC.dma([], ln[1], act.dma_start, KN[:, :], A["mla_kv_norm_2"][li:li + 1, :].broadcast_to([128, 256]))]
                got = [[] for _ in range(NT)]
                for c0, n in ((0, 512), (512, 160)):
                    bs = proj_N(cut(w_in[:, :, c0:c0 + n], n), n, XT, ready)
                    for i, b in enumerate(bs):
                        got[i].append(VE.do([b.tok], ve.tensor_copy, CN[:, i, c0:c0 + n], b.t[:, 0:n]))
                        give(b, got[i][-1])
                tr = []
                for i in range(NT):
                    st = ST[:, i, :]
                    for c0, n, j, g in ((0, 384, 0, QN), (384, 256, 4, KN)):
                        x = CN[:, i, c0:c0 + n]
                        a = AC.do([got[i], AC.last()], act.activation, scr[:, 0:n], x, ACT.Square, accum_out=st[:, j:j + 1])
                        r = rsqrt(st[:, j + 1:j + 2], st[:, j:j + 1], 1.0 / n, 1e-6, st[:, j + 2:j + 3], st[:, j + 3:j + 4], a)
                        v = VE.do([r, k_n], ve.scalar_tensor_tensor, x, x, st[:, j + 1:j + 2], g[:, :], mult, mult)
                    r = rope(CN[:, i, 640:656], CN[:, i, 656:672], CN[:, i, 672:688], CN[:, i, 688:704],
                             cos(i), sin(i), tm[:, 0:16], tm[:, 16:32], v)
                    tr.append([v, r])
                tok_c = []
                for i in range(NT):
                    b = take()
                    t = transposes([(CN[:, i, tile(j)], 128 * j) for j in range(4)], b, tr[i])
                    ps = b.t[:, :].rearrange("p (j t) -> p j t", j=4)
                    u = split(pair(CQ, ALL, ALL, tile(i)), ps[:, 0:3, :], t)
                    w = split(pair(CK, ALL, 0, tile(i)), ps[:, 3, :], t, u)
                    give(b, u, w)
                    b = take()
                    t = transposes([(CN[:, i, 512:640], 0), (CN[:, i, 672:704], 128)], b, tr[i])
                    w2 = split(pair(CK, ALL, 1, tile(i)), b.t[:, 0:128], t)
                    e = [VE.do([t, w2], ve.tensor_copy, KT[n][64:96, tile(i)], b.t[0:32, 128:256]) for n in range(2)]
                    give(b, e)
                    tok_c.append([u, w, w2, e])
            g_tok = []
            for f in range(8):
                b = proj_T(w_in[:, :, 672 + 128 * f:800 + 128 * f], XT, ready)
                a = AC.do([b.tok], act.activation, GT[:, f, :], b.t[:, :], ACT.Silu)
                give(b, a)
                g_tok.append(a)
            w_q = A["mla_w_q_up_2"][li].rearrange("(a p) (h c) -> p a h c", p=128, c=96)
            w_kv = A["mla_w_kv_up_2"][li].rearrange("(a p) (h c) -> p a h c", p=128, c=128)
            with ExitStack() as c2:
                QRn = alloc(c2, "QRn", [128, NT, T])
                RT = alloc(c2, "RT", [128, 2, 16, 16])
                bs = proj_N([(w_q[:, a, :, 64:96], 1) for a in range(3)], 512, CQ, tok_c)
                qn = []
                for i, b in enumerate(bs):
                    v = VE.do([b.tok], ve.tensor_scalar, QRn[:, i, :], b.t[:, :], scale, None, mult)
                    give(b, v)
                    q4 = QRn[:, i, :].rearrange("p (h c) -> p h c", c=32)
                    x1, x2 = q4[:, :, 0:16], q4[:, :, 16:32]
                    cs = [x.unsqueeze(1).broadcast_to([128, 16, 16]) for x in (cos(i), sin(i))]
                    qn.append(rope(x1, x2, x1, x2, cs[0], cs[1], RT[:, 0], RT[:, 1], v, VE.last()))
                qrt = []
                for c in range(4):
                    b = take()
                    t = transposes([(QRn[:, i, tile(c)], 128 * i) for i in range(NT)], b, qn)
                    a = AC.do([t], act.copy, QRT[:, c, :], b.t[:, :])
                    give(b, a)
                    qrt.append(a)
            v_tok = []
            for c in range(2):
                bs = proj_N([(w_kv[:, a, 8 * c:8 * c + 8, 64:128], 1) for a in range(2)], 512, CK, tok_c)
                for i, b in enumerate(bs):
                    e = VE.do([b.tok], ve.tensor_copy, V[:, i, 512 * c:512 * c + 512], b.t[:, :])
                    give(b, e)
                    v_tok.append(e)
            att = Attention(cm)
            w_qh, w_kh = by_rows(A["mla_w_q_up_2"][li]), by_rows(A["mla_w_kv_up_2"][li])
            free = [None, None]

            def prepare(h):
                s = h % 2
                b = proj_T(w_qh[:, :, 96 * h:96 * h + 96], CQ, tok_c)
                e1 = AC.do([b.tok, free[s]], act.mul, QT[s][0:64, :], b.t[0:64, :], scale)
                give(b, e1)
                e2 = VE.do([qrt, free[s]], ve.tensor_copy, QT[s][64:96, :], QRT[32 * (h % 4):32 * (h % 4) + 32, h // 4, :])
                b = proj_T(w_kh[:, :, 128 * h:128 * h + 128], CK, tok_c)
                e3 = VE.do([b.tok, free[s]], ve.tensor_copy, KT[s][0:64, :], b.t[0:64, :])
                give(b, e3)
                return [e1, e2, e3]

            prep, sc, done = [prepare(0)], None, []
            for h in range(17):
                if h < 16:
                    s = h % 2
                    new = att.scores(lambda i: QT[s][:, tile(i)], lambda n: KT[s][:, 0:n], [prep[h], tok_c])
                    free[s] = PE.last()
                    if h < 15:
                        prep.append(prepare(h + 1))
                if h > 0:
                    g = h - 1
                    if g % 2 == 0:
                        ob = take()
                    tk = att.values(sc, lambda j: V[:, j, 64 * g:64 * g + 64], ob.t[half(g), :], [v_tok, ob.free])
                    if g % 2:
                        done.append(gated(ob, g // 2, GT, [tk, g_tok]))
                sc = new
            return outproj(by_rows(A["mla_w_out_2"][li]), XT, done, ALPHA)

        def swa(ready, cm):
            w = by_rows(A["swa_w_in_2"][0])
            QT, KT = alloc(cm, "QT", [128, 8, T]), alloc(cm, "KT", [128, 2, T])
            V, GT = alloc(cm, "V", [128, NT, 256]), alloc(cm, "GT", [128, 8, T])
            SB = [alloc(cm, "SB", [128, 2, T]) for _ in range(2)]
            P = [alloc(cm, "P", [128, 2, T]) for _ in range(2)]
            PT = [alloc(cm, "PT", [128, 7, 128]) for _ in range(2)]
            sm = [alloc(cm, "sm", [128, 20]) for _ in range(2)]
            SK = alloc(cm, "SK", [128, 16])
            k_s = AC.dma([], lane("l_sk"), act.dma_start, SK[:, :], A["swa_sinks_2"].broadcast_to([128, 16]))
            inits = [VE.do([], ve.memset, SB[s][:, 0, 0:128], -1e30) for s in range(2)]
            q_tok = []
            for c in range(2):
                for a in range(4):
                    n = 128
                    wt = weight([(w[:, :, 64 * (8 * c + a):64 * (8 * c + a) + 64], 0, 0),
                                 (w[:, :, 64 * (8 * c + 4 + a):64 * (8 * c + 4 + a) + 64], 64, 0)], n)
                    b = take()
                    for k in range(8):
                        tok = mm3(b.t[:, :], wt(k, 0, n), pair(XT, ALL, k, ALL), k == 0, k == 7, [wt.ready, b.free, ready])
                    released[wt.i] = tok
                    e = AC.do([tok], act.mul, QT[:, 4 * c + a, :], b.t[:, :], 0.125)
                    give(b, e)
                    q_tok.append(e)
            for c in range(2):
                b = proj_T(w[:, :, 1024 + 128 * c:1152 + 128 * c], XT, ready)
                e = VE.do([b.tok], ve.tensor_copy, KT[:, c, :], b.t[:, :])
                give(b, e)
                q_tok.append(e)
            bs = proj_N(cut(w[:, :, 1280:1536], 256), 256, XT, ready)
            for i, b in enumerate(bs):
                e = VE.do([b.tok], ve.tensor_copy, V[:, i, :], b.t[:, 0:256])
                give(b, e)
                q_tok.append(e)
            g_tok = []
            for f in range(8):
                b = proj_T(w[:, :, 1536 + 128 * f:1664 + 128 * f], XT, ready)
                a = AC.do([b.tok], act.activation, GT[:, f, :], b.t[:, :], ACT.Silu)
                give(b, a)
                g_tok.append(a)
            DIST = CST[:, C_DIST:C_DIST + 256].unsqueeze(1)
            p_free, t_free = [None, None], [None, None]

            def scores(h):
                s, g = h % 2, h // 4
                c, r = g // 2, half(g)
                S, p, m = SB[s], P[s], sm[s]
                slope = 2.0 ** (-0.5 * (h + 1))
                for u in range(2):
                    b = take()
                    for i in (2 * u, 2 * u + 1):
                        lo = max(0, i - 1)
                        o = b.t[:, (256 * (i % 2) + 128 if i == 0 else 256 * (i % 2)):256 * (i % 2) + 256]
                        t = PE.do([b.free, q_tok], pe.matmul, o, QT[r, 4 * c + h % 4, tile(i)],
                                  KT[r, c, 128 * lo:128 * i + 128], start=True, stop=True)
                    if u == 0:
                        v = VE.do([t, p_free[s]], ve.scalar_tensor_tensor, S[:, 0, 128:256], CST[:, C_DIST + 128:C_DIST + 256],
                                  -slope, b.t[:, 128:256], mult, add)
                        v = VE.do([t], ve.scalar_tensor_tensor, S[:, 0, 256:512], CST[:, C_DIST:C_DIST + 256],
                                  -slope, b.t[:, 256:512], mult, add)
                    else:
                        v = VE.do([t], ve.scalar_tensor_tensor, S[:, 1, :].rearrange("p (i k) -> p i k", i=2),
                                  DIST.broadcast_to([128, 2, 256]), -slope,
                                  b.t[:, :].rearrange("p (i k) -> p i k", i=2), mult, add)
                    give(b, v)
                    v = VE.do([v, inits], ve.reduce_max, m[:, 2 * u:2 * u + 2], S[:, u, :].rearrange("p (i k) -> p i k", i=2), AX.X)
                v = VE.do([v, k_s], ve.tensor_scalar, m[:, 0:4], m[:, 0:4], SK[:, h:h + 1], -1.0, ALU.max, mult)
                for i in range(NT):
                    a = AC.do([v, p_free[s]], act.activation, p[:, i // 2, 256 * (i % 2):256 * (i % 2) + 256],
                              S[:, i // 2, 256 * (i % 2):256 * (i % 2) + 256], ACT.Exp, bias=m[:, i:i + 1],
                              accum_out=m[:, 4 + i:5 + i])
                a = AC.do([v], act.activation, m[:, 8:12], m[:, 0:4], ACT.Exp, bias=SK[:, h:h + 1])
                v = VE.do([a], ve.tensor_tensor, m[:, 4:8], m[:, 4:8], m[:, 8:12], add)
                v = VE.do([v], ve.reciprocal, m[:, 12:16], m[:, 4:8])
                for i in range(NT):
                    x = p[:, i // 2, 256 * (i % 2):256 * (i % 2) + 256]
                    v2 = VE.do([v], ve.tensor_scalar, x, x, m[:, 12 + i:13 + i], None, mult)
                return s, v2

            def values(h, sc, o, rdy):
                s, done = sc
                p, pt = P[s], PT[s]
                blocks = [(j, i) for j in range(NT) for i in (j, j + 1) if i < NT]
                evs = []
                for part in (blocks[0:4], blocks[4:7]):
                    b = take()
                    n0 = 0 if part[0] == blocks[0] else 4
                    t = transposes([(p[:, i // 2, 256 * (i % 2) + (128 if i == j else 0):256 * (i % 2) + (256 if i == j else 128)],
                                     128 * x) for x, (j, i) in enumerate(part)], b, done)
                    dst, src = pt[:, n0:n0 + len(part), :].rearrange("p a b -> p (a b)"), b.t[:, 0:128 * len(part)]
                    e = (VE.do([t, t_free[s]], ve.tensor_copy, dst, src) if n0 else AC.do([t, t_free[s]], act.copy, dst, src))
                    give(b, e)
                    evs.append(e)
                p_free[s] = PE.last()
                for i in range(NT):
                    js = [j for j in (i - 1, i) if j >= 0]
                    for j in js:
                        f = PE.do if (i, j) == (NT - 1, NT - 1) else PE.quiet
                        tok = f([evs, rdy], pe.matmul, o[:, tile(i)], V[:, j, 64 * (h // 4):64 * (h // 4) + 64],
                                pt[:, blocks.index((j, i)), :], start=j == js[0], stop=j == i)
                t_free[s] = tok
                return tok

            sc, done = None, []
            for h in range(17):
                if h < 16:
                    new = scores(h)
                if h > 0:
                    g = h - 1
                    if g % 2 == 0:
                        ob = take()
                    tk = values(g, sc, ob.t[half(g), :], [ob.free])
                    if g % 2:
                        done.append(gated(ob, g // 2, GT, [tk, g_tok]))
                sc = new
            return outproj(by_rows(A["swa_w_out_2"][0]), XT, done, ALPHA)

        def log_sigmoid(dst, z, t, scale, after):
            a = AC.do(after, act.activation, t, z, ACT.Abs)
            a = AC.do([a], act.activation, t, t, ACT.Exp, scale=-1.0)
            a = AC.do([a], act.activation, t, t, ACT.Ln, bias=1.0)
            v = VE.do([after, a], ve.tensor_scalar, z, z, 0.0, scale, ALU.min, mult)
            return VE.do([v, a], ve.scalar_tensor_tensor, dst, t, -scale, z, mult, add)

        def fox(ready, cm):
            w = by_rows(A["fox_w_in_2"][0])
            QT, KT = alloc(cm, "QT", [128, 8, T]), alloc(cm, "KT", [128, 8, T])
            V, GT = alloc(cm, "V", [128, NT, D]), alloc(cm, "GT", [128, 8, T])
            CB = [alloc(cm, "CB", [96, T], B16) for _ in range(2)]
            zero = VE.do([], ve.memset, CB[0][:, :], 0.0)
            zero = VE.do([], ve.memset, CB[1][:, :], 0.0)
            with ExitStack() as c1:
                FZ, FT, FC = (alloc(c1, n, [16, T]) for n in ("FZ", "FT", "FC"))
                FB = alloc(c1, "FB", [16, 1])
                k_f = AC.dma([], lane("l_fb"), act.dma_start, FB[:, :], A["fox_b_f_2"].rearrange("o h -> h o"))
                b = proj_T(w[:, :, 3072:3200], XT, ready)
                v = VE.do([b.tok, k_f], ve.tensor_scalar, FZ[:, :], b.t[0:16, :], FB[:, 0:1], None, add)
                give(b, v)
                v = log_sigmoid(FC[:, :], FZ[:, :], FT[:, :], 1.0, [v])
                one = VE.do([v], ve.memset, FT[:, :], 1.0)
                v = VE.do([v, one], ve.tensor_tensor_scan, FZ[:, :], FT[:, :], FC[:, :], 0.0, mult, add)
                for k in range(3):
                    c = CB[0][32 * k:32 * k + 16, :]
                    v = VE.do([v, zero], ve.tensor_copy, c, FZ[:, :])
                    v2 = VE.do([v], ve.tensor_scalar, CB[1][32 * k:32 * k + 16, :], c, -1.0, None, mult)
                    if k < 2:
                        v = VE.do([v], ve.tensor_copy, FT[:, :], c)
                        v = VE.do([v], ve.tensor_tensor, FZ[:, :], FZ[:, :], FT[:, :], sub)
                cb = v2
            toks = []
            for f in range(8):
                b = proj_T(w[:, :, tile(f)], XT, ready)
                e = AC.do([b.tok], act.mul, QT[:, f, :], b.t[:, :], 0.125)
                give(b, e)
                toks.append(e)
            for f in range(8):
                b = proj_T(w[:, :, 1024 + 128 * f:1152 + 128 * f], XT, ready)
                e = VE.do([b.tok], ve.tensor_copy, KT[:, f, :], b.t[:, :])
                give(b, e)
                toks.append(e)
            for c in range(2):
                bs = proj_N(cut(w[:, :, 2048 + 512 * c:2560 + 512 * c], 512), 512, XT, ready)
                for i, b in enumerate(bs):
                    e = VE.do([b.tok], ve.tensor_copy, V[:, i, 512 * c:512 * c + 512], b.t[:, :])
                    give(b, e)
                    toks.append(e)
            g_tok = []
            for f in range(8):
                b = proj_T(w[:, :, 3088 + 128 * f:3216 + 128 * f], XT, ready)
                a = AC.do([b.tok], act.activation, GT[:, f, :], b.t[:, :], ACT.Silu)
                give(b, a)
                g_tok.append(a)
            att = Attention(cm)
            sc, done = None, []
            for h in range(17):
                if h < 16:
                    sel = SLB[0:96, h:h + 1]
                    new = att.scores(lambda i: QT[half(h), h // 2, tile(i)], lambda n: KT[half(h), h // 2, 0:n], [toks, cb],
                                     extra=[(lambda i: CB[0][:, tile(i)], lambda n: sel.broadcast_to([96, n])),
                                            (lambda i: sel.broadcast_to([96, 128]), lambda n: CB[1][:, 0:n])])
                if h > 0:
                    g = h - 1
                    if g % 2 == 0:
                        ob = take()
                    tk = att.values(sc, lambda j: V[:, j, 64 * g:64 * g + 64], ob.t[half(g), :], [ob.free])
                    if g % 2:
                        done.append(gated(ob, g // 2, GT, [tk, g_tok]))
                sc = new
            return outproj(by_rows(A["fox_w_out_2"][0]), XT, done, ALPHA)

        def mix(ready, cm):
            w = by_rows(A["w_in"][0])
            OA = (alloc(cm, "OAh", [128, 4, T], R), alloc(cm, "OAl", [128, 4, T], R))
            OB = (alloc(cm, "OBh", [128, 4, T], R), alloc(cm, "OBl", [128, 4, T], R))
            done_a = nsa(w, ready, OA)
            fence()
            done_b = gla(w, ready, OB)
            fence()
            with ExitStack() as c1:
                MT = (alloc(c1, "MTh", [128, 8, T], R), alloc(c1, "MTl", [128, 8, T], R))
                sg = [alloc(c1, "sg", [128, T]) for _ in range(4)]
                wa, wb = by_rows(A["w_up_nsa"][0]), by_rows(A["w_up_gla"][0])
                used, toks = [None, None], []
                for f in range(8):
                    s = f % 2
                    ga, gb = sg[2 * s], sg[2 * s + 1]
                    b1 = proj_T(w[:, :, 2856 + 128 * f:2984 + 128 * f], XT, ready)
                    a1 = AC.do([b1.tok, used[s]], act.activation, ga[:, :], b1.t[:, :], ACT.Sigmoid)
                    give(b1, a1)
                    b2 = proj_T(w[:, :, 3880 + 128 * f:4008 + 128 * f], XT, ready)
                    a2 = AC.do([b2.tok, used[s]], act.activation, gb[:, :], b2.t[:, :], ACT.Sigmoid)
                    give(b2, a2)
                    b3 = proj_T(wa[:, :, tile(f)], OA, done_a)
                    v1 = VE.do([a1, b3.tok], ve.tensor_tensor, ga[:, :], ga[:, :], b3.t[:, :], mult)
                    give(b3, v1)
                    b4 = proj_T(wb[:, :, tile(f)], OB, done_b)
                    v2 = VE.do([a2, b4.tok], ve.tensor_tensor, gb[:, :], gb[:, :], b4.t[:, :], mult)
                    give(b4, v2)
                    v = VE.do([v2], ve.tensor_tensor, ga[:, :], ga[:, :], gb[:, :], add)
                    used[s] = split(pair(MT, ALL, f, ALL), ga[:, :], v)
                    toks.append(used[s])
                return outproj(by_rows(A["w_out"][0]), MT, toks, 1.0)

        def nsa(w, ready, OA):
            with ExitStack() as cm:
                QR, QT = alloc(cm, "QR", [128, 4, T]), alloc(cm, "QT", [128, 4, T])
                KV = alloc(cm, "KV", [128, NT, T])
                KS = [alloc(cm, "KS", [128, T]) for _ in range(2)]
                GN = alloc(cm, "GN", [128, NT, 24])
                KC, VC = alloc(cm, "KC", [128, 32]), alloc(cm, "VC", [32, 2, 64])
                cos = CST[:, C_NROPE:C_NROPE + 32].rearrange("p (i c) -> p i c", c=8)
                sin = CST[:, C_NROPE + 32:C_NROPE + 64].rearrange("p (i c) -> p i c", c=8)
                with ExitStack() as c1:
                    qn, qr = alloc(c1, "qn", [128, NT, T]), alloc(c1, "qr", [128, NT, T])
                    tm = alloc(c1, "tm", [128, 2, 4 * 8 * 8])
                    bs = proj_N(cut(w[:, :, 0:512], 512), 512, XT, ready)
                    e1, e2 = [], []
                    for i, b in enumerate(bs):
                        e1.append(AC.do([b.tok], act.mul, qn[:, i, :].rearrange("p (a g d) -> p g a d", a=4, g=2),
                                        b.t[:, :].rearrange("p (g a d) -> p g a d", a=4, g=2), 0.125))
                        e2.append(VE.do([e1[-1]], ve.tensor_copy, qr[:, i, :], qn[:, i, :]))
                        give(b, e1[-1])
                    for i in range(NT):
                        q4 = qn[:, i, :].rearrange("p (h c) -> p h c", c=64)
                        o4 = qr[:, i, :].rearrange("p (h c) -> p h c", c=64)
                        cs = [x[:, i, :].unsqueeze(1).broadcast_to([128, 8, 8]) for x in (cos, sin)]
                        t = [tm[:, u, 0:64].rearrange("p (h c) -> p h c", c=8) for u in range(2)]
                        r_q = rope(q4[:, :, 0:8], q4[:, :, 8:16], o4[:, :, 0:8], o4[:, :, 8:16], cs[0], cs[1], t[0], t[1],
                                   e1, e2, VE.last())
                    bs = proj_N(cut(w[:, :, 768:1280], 512), 512, XT, ready)
                    for i, b in enumerate(bs):
                        v = VE.do([b.tok], ve.tensor_copy, KV[:, i, :], b.t[:, :])
                        give(b, v)
                        cs = [x[:, i, :].unsqueeze(1).broadcast_to([128, 2, 8]) for x in (cos, sin)]
                        for c in (0, 256):
                            k4 = KV[:, i, c:c + 128].rearrange("p (g c) -> p g c", c=64)
                            t = [tm[:, u, 0:16].rearrange("p (h c) -> p h c", c=8) for u in range(2)]
                            r_k = rope(k4[:, :, 0:8], k4[:, :, 8:16], k4[:, :, 0:8], k4[:, :, 8:16], cs[0], cs[1],
                                       t[0], t[1], v, VE.last())
                    ready_q = []
                    for a in range(4):
                        for src, dst, r in ((qn, QR, e1), (qr, QT, r_q)):
                            b = take()
                            t = transposes([(src[:, i, tile(a)], 128 * i) for i in range(NT)], b, r)
                            e = AC.do([t], act.copy, dst[:, a, :], b.t[:, :])
                            give(b, e)
                            ready_q.append(e)
                    for c in range(2):
                        b = take()
                        t = transposes([(KV[:, i, 256 * c:256 * c + 128], 128 * i) for i in range(NT)], b, r_k)
                        e = VE.do([t], ve.tensor_copy, KS[c][:, :], b.t[:, :])
                        give(b, e)
                        ready_q.append(e)
                    bs = proj_N([(w[:, :, 1280:1304], 8)], 24, XT, ready)
                    g_tok = []
                    for i, b in enumerate(bs):
                        e = AC.do([b.tok], act.activation, GN[:, i, :], b.t[:, 0:24], ACT.Sigmoid)
                        give(b, e)
                        g_tok.append(e)
                fence()
                with ExitStack() as c1:
                    KX = [[alloc(c1, "KX", [128, 560], R) for h in "hl"] for _ in range(2)]
                    PF = [alloc(c1, "PF", [32, 128]) for _ in range(2)]
                    W2 = [alloc(c1, "W2", [128, 64]) for _ in range(2)]
                    Z = alloc(c1, "Z", [128, 16])
                    HB, HC = alloc(c1, "HB", [128, 4]), alloc(c1, "HC", [128, 4, 32])
                    lz = [lane(f"l_c{j}") for j in range(2)]
                    z = VE.do([], ve.memset, Z[:, :], 0.0)
                    c_tok = []
                    for j, nm in enumerate(("k", "v")):
                        for g in range(2):
                            kd = AC.dma([], lz[j], act.dma_start, PF[j][:, 64 * g:64 * g + 64], A[f"cmp_pe_{nm}"][0])
                        kd = AC.dma([], lz[j], act.dma_start, W2[j][:, :], A[f"cmp_{nm}_w2"][0])
                        b = proj_T(w[:, :, 512 + 128 * j:640 + 128 * j], XT, ready)
                        K = KX[j]
                        t1 = split([K[0][:, 0:512], K[1][:, 0:512]], b.t[:, :], b.tok)
                        give(b, t1)
                        b = take()
                        t = transposes([(PF[j][:, :], 0)], b, [kd])
                        t2 = split([K[0][:, 528:560], K[1][:, 528:560]], b.t[:, 0:32], t)
                        give(b, t2)
                        t3 = split([K[0][:, 512:528], K[1][:, 512:528]], Z[:, :], z)
                        w1 = A[f"cmp_{nm}_w1"][0].rearrange("(l d) n -> d l n", d=64)
                        hb = [take(), take()]
                        for l0 in range(0, 32, 8):
                            wt = weight([(w1[:, l0:l0 + 8, :], 0, 0), (w1[:, l0:l0 + 8, :], 0, 64)], 128)
                            for g in range(2):
                                for l in range(8):
                                    rs = slice(64 * g, 64 * g + 64)
                                    rh = [K[h][rs, l0 + l:l0 + l + 529:16] for h in range(2)]
                                    tok = mm3(hb[g].t[:, 0:34], wt(l, 0, 128, 64 * g, 64 * g + 64), rh, l0 + l == 0,
                                              l0 + l == 31, [wt.ready, hb[g].free, t1, t2, t3], sig=g == 1 and l == 7)
                                    if tok:
                                        released[wt.i] = hb[g].tok = tok
                        for g in range(2):
                            x = 2 * j + g
                            e = AC.do([hb[g].tok], act.copy, HB[:, x:x + 1], hb[g].t[:, 33:34])
                            e = AC.do([e], act.activation, HC[:, x, 0:31], hb[g].t[:, 0:31], ACT.Silu, bias=HB[:, x:x + 1])
                            give(hb[g], e)
                            b = take()
                            if j == 0:
                                t = PE.do([e, kd, b.free], pe.matmul, b.t[64 * g:64 * g + 64, 0:31], W2[0][:, :], HC[:, x, 0:31],
                                          start=True, stop=True)
                                c = VE.do([t], ve.tensor_copy, KC[64 * g:64 * g + 64, 0:31], b.t[64 * g:64 * g + 64, 0:31])
                            else:
                                t = PE.do([e, kd, b.free], pe.matmul, b.t[0:31, 0:64], HC[:, x, 0:31], W2[1][:, :],
                                          start=True, stop=True)
                                c = VE.do([t], ve.tensor_copy, VC[0:31, g, :], b.t[0:31, 0:64])
                            give(b, c)
                            c_tok.append(c)
                fence()
                att = Attention(cm)
                MC = alloc(cm, "MC", [128, 2, NT, 32])
                PC = [alloc(cm, "PC", [128, NT, 32]) for _ in range(2)]
                CT = [alloc(cm, "CT", [32, T]) for _ in range(2)]
                cs_ = [alloc(cm, "cs", [128, 16]) for _ in range(2)]
                k_mc = AC.dma([], lane("l_mc"), act.dma_start, MC[:, :, :, :],
                              A["cmask"].rearrange("p (u i n) -> p u i n", u=2, i=NT))
                c_free = [None, None]

                def compressed(h):
                    s, g = h % 2, h // 4
                    b = take()
                    for i in range(NT):
                        t = PE.do([b.free, ready_q, c_tok], pe.matmul, b.t[:, 32 * i:32 * i + 31],
                                  QR[64 * g:64 * g + 64, h % 4, tile(i)], KC[64 * g:64 * g + 64, 0:31], start=True, stop=True)
                    p, c = PC[s], cs_[s]
                    x = b.t[:, 0:128].rearrange("p (i n) -> p i n", i=NT)[:, :, 0:31]
                    v = VE.do([t, k_mc, c_free[s]], ve.tensor_tensor, p[:, :, 0:31], x, MC[:, 0, :, 0:31], mult)
                    give(b, v)
                    v = VE.do([v], ve.tensor_tensor, p[:, :, 0:31], p[:, :, 0:31], MC[:, 1, :, 0:31], add)
                    v = VE.do([v], ve.reduce_max, c[:, 0:4], p[:, :, 0:31], AX.X, negate=True)
                    v = VE.do([v], ve.tensor_tensor, p[:, :, 0:31], p[:, :, 0:31],
                              c[:, 0:4].unsqueeze(2).broadcast_to([128, NT, 31]), add)
                    a = AC.do([v], act.activation, p[:, :, 0:31], p[:, :, 0:31], ACT.Exp)
                    v = VE.do([a], ve.reduce_sum, c[:, 4:8], p[:, :, 0:31], AX.X)
                    v = VE.do([v], ve.reciprocal, c[:, 8:12], c[:, 4:8])
                    v = VE.do([v, g_tok], ve.tensor_tensor, c[:, 8:12], c[:, 8:12], GN[:, :, 3 * h], mult)
                    v = VE.do([a], ve.tensor_tensor, p[:, :, 0:31], p[:, :, 0:31], MC[:, 0, :, 0:31], mult)
                    v = VE.do([v], ve.tensor_tensor, p[:, :, 0:31], p[:, :, 0:31],
                              c[:, 8:12].unsqueeze(2).broadcast_to([128, NT, 31]), mult)
                    return s, v

                def c_values(cp):
                    s, v = cp
                    b = take()
                    t = transposes([(PC[s][:, i, 0:31], 128 * i) for i in range(NT)], b, [v])
                    c_free[s] = t
                    e = AC.do([t, ct_free[s]], act.copy, CT[s][0:31, :], b.t[0:31, :])
                    give(b, e)
                    return e

                ct_free = [None, None]
                jobs = [(h, c) for h in range(8) for c in range(2)]
                sc, cp, done = None, None, []
                for x in range(17):
                    if x < 16:
                        h, c = jobs[x]
                        if c == 0:
                            cp_new = compressed(h)
                        r = slice(64 * (h // 4), 64 * (h // 4) + 64)
                        new = att.scores(lambda i: QT[r, h % 4, tile(i)], lambda n: KS[c][r, 0:n], [ready_q],
                                         gate=GN[:, :, 3 * h + 1 + c])
                    if x > 0:
                        h, c = jobs[x - 1]
                        g, s = h // 4, h % 2
                        if c == 0:
                            if h % 2 == 0:
                                ob = take()
                            o = ob.t[half(h), :]
                            e = c_values(cp)
                            ct_free[s] = PE.do([e, ob.free], pe.matmul, o, VC[0:31, g, :], CT[s][0:31, :], start=True, stop=False)
                        tk = att.values(sc, lambda j: KV[:, j, 256 * c + 128 + 64 * g:256 * c + 192 + 64 * g], o, [],
                                        start=False, stop=c == 1)
                        if c == 1 and h % 2:
                            d = split(pair(OA, ALL, h // 2, ALL), ob.t[:, :], tk)
                            give(ob, d)
                            done.append(d)
                    sc, cp = new, cp_new
                return done

        def gla(w, ready, OB):
            with ExitStack() as cm:
                GQ, GK = alloc(cm, "GQ", [128, 2, T]), alloc(cm, "GK", [128, 2, T])
                GV, GR = alloc(cm, "GV", [128, NT, T]), alloc(cm, "GR", [128, NT, T])
                LR, W2, BC = alloc(cm, "LR", [16, T]), alloc(cm, "W2", [16, 256]), alloc(cm, "BC", [128, 2])
                MK = alloc(cm, "MK", [128, 8, 128])
                GG = alloc(cm, "GG", [128, 128])
                C, S, E, Z, T1, EX = (alloc(cm, n, [128, T]) for n in ("C", "S", "E", "Z", "T1", "EX"))
                DG, OD = alloc(cm, "DG", [128, 2, NT, 128]), alloc(cm, "OD", [128, 2, 6, 128])
                ON, O2 = alloc(cm, "ON", [128, 2, 256]), alloc(cm, "O2", [128, 256])
                ss = alloc(cm, "ss", [128, 8])
                lz = [lane(f"l_gl{j}") for j in range(4)]
                kw = [AC.dma([], lz[0], act.dma_start, W2[:, :], A["gla_gate_w2"][0]),
                      [AC.dma([], lz[1], act.dma_start, BC[:, c:c + 1], A["gla_gate_b"][0, tile(c)].rearrange("(p o) -> p o", o=1))
                       for c in range(2)],
                      AC.dma([], lz[2], act.dma_start, GG[:, :], A["gla_norm"].broadcast_to([128, 128])),
                      AC.dma([], lz[3], act.dma_start, MK[:, :, :], A["cst"][:, C_GLA:C_END].rearrange("p (m n) -> p m n", m=8))]
                toks = []
                b = proj_T(w[:, :, 2328:2456], XT, ready)
                e = AC.do([b.tok], act.copy, LR[:, :], b.t[0:16, :])
                give(b, e)
                toks.append(e)
                for c in range(2):
                    b = proj_T(w[:, :, 1304 + 128 * c:1432 + 128 * c], XT, ready)
                    e = AC.do([b.tok], act.mul, GQ[:, c, :], b.t[:, :], 0.125)
                    give(b, e)
                    toks.append(e)
                    b = proj_T(w[:, :, 1560 + 128 * c:1688 + 128 * c], XT, ready)
                    e = AC.do([b.tok], act.copy, GK[:, c, :], b.t[:, :])
                    give(b, e)
                    toks.append(e)
                bs = proj_N(cut(w[:, :, 1816:2328], 512), 512, XT, ready)
                for i, b in enumerate(bs):
                    e = AC.do([b.tok], act.copy, GV[:, i, :], b.t[:, :])
                    give(b, e)
                    toks.append(e)
                bs = proj_N(cut(w[:, :, 2344:2856], 512), 512, XT, ready)
                for i, b in enumerate(bs):
                    e = AC.do([b.tok], act.activation, GR[:, i, :], b.t[:, :], ACT.Silu)
                    give(b, e)
                    toks.append(e)
                done, ob_free = [None] * NT, [None, None]
                o2_tok = None
                for dp in range(2):
                    prev = [PE.last(), AC.last(), VE.last()]
                    b = take()
                    t = PE.do([b.free, kw, toks], pe.matmul, b.t[:, :], W2[:, tile(dp)], LR[:, :], start=True, stop=True)
                    v = VE.do([t, prev], ve.tensor_scalar, Z[:, :], b.t[:, :], BC[:, dp:dp + 1], None, add)
                    give(b, v)
                    v = log_sigmoid(E[:, :], Z[:, :], T1[:, :], 1.0 / 16, [v])
                    one = VE.do([v], ve.memset, T1[:, :], 1.0)
                    for c in range(8):
                        cs = slice(64 * c, 64 * c + 64)
                        v = VE.do([one, prev], ve.tensor_tensor_scan, C[:, cs], T1[:, cs], E[:, cs], 0.0, mult, add)
                    z0 = VE.do([prev], ve.memset, DG[:, :, :, :], 0.0)
                    c_ok = v
                    q, k = GQ[:, dp, :], GK[:, dp, :]

                    for hh in range(2):
                        b = take()
                        r = slice(64 * hh, 64 * hh + 64)
                        for i in range(NT):
                            t = PE.do([b.free, toks], pe.matmul, b.t[:, tile(i)], GK[r, dp, tile(i)], GQ[r, dp, tile(i)],
                                      start=True, stop=True)
                        v = VE.do([t, z0, kw], ve.copy_predicated, DG[:, hh, :, :],
                                  MK[:, 7, :].bitcast(I32).unsqueeze(1).broadcast_to([128, NT, 128]),
                                  b.t[:, :].rearrange("p (i t) -> p i t", i=NT))
                        give(b, v)
                    e_free, z_free = [v, c_ok], [v]
                    for li, m in enumerate((256, 128, 64, 32, 16, 8, 4, 2, 1)):
                        if m >= 128:
                            for c in range(T // m):
                                cs = slice(m * c, m * c + m)
                                v = VE.do([e_free, one], ve.tensor_tensor_scan, S[:, cs], T1[:, cs], E[:, cs], 0.0, mult, add)
                            src, ok = S, v
                        else:
                            src, ok = C, c_ok
                        s3 = src[:, :].rearrange("p (b u m) -> p b u m", u=2, m=m)
                        e3 = EX[:, :].rearrange("p (b u m) -> p b u m", u=2, m=m)
                        nb = T // (2 * m)
                        v1 = VE.do([ok, e_free], ve.tensor_tensor, e3[:, :, 0, :],
                                   s3[:, :, 0, m - 1:m].broadcast_to([128, nb, m]), s3[:, :, 0, :], sub)
                        if m >= 64:
                            v2 = VE.do([ok, e_free], ve.tensor_copy, e3[:, :, 1, :], s3[:, :, 1, :])
                        else:
                            v2 = VE.do([ok, e_free], ve.tensor_tensor, e3[:, :, 1, :], s3[:, :, 1, :],
                                       s3[:, :, 0, m - 1:m].broadcast_to([128, nb, m]), sub)
                        a = AC.do([v1, v2], act.activation, EX[:, :], EX[:, :], ACT.Exp)
                        z3 = Z[:, :].rearrange("p (b u m) -> p b u m", u=2, m=m)
                        q3 = q.rearrange("p (b u m) -> p b u m", u=2, m=m)
                        k3 = k.rearrange("p (b u m) -> p b u m", u=2, m=m)
                        v1 = VE.do([a, z_free, toks], ve.tensor_tensor, z3[:, :, 0, :], e3[:, :, 0, :], k3[:, :, 0, :], mult)
                        v2 = VE.do([a, z_free], ve.tensor_tensor, z3[:, :, 1, :], e3[:, :, 1, :], q3[:, :, 1, :], mult)
                        e_free = [v1, v2]
                        for hh in range(2):
                            b = take()
                            r = slice(64 * hh, 64 * hh + 64)
                            if m == 256:
                                for s in range(2):
                                    t = PE.do([b.free, v1, v2], pe.matmul, b.t[:, 256 * s:256 * s + 256], Z[r, tile(s)],
                                              Z[r, 256:512], start=True, stop=True)
                                v = VE.do([t, prev], ve.tensor_copy, OD[:, hh, 0:4, :], b.t[:, :].rearrange("p (i t) -> p i t", i=4))
                            elif m == 128:
                                for s in range(2):
                                    t = PE.do([b.free, v1, v2], pe.matmul, b.t[:, tile(s)], Z[r, tile(2 * s)],
                                              Z[r, tile(2 * s + 1)], start=True, stop=True)
                                v = VE.do([t, prev], ve.tensor_copy, OD[:, hh, 4:6, :], b.t[:, 0:256].rearrange("p (i t) -> p i t", i=2))
                            else:
                                for i in range(NT):
                                    t = PE.do([b.free, v1, v2], pe.matmul, b.t[:, tile(i)], Z[r, tile(i)], Z[r, tile(i)],
                                              start=True, stop=True)
                                v = VE.do([t, z0, kw], ve.copy_predicated, DG[:, hh, :, :],
                                          MK[:, li - 2, :].bitcast(I32).unsqueeze(1).broadcast_to([128, NT, 128]),
                                          b.t[:, :].rearrange("p (i t) -> p i t", i=NT))
                            give(b, v)
                            last_v = v
                        z_free = [PE.last()]
                    for i in range(NT):
                        b = take()
                        for hh in range(2):
                            for s in range(i + 1):
                                if s == i:
                                    l = DG[:, hh, i, :]
                                elif (s, i) in ((0, 1), (2, 3)):
                                    l = OD[:, hh, 4 + s // 2, :]
                                else:
                                    l = OD[:, hh, 2 * s + i - 2, :]
                                t = PE.do([b.free, last_v, toks], pe.matmul, b.t[:, tile(hh)], l,
                                          GV[:, s, 256 * dp + 128 * hh:256 * dp + 128 * hh + 128], start=s == 0, stop=s == i)
                        on = ON[:, i % 2, :]
                        a = AC.do([t, o2_tok, prev], act.activation, O2[:, :], b.t[:, 0:256], ACT.Square)
                        v = VE.do([a], ve.reduce_sum, ss[:, 0:2], O2[:, :].rearrange("p (h v) -> p h v", h=2), AX.X)
                        o2_tok = v
                        r = rsqrt(ss[:, 2:4], ss[:, 0:2], 1.0 / 128, 1e-6, ss[:, 4:6], ss[:, 6:8], v)
                        for hh in range(2):
                            v = VE.do([r, a, ob_free[i % 2]], ve.scalar_tensor_tensor, on[:, tile(hh)], b.t[:, tile(hh)],
                                      ss[:, 2 + hh:3 + hh], GG[:, :], mult, mult)
                        give(b, v)
                        v = VE.do([v, toks], ve.tensor_tensor, on, on, GR[:, i, 256 * dp:256 * dp + 256], mult)
                        b = take()
                        t = transposes([(on[:, tile(hh)], 128 * hh) for hh in range(2)], b, [v])
                        ob_free[i % 2] = t
                        d = split(pair(OB, ALL, slice(2 * dp, 2 * dp + 2), tile(i)),
                                  b.t[:, 0:256].rearrange("p (j t) -> p j t", j=2), t)
                        give(b, d)
                        done[i] = [done[i], d]
                return done

        final = "mla1" if "mla1" in stages else stages[-1]
        ready, xr = None, [k_x] * NT
        done = None
        if "mix" in stages:
            with ExitStack() as cm:
                g = gains(A["norm_mix"][0])
                ready = rms_norm(g, None, cm)
            fence()
            with ExitStack() as cm:
                done = mix(ready, cm)
            fence()
        if "ffn" in stages:
            with ExitStack() as cm:
                ready = rms_norm(gains(A["norm_ffn"][0]), done or xr, cm)
            fence()
            with ExitStack() as cm:
                done = ffn(ready, cm)
            fence()
            with ExitStack() as cm:
                ready = rms_norm(gains(A["norm_final"]), done, cm, to_x=True)
            done = ready
            fence()
        for n, (name, f) in enumerate((("mla0", lambda r, c: mla(0, r, c)), ("swa", swa), ("fox", fox),
                                       ("mla1", lambda r, c: mla(1, r, c)))):
            if name not in stages:
                continue
            if ready is None or (done is None):
                ready = [to_XT(X[:, i, :], i, k_x) for i in range(NT)]
            g = gains(A["ln_g_2"][n], A["ln_b_2"][n])
            with ExitStack() as cm:
                done = f(ready, cm)
            fence()
            ready = layer_norm(g, done, transposed=name != final)
            done = ready
        o_tok = []
        o_v = out.rearrange("o (i p) d -> p (o i) d", p=128)
        l_o = [lane(f"l_o{i}") for i in range(NT)]
        for i in range(NT):
            o_tok.append(SP.dma([done[i]], l_o[i], nc.sync.dma_start, o_v[:, i, :], X[:, i, :]))
        SP.wait(*o_tok)

        block = top.enter_context(nc.Block())

        @block.sync
        def _(e):
            SP.play(e)

        @block.scalar
        def _(e):
            AC.play(e)

        @block.vector
        def _(e):
            VE.play(e)

        @block.gpsimd
        def _(e):
            PO.play(e)

        @block.tensor
        def _(e):
            PE.play(e)


def constants():
    c = np.zeros((128, C_END), np.float32)
    p = np.arange(128)
    c[:, C_ID:C_ID + 128] = np.eye(128)
    c[:, C_MASK:C_MASK + 128] = np.where(p[None, :] > p[:, None], -1e30, 0.0)
    dist = p[:, None] + 128 - np.arange(256)[None, :]
    c[:, C_DIST:C_DIST + 256] = np.where((dist >= 0) & (dist < 128), dist, 3e35)
    t = (np.arange(4)[None, :] * 128 + p[:, None]).astype(np.float32)
    inv = (np.float32(500000.0) ** (-np.arange(8, dtype=np.float32) / np.float32(8))).astype(np.float32)
    ang = (t[:, :, None] * inv).astype(np.float32)
    c[:, C_NROPE:C_NROPE + 32] = np.cos(ang).reshape(128, 32)
    c[:, C_NROPE + 32:C_NROPE + 64] = np.sin(ang).reshape(128, 32)
    inv = (np.float32(10000.0) ** (-np.arange(0, 32, 2, dtype=np.float32) / np.float32(32))).astype(np.float32)
    ang = (t[:, :, None] * inv).astype(np.float32)
    c[:, C_MROPE:C_MROPE + 64] = np.cos(ang).reshape(128, 64)
    c[:, C_MROPE + 64:C_MROPE + 128] = np.sin(ang).reshape(128, 64)
    for h in range(16):
        c[[h, 32 + h, 64 + h], C_SEL + h] = 1.0
    s, q = p[:, None], p[None, :]
    for i, m in enumerate((64, 32, 16, 8, 4, 2, 1)):
        c[:, C_GLA + 128 * i:C_GLA + 128 * i + 128] = (s // (2 * m) == q // (2 * m)) & (s // m % 2 == 0) & (q // m % 2 == 1)
    c[:, C_GLA + 896:C_GLA + 1024] = np.eye(128)
    seen = (16 * np.arange(32)[None, None, :] + 31 <= t[:, :, None]).astype(np.float32)
    m = np.stack([seen, (seen - 1) * np.float32(1e30)], 1).reshape(128, 256)
    return c, m


_OUT = (1, T, D)
_INS = ["x", "norm_mix", "w_in", "cmp_pe_k", "cmp_pe_v", "cmp_k_w1", "cmp_k_w2", "cmp_v_w1", "cmp_v_w2", "gla_gate_w2",
        "gla_gate_b", "gla_norm", "w_up_nsa", "w_up_gla", "w_out", "norm_ffn", "w_ffn_gate", "w_ffn_up", "w_ffn_down",
        "norm_final", "ln_g_2", "ln_b_2", "mla_w_in_2", "mla_q_norm_2", "mla_w_q_up_2", "mla_kv_norm_2",
        "mla_w_kv_up_2", "mla_w_out_2", "swa_w_in_2", "swa_sinks_2", "swa_w_out_2", "fox_w_in_2", "fox_b_f_2",
        "fox_w_out_2"]


def kernel(**inputs):
    import concourse.bacc as bacc
    from concourse.bass_utils import run_bass_kernel_spmd

    nc = bacc.Bacc("TRN2", target_bir_lowering=False, num_devices=1)
    cst, cmask = constants()
    arrays = {n: np.ascontiguousarray(inputs[n]) for n in _INS}
    arrays["cst"], arrays["cmask"] = cst, cmask
    aps = {n: nc.dram_tensor(f"in_{n}", a.shape, mybir.dt.from_np(a.dtype), kind="ExternalInput").ap()
           for n, a in arrays.items()}
    out = nc.dram_tensor("out_x", _OUT, F, kind="ExternalOutput").ap()
    program(nc, aps, out)
    r = run_bass_kernel_spmd(nc, [{f"in_{n}": a for n, a in arrays.items()}], core_ids=[0])
    return r.results[0]["out_x"]
```

```python
import numpy as np
import concourse.bass as bass
from concourse import mybir
from contextlib import ExitStack

F = mybir.dt.float32
R = mybir.dt.float32r
B16 = mybir.dt.bfloat16
I32 = mybir.dt.int32
ALU = mybir.AluOpType
ACT = mybir.ActivationFunctionType
AX = mybir.AxisListType

T = 512
D = 1024
NT = 4
DFF = 2816
RAW_SLOTS = 3
W_SLOTS = 5
LOOK = 3
LAST = 4
PIECE = 1024
OFF = (0, 128, 384, 768)
ALPHA = 8.0 ** 0.25
C_ID, C_MASK, C_DIST, C_NROPE, C_MROPE, C_SEL, C_GLA, C_END = 0, 128, 256, 512, 576, 704, 720, 1744


class Queue:

    def __init__(self, sem):
        self.sem, self.n, self.items = sem, 0, []

    def do(self, after, f, *a, **k):
        self.n += 1
        self.items.append((after, f, a, k, (self.sem, 1)))
        return (self.sem, self.n)

    def quiet(self, after, f, *a, **k):
        self.items.append((after, f, a, k, None))

    def wait(self, *after):
        self.items.append((list(after), None, (), {}, None))

    def dma(self, after, lane, f, *a):
        lane[1] += 16
        self.items.append((after, f, a, {}, (lane[0], 16)))
        return (lane[0], lane[1])

    def slot(self):
        own = []
        self.items.append(own)
        return own

    def last(self):
        return (self.sem, self.n)

    def play(self, eng):
        seen, flat = {}, []
        for it in self.items:
            flat += it if isinstance(it, list) else [it]
        for after, f, a, k, inc in flat:
            stack = [after]
            while stack:
                t = stack.pop(0)
                if t is None:
                    continue
                if isinstance(t, list):
                    stack = t + stack
                    continue
                sem, v = t
                if v > seen.get(sem.name, 0):
                    eng.wait_ge(sem, v)
                    seen[sem.name] = v
            if f is not None:
                ins = f(*a, **k)
                if inc is not None:
                    ins.then_inc(inc[0], inc[1])


class Bank:

    def __init__(self, t):
        self.t, self.free, self.tok = t, None, None


def program(nc, A, out, stages=("mix", "ffn", "mla0", "swa", "fox", "mla1")):
    top = ExitStack()
    with top:
        names = {}

        def sem(name):
            return top.enter_context(nc.semaphore(name))

        def alloc(cm, name, shape, dt=F, side="left"):
            names[name] = names.get(name, 0) + 1
            return cm.enter_context(nc.sbuf_tensor(f"{name}_{names[name]}", shape, dt, side=side))

        PE, AC, VE, PO = (Queue(sem(n)) for n in ("s_pe", "s_act", "s_dve", "s_pool"))
        SP = Queue(None)
        pe, act, ve, po = nc.tensor, nc.scalar, nc.vector, nc.gpsimd
        mult, add, sub = ALU.mult, ALU.add, ALU.subtract

        X = alloc(top, "X", [128, NT, D])
        XT = (alloc(top, "XTh", [128, 8, T], R), alloc(top, "XTl", [128, 8, T], R))
        Wr = [alloc(top, "Wr", [128, PIECE]) for i in range(RAW_SLOTS)]
        Wh = [alloc(top, "Wh", [128, PIECE], R) for i in range(W_SLOTS)]
        Wl = [alloc(top, "Wl", [128, PIECE], R) for i in range(W_SLOTS)]
        CST = alloc(top, "CST", [128, C_GLA])
        IDB = alloc(top, "IDB", [128, 128], B16)
        MKB = alloc(top, "MKB", [128, 128], B16)
        SLB = alloc(top, "SLB", [128, 16], B16)
        GB = alloc(top, "GB", [128, 2, D])
        ST = alloc(top, "ST", [128, NT, 24])

        all_banks = [Bank(top.enter_context(nc.psum_tensor(f"PS{i}", [128, 512], F))) for i in range(8)]
        idle = list(all_banks)

        def take():
            return idle.pop(0)

        def give(b, *toks):
            b.free = list(toks)
            idle.append(b)

        IDN = CST[:, C_ID:C_ID + 128]

        def logs():
            AC.quiet([], act.preload_act_table_set, "natural_log_exp_and_others")

        def lane(name):
            return [sem(name), 0]

        def tile(i):
            return slice(128 * i, 128 * i + 128)

        x_in = A["x"].rearrange("o (i p) d -> p (o i) d", p=128)
        l_x = [lane(f"l_x{i}") for i in range(NT)]
        k_x = [AC.dma([], l_x[i], act.dma_start, X[:, i, :], x_in[:, i, :]) for i in range(NT)]
        k_cst = AC.dma([], lane("l_cst"), act.dma_start, CST[:, :], A["cst"][:, 0:C_GLA])
        VE.do([k_cst], ve.tensor_copy, IDB[:, :], IDN)
        VE.do([k_cst], ve.tensor_copy, SLB[:, :], CST[:, C_SEL:C_SEL + 16])
        k_idb = VE.do([k_cst], ve.tensor_copy, MKB[:, :], CST[:, C_MASK:C_MASK + 128])

        l_g = [lane("l_g0"), lane("l_g1")]
        gb_free = [None]

        def gains(*rs):
            return [AC.dma([gb_free[0]], l_g[j], act.dma_start, GB[:, j, :],
                           r.rearrange("(o n) -> o n", o=1).broadcast_to([128, D])) for j, r in enumerate(rs)]

        l_raw = [lane(f"l_raw{i}") for i in range(RAW_SLOTS)]
        s_hi, s_lo = sem("s_hi"), sem("s_lo")
        released, places, at, slots, where = {}, [], [], {}, {}

        class Piece:
            def __init__(self, i, n, p=128):
                self.ready, self.i, self.n, self.p = (s_lo, i + 1), i, n, p
                self.t = (Wh[i % W_SLOTS], Wl[i % W_SLOTS])

            def __call__(self, a, c0, c1, p0=0, p1=128):
                return [t[p0:p1, a * self.n + c0:a * self.n + c1] for t in self.t]

        def weight(srcs, n, rows=None, p=128):
            i = len(places)
            places.append(AC.slot())
            at.append(len(AC.items))
            raw, lan = Wr[i % RAW_SLOTS], l_raw[i % RAW_SLOTS]
            a = srcs[0][0].shape[1]
            for src, c, p0 in srcs:
                pp, m = src.shape[0], src.shape[2]
                dst = raw[p0:p0 + pp, 0:a * n].rearrange("p (a n) -> p a n", n=n)[:, :, c:c + m]
                tok = SP.dma([(s_lo, i - RAW_SLOTS + 1)] if i >= RAW_SLOTS else [], lan, nc.sync.dma_start, dst, src)
            used = a * n
            free = [released[i - W_SLOTS]] if i >= W_SLOTS else []
            h, l = Wh[i % W_SLOTS], Wl[i % W_SLOTS]
            j = max(i - LOOK, 0)
            later = i >= W_SLOTS and where[i - W_SLOTS] > at[j]
            (slots[i - W_SLOTS] if later else places[j]).append(([tok] + free, act.copy, (h[0:p, 0:used], raw[0:p, 0:used]), {}, (s_hi, 1)))
            PO.items.append(([tok, (s_hi, i + 1)] + free, po.tensor_tensor,
                             (l[0:p, 0:used], raw[0:p, 0:used], h[0:p, 0:used].bitcast(F), sub), {}, (s_lo, 1)))
            return Piece(i, rows if rows else n)

        def release(w, tok):
            released[w.i] = tok
            slots[w.i] = AC.slot()
            where[w.i] = len(AC.items)

        def mm3(o, l, r, start, stop, after, sig=False):
            PE.quiet(after, pe.matmul, o, l[0], r[1], start=start, stop=False)
            PE.quiet([], pe.matmul, o, l[1], r[0], start=False, stop=False)
            f = PE.do if stop or sig else PE.quiet
            return f([], pe.matmul, o, l[0], r[0], start=False, stop=stop)

        def pair(p, *ix):
            return [t[ix] for t in p]

        def by_rows(w):
            return w.rearrange("(a p) n -> p a n", p=128)

        ALL = slice(None)

        def feature_tile(src):
            srcs = src if isinstance(src, list) else [(src, 0, 0)]
            return weight(srcs, max(c + x.shape[2] for x, c, _ in srcs)), srcs[0][0].shape[1]

        def proj_T(src, rhs, rdy):
            w, kts = feature_tile(src)
            b = take()
            for a in range(kts):
                tok = mm3(b.t[0:w.n, :], w(a, 0, w.n), pair(rhs, ALL, a, ALL), a == 0, a == kts - 1,
                          [w.ready, b.free, rdy])
            b.tok = tok
            release(w, tok)
            return b

        pending = []

        def settle():
            while pending:
                pending.pop(0)()
            f = [PE.last(), AC.last(), VE.last()]
            for q in (AC, VE):
                q.wait(*f)

        def first_T(srcs, rhs, rdy):
            ws, bs = [feature_tile(s) for s in srcs], [take() for _ in srcs]
            for i0, i1 in ((0, 2), (2, 3), (3, 4)):
                if i0 == 2:
                    settle()
                c = slice(128 * i0, 128 * i1)
                for (w, kts), b in zip(ws, bs):
                    for a in range(kts):
                        b.tok = mm3(b.t[0:w.n, c], w(a, 0, w.n), pair(rhs, ALL, a, c), a == 0, a == kts - 1,
                                    [w.ready, b.free, rdy[i0:i1]])
                    if i1 == NT:
                        release(w, b.tok)
            return bs

        def first_N(pieces, n, lhs, rdy):
            bs = [take() for _ in range(NT)]
            ws, a0 = [], 0
            for src, k in pieces:
                ws.append((weight([(src, 0, 0)], src.shape[2], rows=n), a0, k))
                a0 += k
            for i in range(NT):
                if i == 2:
                    settle()
                for w, a1, k in ws:
                    for a in range(k):
                        tok = mm3(bs[i].t[:, 0:n], pair(lhs, ALL, a1 + a, tile(i)), w(a, 0, n), a1 + a == 0,
                                  a1 + a == a0 - 1, [w.ready, bs[i].free, rdy[i]], sig=i == NT - 1 and a == k - 1)
                    if i == NT - 1:
                        release(w, tok)
                bs[i].tok = tok
            return bs

        def proj_N(pieces, n, lhs, rdy):
            bs = [take() for _ in range(NT)]
            kts, a0 = sum(k for _, k in pieces), 0
            for src, k in pieces:
                w = weight([(src, 0, 0)], src.shape[2], rows=n)
                for i in range(NT):
                    for a in range(k):
                        tok = mm3(bs[i].t[:, 0:n], pair(lhs, ALL, a0 + a, tile(i)), w(a, 0, n), a0 + a == 0,
                                  a0 + a == kts - 1, [w.ready, bs[i].free, rdy[i]], sig=i == NT - 1 and a == k - 1)
                        if tok:
                            bs[i].tok = tok
                release(w, tok)
                a0 += k
            return bs

        def cut(src, n):
            k, per = src.shape[1], max(1, PIECE // n)
            return [(src[:, j:min(j + per, k), :], min(per, k - j)) for j in range(0, k, per)]

        def outproj(src, lhs, rdy, alpha, norm=None):
            bs = [[take(), take()] for _ in range(NT)]
            kts = src.shape[1]
            tail = 4 if norm else 1
            done = []

            def product(w, a, i):
                for c in range(2):
                    b = bs[i][c]
                    tok = mm3(b.t[:, :], pair(lhs, ALL, a, tile(i)), w(0, 512 * c, 512 * c + 512), a == 0, a == kts - 1,
                              [w.ready, b.free, rdy[min(a, len(rdy) - 1)]], sig=i == NT - 1 and c == 1)
                    if tok:
                        b.tok = tok
                        if i == NT - 1 and c == 1:
                            release(w, tok)

            for a in range(kts - tail):
                w = weight([(src[:, a:a + 1, :], 0, 0)], D)
                for i in range(NT):
                    product(w, a, i)
            ws = [(weight([(src[:, a:a + 1, :], 0, 0)], D), a) for a in range(kts - tail, kts)]
            for i in range(NT):
                for w, a in ws:
                    product(w, a, i)
                for c in range(2):
                    b, xs = bs[i][c], X[:, i, 512 * c:512 * c + 512]
                    t = VE.do([b.tok, k_x[i]], ve.scalar_tensor_tensor, xs, xs, alpha, b.t[:, :], mult, add)
                    give(b, t)
                done.append(t)
                if norm:
                    norm.compute(i, t)
                    if i > 0:
                        norm.finish(i - 1)
            if norm:
                pending.append(lambda: norm.finish(NT - 1))
            return norm.toks if norm else done

        def split(pr, src, *after):
            a = AC.do(list(after), act.copy, pr[0], src)
            return VE.do([a, list(after)], ve.tensor_tensor, pr[1], src, pr[0].bitcast(F), sub)

        def rsqrt(dst, src, scale, eps, v, q, *after):
            a = VE.do(list(after), ve.tensor_scalar, v, src, scale, eps, mult, add)
            a = AC.do([a], act.activation, q, v, ACT.Ln)
            a = AC.do([a], act.activation, dst, q, ACT.Exp, scale=-0.5)
            a = VE.do([a], ve.tensor_tensor, q, dst, dst, mult)
            a = VE.do([a], ve.tensor_tensor, q, q, v, mult)
            a = VE.do([a], ve.tensor_scalar, q, q, -0.5, 1.5, mult, add)
            return VE.do([a], ve.tensor_tensor, dst, dst, q, mult)

        def transposes(blocks, b, after):
            after = [after, b.free, k_cst]
            for s, c in blocks:
                p, m = s.shape[0], int(np.prod(s.shape[1:]))
                f = PE.do if c == blocks[-1][1] else PE.quiet
                tok = f(after, pe.transpose, b.t[0:m, c:c + p], s, IDN[0:p, 0:p])
            return tok

        def to_XT(src, i, after):
            toks = []
            for c in range(2):
                b = take()
                t = transposes([(src[:, tile(4 * c + j)], 128 * j) for j in range(4)], b, [after[c]])
                ps = b.t[:, :].rearrange("p (j t) -> p j t", j=4)
                v = split(pair(XT, ALL, slice(4 * c, 4 * c + 4), tile(i)), ps, t)
                give(b, v)
                toks.append(v)
            return toks

        class RmsNorm:

            def __init__(self, row, cm, to_x=False):
                self.gt, self.H, self.to_x = gains(row), alloc(cm, "H", [128, 2, D]), to_x
                self.toks, self.used, self.v = [], [None, None], [None] * NT

            def compute(self, i, ready):
                st, h = ST[:, i, :], self.H[:, i % 2, :]
                a = AC.do([ready, self.used[i % 2]], act.activation, h, X[:, i, :], ACT.Square, accum_out=st[:, 0:1])
                r = rsqrt(st[:, 1:2], st[:, 0:1], 1.0 / D, 1e-6, st[:, 2:3], st[:, 3:4], a)
                o = X[:, i, :] if self.to_x else h
                self.o = [(X[:, j, :] if self.to_x else self.H[:, j % 2, :]) for j in range(NT)]
                self.v[i] = [VE.do([r, a, self.gt], ve.scalar_tensor_tensor, o[:, c], X[:, i, c], st[:, 1:2],
                                   GB[:, 0, c], mult, mult) for c in (slice(0, 512), slice(512, D))]
                gb_free[0] = VE.last()

            def finish(self, i):
                self.toks.append(to_XT(self.o[i], i, self.v[i]))
                self.used[i % 2] = PE.last()

        class LayerNorm:

            def __init__(self, g, b, transposed=True):
                self.gt, self.transposed, self.toks, self.v = gains(g, b), transposed, [], [None] * NT

            def compute(self, i, ready):
                st, x = ST[:, i, :], X[:, i, :]
                cs = (slice(0, 512), slice(512, D))
                for c in range(2):
                    v = VE.do([ready], ve.bn_stats, st[:, 6 * c:6 * c + 6], x[:, cs[c]])
                v = VE.do([v], ve.bn_aggr, st[:, 12:14], st[:, 0:12])
                w = [VE.do([v, self.gt], ve.scalar_tensor_tensor, x[:, c], x[:, c], st[:, 12:13], GB[:, 0, c], sub, mult)
                     for c in cs]
                r = rsqrt(st[:, 14:15], st[:, 13:14], 1.0, 1e-5, st[:, 15:16], st[:, 16:17], v)
                self.v[i] = [VE.do([w[n], r], ve.scalar_tensor_tensor, x[:, c], x[:, c], st[:, 14:15], GB[:, 1, c],
                                   mult, add) for n, c in enumerate(cs)]
                gb_free[0] = VE.last()

            def finish(self, i):
                self.toks.append(to_XT(X[:, i, :], i, self.v[i]) if self.transposed else self.v[i])

        def rope(x1, x2, o1, o2, cos, sin, t1, t2, *after):
            VE.do([list(after), k_cst], ve.tensor_tensor, t1, x2, sin, mult)
            a = VE.do([], ve.tensor_tensor, t2, x1, sin, mult)
            VE.do([a], ve.tensor_tensor, o1, x1, cos, mult)
            a = VE.do([a], ve.tensor_tensor, o2, x2, cos, mult)
            VE.do([a], ve.tensor_tensor, o1, o1, t1, sub)
            return VE.do([a], ve.tensor_tensor, o2, o2, t2, add)

        class Attention:
            def __init__(self, cm):
                self.P = [alloc(cm, "P", [128, 1280]) for i in range(2)]
                self.PT = [alloc(cm, "PT", [128, 1280]) for i in range(2)]
                self.sm = [alloc(cm, "sm", [128, 20]) for i in range(2)]
                self.p_free, self.t_free, self.n, self.m, self.flip = [None, None], [None, None], 0, 0, 0

            def scores(self, q, k, rdy, extra=(), gate=None):
                s = self.n % 2
                self.n += 1
                P, sm = self.P[s], self.sm[s]
                toks = []
                for i in range(NT):
                    n = (i + 1) * 128
                    b = take()
                    PE.quiet([b.free, rdy], pe.matmul, b.t[:, 0:n], q(i), k(n), start=True, stop=False)
                    for l, r in extra:
                        PE.quiet([], pe.matmul, b.t[:, 0:n], l(i), r(n), start=False, stop=False)
                    t = PE.do([k_idb], pe.matmul, b.t[:, n - 128:n], IDB[:, :], MKB[:, :], start=False, stop=True)
                    v = VE.do([t, self.p_free[s]], ve.reduce_max, sm[:, i:i + 1], b.t[:, 0:n], AX.X, negate=True)
                    a = AC.do([v, self.p_free[s]], act.activation, P[:, OFF[i]:OFF[i] + n], b.t[:, 0:n], ACT.Exp,
                              bias=sm[:, i:i + 1], accum_out=sm[:, 4 + i:5 + i])
                    give(b, a)
                    toks.append(a)
                return s, toks, gate

            def normalise(self, sc):
                s, toks, gate = sc
                P, sm = self.P[s], self.sm[s]
                v = VE.do([toks], ve.reciprocal, sm[:, 8:12], sm[:, 4:8])
                if gate is not None:
                    v = VE.do([v], ve.tensor_tensor, sm[:, 8:12], sm[:, 8:12], gate, mult)
                for i in range(NT):
                    n = (i + 1) * 128
                    p = P[:, OFF[i]:OFF[i] + n]
                    v2 = VE.do([v], ve.tensor_scalar, p, p, sm[:, 8 + i:9 + i], None, mult)
                return s, v2

            def evacuate(self, dst, src, after):
                self.flip ^= 1
                if self.flip:
                    return AC.do(after, act.copy, dst, src)
                return VE.do(after, ve.tensor_copy, dst, src)

            def turn(self, ps):
                s, done = ps
                m = self.m % 2
                self.m += 1
                P, PT = self.P[s], self.PT[m]
                evs = []
                for js, base in (((0,), 0), ((1, 3), 512), ((2,), 1024)):
                    b = take()
                    cols = [(i, j) for j in js for i in range(j, NT)]
                    n = 128 * len(cols)
                    t = transposes([(P[:, OFF[i] + 128 * j:OFF[i] + 128 * j + 128], 128 * c)
                                    for c, (i, j) in enumerate(cols)], b, done)
                    e = self.evacuate(PT[:, base:base + n], b.t[:, 0:n], [t, self.t_free[m]])
                    give(b, e)
                    evs.append(e)
                self.p_free[s] = PE.last()
                return m, evs

            def values(self, turned, v, o, rdy, start=True, stop=True):
                m, evs = turned
                PT = self.PT[m]
                src = (0, 512, 1024, 896)
                for j in range(NT):
                    f = PE.quiet if j < NT - 1 else PE.do
                    tok = f([evs, rdy], pe.matmul, o[:, 128 * j:512], v(j), PT[:, src[j]:src[j] + 512 - 128 * j],
                            start=start and j == 0, stop=stop and j == NT - 1)
                self.t_free[m] = tok
                return tok

        def heads(n, att, score, value, fills):
            first, new = score(0), score(1)
            ps = att.normalise(first)
            for h in range(n):
                turned = att.turn(ps)
                if h + 1 < n:
                    ps = att.normalise(new)
                if h + 2 < n:
                    new = score(h + 2)
                value(h, turned)
                fills.share(h, n - LAST)

        class Fills:

            def __init__(self, *jobs):
                self.jobs, self.all, self.done = list(jobs), len(jobs), {}

            def one(self):
                name, f = self.jobs.pop(0)
                self.done[name] = f()

            def start(self, n):
                for _ in range(n):
                    self.one()
                self.all = len(self.jobs)

            def get(self, name):
                while name not in self.done:
                    self.one()
                return self.done[name]

            def share(self, h, n):
                while self.jobs and (self.all - len(self.jobs)) * n < self.all * (h + 1):
                    self.one()

        class Gates:

            def __init__(self, src, rdy, GT):
                self.src, self.rdy, self.GT, self.n, self.toks, self.wait, self.out = src, rdy, GT, 0, [None] * 8, [], [None] * 8

            def job(self, f):
                def run():
                    b = proj_T(self.src[:, :, tile(f)], XT, self.rdy)
                    a = AC.do([b.tok], act.activation, self.GT[:, f, :], b.t[:, :], ACT.Tanh, scale=0.5)
                    v = VE.do([a], ve.scalar_tensor_tensor, self.GT[:, f, :], self.GT[:, f, :], 1.0, b.t[:, :], add, mult)
                    give(b, v)
                    self.toks[f] = v
                    self.last_read = b.tok
                    return v
                return (f"g{f}", run)

            def output(self, f, ob, tok, fills):
                fills.get(f"g{f}")
                G = self.GT[:, f, :]
                v = VE.do([tok, self.toks[f]], ve.scalar_tensor_tensor, G, G, 0.5, ob.t[:, :], mult, mult)
                give(ob, v)
                self.wait.append((f, v))
                for _ in range(8 if f == 7 else 2):
                    if self.wait and not fills.jobs:
                        f, v = self.wait.pop(0)
                        self.out[f] = split(pair(XT, ALL, f, ALL), self.GT[:, f, :], v, self.last_read)

        def half(h):
            return slice(64 * (h % 2), 64 * (h % 2) + 64)

        def ffn(ready, cm, norm):
            wg, wu, wd = by_rows(A["w_ffn_gate"][0]), by_rows(A["w_ffn_up"][0]), by_rows(A["w_ffn_down"][0])
            HT = [(alloc(cm, "HTh", [128, 8, T], R), alloc(cm, "HTl", [128, 8, T], R)) for _ in range(2)]
            sg = [alloc(cm, "sg", [128, T]) for _ in range(2)]
            hf = [alloc(cm, "hf", [128, T]) for _ in range(2)]
            f0, n, used = 0, 0, [None, None]
            free = [None, None]
            early = first_T([m[:, :, tile(f)] for f in range(2) for m in (wg, wu)], XT, ready)
            for g, cnt in enumerate((8, 7, 7)):
                H, toks = HT[g % 2], []
                for f in range(cnt):
                    c = slice(128 * (f0 + f), 128 * (f0 + f) + 128)
                    bg = early.pop(0) if early else proj_T(wg[:, :, c], XT, ready)
                    bu = early.pop(0) if early else proj_T(wu[:, :, c], XT, ready)
                    s = n % 2
                    n += 1
                    a = AC.do([bg.tok, used[s]], act.activation, sg[s][:, :], bg.t[:, :], ACT.Silu)
                    give(bg, a)
                    v = VE.do([a, bu.tok, used[s]], ve.tensor_tensor, hf[s][:, :], sg[s][:, :], bu.t[:, :], mult)
                    give(bu, v)
                    toks.append(split(pair(H, ALL, f, ALL), hf[s][:, :], v, free[g % 2]))
                    used[s] = toks[-1]
                done = outproj(wd[:, f0:f0 + cnt, :], H, toks, 1.0, norm if g == 2 else None)
                free[g % 2] = PE.last()
                f0 += cnt
            return done

        def mla(li, ready, cm, norm):
            w_in = by_rows(A["mla_w_in_2"][li])
            CQ = [alloc(cm, "CQ", [128, 3, T], R) for h in "hl"]
            CK = [alloc(cm, "CK", [128, 2, T], R) for h in "hl"]
            GT = alloc(cm, "GT", [128, 8, T])
            QT = [alloc(cm, "QT", [96, T]) for i in range(2)]
            KT = [alloc(cm, "KT", [96, T]) for i in range(2)]
            QRT = alloc(cm, "QRT", [128, NT, T])
            V = alloc(cm, "V", [128, NT, D])
            cos = lambda i: CST[:, C_MROPE + 16 * i:C_MROPE + 16 * i + 16]
            sin = lambda i: CST[:, C_MROPE + 64 + 16 * i:C_MROPE + 64 + 16 * i + 16]
            scale = 96.0 ** -0.5
            gates = Gates(w_in[:, :, 672:1696], ready, GT)
            fills = Fills(*[gates.job(f) for f in range(3)], ("v0", lambda: vals(0)), gates.job(3), ("v1", lambda: vals(1)),
                          *[gates.job(f) for f in range(4, 8)])
            with ExitStack() as c1:
                QN, KN = alloc(c1, "QN", [128, 384]), alloc(c1, "KN", [128, 256])
                CN = alloc(c1, "CN", [128, NT, 704])
                scr = alloc(c1, "scr", [128, 384])
                tm = alloc(c1, "tm", [128, 32])
                ln = lane(f"l_n{li}"), lane(f"l_m{li}")
                bs = first_N(cut(w_in[:, :, 0:512], 512), 512, XT, ready)
                k_n = [AC.dma([], ln[0], act.dma_start, QN[:, :], A["mla_q_norm_2"][li:li + 1, :].broadcast_to([128, 384])),
                       AC.dma([], ln[1], act.dma_start, KN[:, :], A["mla_kv_norm_2"][li:li + 1, :].broadcast_to([128, 256]))]
                got = [[] for _ in range(NT)]
                for c0, n in ((0, 512), (512, 160)):
                    if c0:
                        bs = proj_N(cut(w_in[:, :, c0:c0 + n], n), n, XT, ready)
                    for i, b in enumerate(bs):
                        got[i].append(VE.do([b.tok], ve.tensor_copy, CN[:, i, c0:c0 + n], b.t[:, 0:n]))
                        give(b, got[i][-1])
                tr = []
                for i in range(NT):
                    st = ST[:, i, :]
                    for c0, n, j, g in ((0, 384, 0, QN), (384, 256, 4, KN)):
                        x = CN[:, i, c0:c0 + n]
                        a = AC.do([got[i], AC.last()], act.activation, scr[:, 0:n], x, ACT.Square, accum_out=st[:, j:j + 1])
                        r = rsqrt(st[:, j + 1:j + 2], st[:, j:j + 1], 1.0 / n, 1e-6, st[:, j + 2:j + 3], st[:, j + 3:j + 4], a)
                        v = VE.do([r, k_n], ve.scalar_tensor_tensor, x, x, st[:, j + 1:j + 2], g[:, :], mult, mult)
                    r = rope(CN[:, i, 640:656], CN[:, i, 656:672], CN[:, i, 672:688], CN[:, i, 688:704],
                             cos(i), sin(i), tm[:, 0:16], tm[:, 16:32], v)
                    tr.append([v, r])
                fills.start(3)
                tok_c = []
                for i in range(NT):
                    b = take()
                    t = transposes([(CN[:, i, tile(j)], 128 * j) for j in range(4)], b, tr[i])
                    ps = b.t[:, :].rearrange("p (j t) -> p j t", j=4)
                    u = split(pair(CQ, ALL, ALL, tile(i)), ps[:, 0:3, :], t)
                    w = split(pair(CK, ALL, 0, tile(i)), ps[:, 3, :], t, u)
                    give(b, u, w)
                    b = take()
                    t = transposes([(CN[:, i, 512:640], 0), (CN[:, i, 672:704], 128)], b, tr[i])
                    w2 = split(pair(CK, ALL, 1, tile(i)), b.t[:, 0:128], t)
                    e = [VE.do([t, w2], ve.tensor_copy, KT[n][64:96, tile(i)], b.t[0:32, 128:256]) for n in range(2)]
                    give(b, e)
                    tok_c.append([u, w, w2, e])
            w_q = A["mla_w_q_up_2"][li].rearrange("(a p) (h c) -> p a h c", p=128, c=96)
            w_kv = A["mla_w_kv_up_2"][li].rearrange("(a p) (h c) -> p a h c", p=128, c=128)

            def vals(c):
                toks = []
                bs = proj_N([(w_kv[:, a, 8 * c:8 * c + 8, 64:128], 1) for a in range(2)], 512, CK, tok_c)
                for i, b in enumerate(bs):
                    toks.append(VE.do([b.tok], ve.tensor_copy, V[:, i, 512 * c:512 * c + 512], b.t[:, :]))
                    give(b, toks[-1])
                return toks

            with ExitStack() as c2:
                QRn = alloc(c2, "QRn", [128, NT, T])
                RT = alloc(c2, "RT", [128, 2, 16, 16])
                bs = proj_N([(w_q[:, a, :, 64:96], 1) for a in range(3)], 512, CQ, tok_c)
                qn = []
                for i, b in enumerate(bs):
                    v = VE.do([b.tok], ve.tensor_scalar, QRn[:, i, :], b.t[:, :], scale, None, mult)
                    give(b, v)
                    q4 = QRn[:, i, :].rearrange("p (h c) -> p h c", c=32)
                    x1, x2 = q4[:, :, 0:16], q4[:, :, 16:32]
                    cs = [x.unsqueeze(1).broadcast_to([128, 16, 16]) for x in (cos(i), sin(i))]
                    qn.append(rope(x1, x2, x1, x2, cs[0], cs[1], RT[:, 0], RT[:, 1], v, VE.last()))
                fills.start(1)
                qrt = []
                for c in range(4):
                    b = take()
                    t = transposes([(QRn[:, i, tile(c)], 128 * i) for i in range(NT)], b, qn)
                    a = AC.do([t], act.copy, QRT[:, c, :], b.t[:, :])
                    give(b, a)
                    qrt.append(a)
            att = Attention(cm)
            w_qh, w_kh = by_rows(A["mla_w_q_up_2"][li]), by_rows(A["mla_w_kv_up_2"][li])
            free = [None, None]

            def prepare(h):
                s = h % 2
                b = proj_T(w_qh[:, :, 96 * h:96 * h + 96], CQ, tok_c)
                e1 = AC.do([b.tok, free[s]], act.mul, QT[s][0:64, :], b.t[0:64, :], scale)
                give(b, e1)
                e2 = VE.do([qrt, free[s]], ve.tensor_copy, QT[s][64:96, :], QRT[32 * (h % 4):32 * (h % 4) + 32, h // 4, :])
                b = proj_T(w_kh[:, :, 128 * h:128 * h + 128], CK, tok_c)
                e3 = VE.do([b.tok, free[s]], ve.tensor_copy, KT[s][0:64, :], b.t[0:64, :])
                give(b, e3)
                return [e1, e2, e3]

            prep, ob = [prepare(0), prepare(1)], [None]

            def score(h):
                s = h % 2
                sc = att.scores(lambda i: QT[s][:, tile(i)], lambda n: KT[s][:, 0:n], [prep[h], tok_c])
                free[s] = PE.last()
                if h == 0:
                    prep.append(prepare(2))
                return sc

            def value(h, turned):
                if h + 3 < 16:
                    prep.append(prepare(h + 3))
                if h % 2 == 0:
                    ob[0] = take()
                vt = fills.get(f"v{h // 8}")
                tk = att.values(turned, lambda j: V[:, j, 64 * h:64 * h + 64], ob[0].t[half(h), :], [vt, ob[0].free])
                if h % 2:
                    gates.output(h // 2, ob[0], tk, fills)

            heads(16, att, score, value, fills)
            logs()
            return outproj(by_rows(A["mla_w_out_2"][li]), XT, gates.out, ALPHA, norm)

        def swa(ready, cm, norm):
            w = by_rows(A["swa_w_in_2"][0])
            QT, KT = alloc(cm, "QT", [128, 8, T]), alloc(cm, "KT", [128, 2, T])
            V, GT = alloc(cm, "V", [128, NT, 256]), alloc(cm, "GT", [128, 8, T])
            SB = [alloc(cm, "SB", [128, 2, T]) for _ in range(2)]
            P = [alloc(cm, "P", [128, 2, T]) for _ in range(2)]
            PT = [alloc(cm, "PT", [128, 7, 128]) for _ in range(2)]
            sm = [alloc(cm, "sm", [128, 20]) for _ in range(2)]
            SK = alloc(cm, "SK", [128, 16])
            def q_cols(c, a):
                return [(w[:, :, 64 * (8 * c + a):64 * (8 * c + a) + 64], 0, 0),
                        (w[:, :, 64 * (8 * c + 4 + a):64 * (8 * c + 4 + a) + 64], 64, 0)]

            early = dict(zip(("k0", "q00", "q01", "q02"),
                             first_T([w[:, :, 1024:1152]] + [q_cols(0, a) for a in range(3)], XT, ready)))
            k_s = AC.dma([], lane("l_sk"), act.dma_start, SK[:, :], A["swa_sinks_2"].broadcast_to([128, 16]))
            inits = [VE.do([], ve.memset, SB[s][:, 0, 0:128], -1e30) for s in range(2)]
            def queries(c, a):
                def run():
                    b = early.pop(f"q{c}{a}", None) or proj_T(q_cols(c, a), XT, ready)
                    e = AC.do([b.tok], act.mul, QT[:, 4 * c + a, :], b.t[:, :], 0.125)
                    give(b, e)
                    return e
                return (f"q{c}{a}", run)

            def keys(c):
                def run():
                    b = early.pop(f"k{c}", None) or proj_T(w[:, :, 1024 + 128 * c:1152 + 128 * c], XT, ready)
                    e = VE.do([b.tok], ve.tensor_copy, KT[:, c, :], b.t[:, :])
                    give(b, e)
                    return e
                return (f"k{c}", run)

            def vals():
                toks = []
                bs = proj_N(cut(w[:, :, 1280:1536], 256), 256, XT, ready)
                for i, b in enumerate(bs):
                    toks.append(VE.do([b.tok], ve.tensor_copy, V[:, i, :], b.t[:, 0:256]))
                    give(b, toks[-1])
                return toks

            gates = Gates(w[:, :, 1536:2560], ready, GT)
            fills = Fills(keys(0), queries(0, 0), queries(0, 1), queries(0, 2), ("v", vals), queries(0, 3), gates.job(0),
                          gates.job(1), keys(1), queries(1, 0), gates.job(2), queries(1, 1), gates.job(3), queries(1, 2),
                          gates.job(4), queries(1, 3), gates.job(5), gates.job(6), gates.job(7))
            fills.start(4)
            DIST = CST[:, C_DIST:C_DIST + 256].unsqueeze(1)
            p_free, t_free = [None, None], [None, None]

            def scores(h):
                s, g = h % 2, h // 4
                c, r = g // 2, half(g)
                q_tok = [fills.get(f"k{c}"), fills.get(f"q{c}{h % 4}")]
                S, p, m = SB[s], P[s], sm[s]
                slope = 2.0 ** (-0.5 * (h + 1))
                for u in range(2):
                    b = take()
                    for i in (2 * u, 2 * u + 1):
                        lo = max(0, i - 1)
                        o = b.t[:, (256 * (i % 2) + 128 if i == 0 else 256 * (i % 2)):256 * (i % 2) + 256]
                        t = PE.do([b.free, q_tok], pe.matmul, o, QT[r, 4 * c + h % 4, tile(i)],
                                  KT[r, c, 128 * lo:128 * i + 128], start=True, stop=True)
                    if u == 0:
                        v = VE.do([t, p_free[s]], ve.scalar_tensor_tensor, S[:, 0, 128:256], CST[:, C_DIST + 128:C_DIST + 256],
                                  -slope, b.t[:, 128:256], mult, add)
                        v = VE.do([t], ve.scalar_tensor_tensor, S[:, 0, 256:512], CST[:, C_DIST:C_DIST + 256],
                                  -slope, b.t[:, 256:512], mult, add)
                    else:
                        v = VE.do([t], ve.scalar_tensor_tensor, S[:, 1, :].rearrange("p (i k) -> p i k", i=2),
                                  DIST.broadcast_to([128, 2, 256]), -slope,
                                  b.t[:, :].rearrange("p (i k) -> p i k", i=2), mult, add)
                    give(b, v)
                    v = VE.do([v, inits], ve.reduce_max, m[:, 2 * u:2 * u + 2], S[:, u, :].rearrange("p (i k) -> p i k", i=2), AX.X)
                v = VE.do([v, k_s], ve.tensor_scalar, m[:, 0:4], m[:, 0:4], SK[:, h:h + 1], -1.0, ALU.max, mult)
                for i in range(NT):
                    a = AC.do([v, p_free[s]], act.activation, p[:, i // 2, 256 * (i % 2):256 * (i % 2) + 256],
                              S[:, i // 2, 256 * (i % 2):256 * (i % 2) + 256], ACT.Exp, bias=m[:, i:i + 1],
                              accum_out=m[:, 4 + i:5 + i])
                return s, AC.do([v], act.activation, m[:, 8:12], m[:, 0:4], ACT.Exp, bias=SK[:, h:h + 1])

            def normalise(sc):
                s, a = sc
                p, m = P[s], sm[s]
                v = VE.do([a], ve.tensor_tensor, m[:, 4:8], m[:, 4:8], m[:, 8:12], add)
                v = VE.do([v], ve.reciprocal, m[:, 12:16], m[:, 4:8])
                for i in range(NT):
                    x = p[:, i // 2, 256 * (i % 2):256 * (i % 2) + 256]
                    v2 = VE.do([v], ve.tensor_scalar, x, x, m[:, 12 + i:13 + i], None, mult)
                return s, v2

            def turn(sc):
                s, done = sc
                p, pt = P[s], PT[s]
                evs = []
                for part in (blocks[0:4], blocks[4:7]):
                    b = take()
                    n0 = 0 if part[0] == blocks[0] else 4
                    t = transposes([(p[:, i // 2, 256 * (i % 2) + (128 if i == j else 0):256 * (i % 2) + (256 if i == j else 128)],
                                     128 * x) for x, (j, i) in enumerate(part)], b, done)
                    dst, src = pt[:, n0:n0 + len(part), :].rearrange("p a b -> p (a b)"), b.t[:, 0:128 * len(part)]
                    e = (VE.do([t, t_free[s]], ve.tensor_copy, dst, src) if n0 else AC.do([t, t_free[s]], act.copy, dst, src))
                    give(b, e)
                    evs.append(e)
                p_free[s] = PE.last()
                return s, evs

            blocks = [(j, i) for j in range(NT) for i in (j, j + 1) if i < NT]

            def values(h, turned, o, rdy):
                s, evs = turned
                pt = PT[s]
                for i in range(NT):
                    js = [j for j in (i - 1, i) if j >= 0]
                    for j in js:
                        f = PE.do if (i, j) == (NT - 1, NT - 1) else PE.quiet
                        tok = f([evs, rdy], pe.matmul, o[:, tile(i)], V[:, j, 64 * (h // 4):64 * (h // 4) + 64],
                                pt[:, blocks.index((j, i)), :], start=j == js[0], stop=j == i)
                t_free[s] = tok
                return tok

            ob = [None]

            def value(h, turned):
                if h % 2 == 0:
                    ob[0] = take()
                tk = values(h, turned, ob[0].t[half(h), :], [ob[0].free, fills.get("v")])
                if h % 2:
                    gates.output(h // 2, ob[0], tk, fills)

            class Banded:
                pass
            banded = Banded()
            banded.normalise, banded.turn = normalise, turn
            heads(16, banded, scores, value, fills)
            logs()
            return outproj(by_rows(A["swa_w_out_2"][0]), XT, gates.out, ALPHA, norm)

        def log_sigmoid(dst, z, t, scale, after):
            a = AC.do(after, act.activation, t, z, ACT.Abs)
            a = AC.do([a], act.activation, t, t, ACT.Exp, scale=-1.0)
            a = AC.do([a], act.activation, t, t, ACT.Ln, bias=1.0)
            v = VE.do([after, a], ve.tensor_scalar, z, z, 0.0, scale, ALU.min, mult)
            return VE.do([v, a], ve.scalar_tensor_tensor, dst, t, -scale, z, mult, add)

        def fox(ready, cm, norm):
            w = by_rows(A["fox_w_in_2"][0])
            QT, KT = alloc(cm, "QT", [128, 8, T]), alloc(cm, "KT", [128, 8, T])
            V, GT = alloc(cm, "V", [128, NT, D]), alloc(cm, "GT", [128, 8, T])
            CB = [alloc(cm, "CB", [96, T], B16) for _ in range(2)]
            bf, *bs = first_T([w[:, :, 3072:3200], w[:, :, 0:128], w[:, :, 1024:1152]], XT, ready)
            early = dict(zip(("q0", "k0"), bs))
            zero = VE.do([], ve.memset, CB[0][:, :], 0.0)
            zero = VE.do([], ve.memset, CB[1][:, :], 0.0)
            with ExitStack() as c1:
                FZ, FT, FC = (alloc(c1, n, [16, T]) for n in ("FZ", "FT", "FC"))
                FB = alloc(c1, "FB", [16, 1])
                k_f = AC.dma([], lane("l_fb"), act.dma_start, FB[:, :], A["fox_b_f_2"].rearrange("o h -> h o"))
                v = VE.do([bf.tok, k_f], ve.tensor_scalar, FZ[:, :], bf.t[0:16, :], FB[:, 0:1], None, add)
                give(bf, v)
                v = log_sigmoid(FC[:, :], FZ[:, :], FT[:, :], 1.0, [v])
                one = VE.do([v], ve.memset, FT[:, :], 1.0)
                v = VE.do([v, one], ve.tensor_tensor_scan, FZ[:, :], FT[:, :], FC[:, :], 0.0, mult, add)
                for k in range(3):
                    c = CB[0][32 * k:32 * k + 16, :]
                    v = VE.do([v, zero], ve.tensor_copy, c, FZ[:, :])
                    v2 = VE.do([v], ve.tensor_scalar, CB[1][32 * k:32 * k + 16, :], c, -1.0, None, mult)
                    if k < 2:
                        v = VE.do([v], ve.tensor_copy, FT[:, :], c)
                        v = VE.do([v], ve.tensor_tensor, FZ[:, :], FZ[:, :], FT[:, :], sub)
                cb = v2
            def queries(f):
                def run():
                    b = early.pop(f"q{f}", None) or proj_T(w[:, :, tile(f)], XT, ready)
                    e = AC.do([b.tok], act.mul, QT[:, f, :], b.t[:, :], 0.125)
                    give(b, e)
                    return e
                return (f"q{f}", run)

            def keys(f):
                def run():
                    b = early.pop(f"k{f}", None) or proj_T(w[:, :, 1024 + 128 * f:1152 + 128 * f], XT, ready)
                    e = VE.do([b.tok], ve.tensor_copy, KT[:, f, :], b.t[:, :])
                    give(b, e)
                    return e
                return (f"k{f}", run)

            def vals(c):
                def run():
                    toks = []
                    bs = proj_N(cut(w[:, :, 2048 + 512 * c:2560 + 512 * c], 512), 512, XT, ready)
                    for i, b in enumerate(bs):
                        toks.append(VE.do([b.tok], ve.tensor_copy, V[:, i, 512 * c:512 * c + 512], b.t[:, :]))
                        give(b, toks[-1])
                    return toks
                return (f"v{c}", run)

            gates = Gates(w[:, :, 3088:4112], ready, GT)
            jobs = [queries(0), keys(0), vals(0), gates.job(0)]
            for f in range(1, 8):
                jobs += [queries(f), keys(f)] + ([vals(1)] if f == 3 else []) + [gates.job(f)]
            fills = Fills(*jobs)
            fills.start(3)
            att, ob = Attention(cm), [None]

            def score(h):
                sel = SLB[0:96, h:h + 1]
                return att.scores(lambda i: QT[half(h), h // 2, tile(i)], lambda n: KT[half(h), h // 2, 0:n],
                                  [fills.get(f"q{h // 2}"), fills.get(f"k{h // 2}"), cb],
                                  extra=[(lambda i: CB[0][:, tile(i)], lambda n: sel.broadcast_to([96, n])),
                                         (lambda i: sel.broadcast_to([96, 128]), lambda n: CB[1][:, 0:n])])

            def value(h, turned):
                if h % 2 == 0:
                    ob[0] = take()
                tk = att.values(turned, lambda j: V[:, j, 64 * h:64 * h + 64], ob[0].t[half(h), :],
                                [fills.get(f"v{h // 8}"), ob[0].free])
                if h % 2:
                    gates.output(h // 2, ob[0], tk, fills)

            heads(16, att, score, value, fills)
            logs()
            return outproj(by_rows(A["fox_w_out_2"][0]), XT, gates.out, ALPHA, norm)

        def stream(name, src, n, lhs, rdy, post):
            pieces = cut(src, n)
            kts, st = src.shape[1], {}

            def run(j):
                def f():
                    if j == 0:
                        st["b"] = [take() for _ in range(NT)]
                    a0 = sum(k for _, k in pieces[:j])
                    w, k = weight([(pieces[j][0], 0, 0)], n, rows=n), pieces[j][1]
                    for i, b in enumerate(st["b"]):
                        for a in range(k):
                            tok = mm3(b.t[:, 0:n], pair(lhs, ALL, a0 + a, tile(i)), w(a, 0, n), a0 + a == 0,
                                      a0 + a == kts - 1, [w.ready, b.free, rdy[i]], sig=i == NT - 1 and a == k - 1)
                        b.tok = tok
                    release(w, tok)
                    if j == len(pieces) - 1:
                        return [post(i, b) for i, b in enumerate(st["b"])]
                return f
            return [(name if j == len(pieces) - 1 else f"{name}.{j}", run(j)) for j in range(len(pieces))]

        def mix(ready, cm, make_norm):
            w = by_rows(A["w_in"][0])
            OB = [alloc(cm, "OB", [128, 4, T], R) for h in "hl"]
            with ExitStack() as c1:
                n = Nsa(w, ready, c1)
                done_b = gla(w, ready, OB, n)
                settle()
                OA = [alloc(cm, "OA", [128, 4, T], R, side="right") for h in "hl"]
                done_a = n.attend(OA)
            settle()
            with ExitStack() as c1:
                MT = (alloc(c1, "MTh", [128, 8, T], R), alloc(c1, "MTl", [128, 8, T], R))
                sg = [alloc(c1, "sg", [128, T]) for _ in range(4)]
                wa, wb = by_rows(A["w_up_nsa"][0]), by_rows(A["w_up_gla"][0])
                used, toks = [None, None], []
                for f in range(8):
                    s = f % 2
                    ga, gb = sg[2 * s], sg[2 * s + 1]
                    b2 = proj_T(w[:, :, 3880 + 128 * f:4008 + 128 * f], XT, ready)
                    a2 = AC.do([b2.tok, used[s]], act.activation, gb[:, :], b2.t[:, :], ACT.Tanh, scale=0.5)
                    give(b2, a2)
                    b3 = proj_T(wa[:, :, tile(f)], OA, done_a)
                    v1 = VE.do([n.ga[f], b3.tok, used[s]], ve.scalar_tensor_tensor, ga[:, :], n.GA(f), 1.0, b3.t[:, :], add, mult)
                    give(b3, v1)
                    b4 = proj_T(wb[:, :, tile(f)], OB, done_b)
                    v2 = VE.do([a2, b4.tok], ve.scalar_tensor_tensor, gb[:, :], gb[:, :], 1.0, b4.t[:, :], add, mult)
                    give(b4, v2)
                    v = VE.do([v2], ve.tensor_tensor, ga[:, :], ga[:, :], gb[:, :], add)
                    a = AC.do([v], act.mul, MT[0][:, f, :], ga[:, :], 0.5)
                    used[s] = VE.do([a], ve.scalar_tensor_tensor, MT[1][:, f, :], ga[:, :], 0.5, MT[0][:, f, :].bitcast(F), mult, sub)
                    toks.append(used[s])
                    if f % 2:
                        k_x[f // 2] = AC.dma([v1], l_x[f // 2], act.dma_start, X[:, f // 2, :], x_in[:, f // 2, :])
                norm = make_norm(c1)
                logs()
                return outproj(by_rows(A["w_out"][0]), MT, toks, 1.0, norm)

        class Nsa:

            def __init__(self, w, ready, cm):
                self.w, self.ready, self.cm = w, ready, cm
                self.QR, self.QT = alloc(cm, "QR", [128, 4, T]), alloc(cm, "QT", [128, 4, T])
                self.KV = alloc(cm, "KV", [128, NT, T])
                self.KS = [alloc(cm, "KS", [128, T]) for _ in range(2)]
                self.GN = alloc(cm, "GN", [128, NT, 24])
                self.KC, self.VC = alloc(cm, "KC", [128, 32]), alloc(cm, "VC", [32, 2, 64])
                self.ga, self.c_tok = [None] * 8, []

            def GA(self, f):
                return X[:, f // 2, 512 * (f % 2):512 * (f % 2) + 512]

            def jobs(self, c1):
                w, ready, QR, QT, KV, KS = self.w, self.ready, self.QR, self.QT, self.KV, self.KS
                cos = CST[:, C_NROPE:C_NROPE + 32].rearrange("p (i c) -> p i c", c=8)
                sin = CST[:, C_NROPE + 32:C_NROPE + 64].rearrange("p (i c) -> p i c", c=8)
                KX, c2, c3 = [], ExitStack(), ExitStack()
                tm = alloc(c1, "tm", [128, 2, 64])
                PF = [alloc(c1, "PF", [32, 128]) for _ in range(2)]
                W2 = [alloc(c1, "W2", [128, 64]) for _ in range(2)]
                Z = alloc(c1, "Z", [128, 16])
                HB, HC, HT = alloc(c1, "HB", [128, 4]), alloc(c1, "HC", [128, 4, 32]), alloc(c1, "HT", [128, 4, 32])
                qn = [alloc(c2, "qn", [128, T])[:, :] for i in range(NT)]
                lz = [lane(f"l_c{j}") for j in range(2)]
                z = VE.do([], ve.memset, Z[:, :], 0.0)
                kd = {}
                for j, nm in enumerate(("k", "v")):
                    for g in range(2):
                        AC.dma([], lz[j], act.dma_start, PF[j][:, 64 * g:64 * g + 64], A[f"cmp_pe_{nm}"][0])
                    kd[j] = AC.dma([], lz[j], act.dma_start, W2[j][:, :], A[f"cmp_{nm}_w2"][0])
                self.q_tok, self.qt_tok, self.k_tok, k_rot = [], [], [], []

                def q_out(i, b):
                    e = AC.do([b.tok], act.mul, qn[i].rearrange("p (a g d) -> p g a d", a=4, g=2),
                              b.t[:, :].rearrange("p (g a d) -> p g a d", a=4, g=2), 0.125)
                    give(b, e)
                    return e

                def turned(dst, out):
                    def f():
                        src = fills_of["q"] if dst is QR else self.rot
                        for a in range(4):
                            b = take()
                            t = transposes([(qn[i][:, tile(a)], 128 * i) for i in range(NT)], b, src)
                            e = AC.do([t], act.copy, dst[:, a, :], b.t[:, :])
                            give(b, e)
                            out.append(e)
                        if dst is QR:
                            self.rot = []
                            for i in range(NT):
                                q4 = qn[i].rearrange("p (h c) -> p h c", c=64)
                                cs = [x[:, i, :].unsqueeze(1).broadcast_to([128, 8, 8]) for x in (cos, sin)]
                                t2 = [tm[:, u, :].rearrange("p (h c) -> p h c", c=8) for u in range(2)]
                                self.rot.append(rope(q4[:, :, 0:8], q4[:, :, 8:16], q4[:, :, 0:8], q4[:, :, 8:16],
                                                     cs[0], cs[1], t2[0], t2[1], t, VE.last()))
                        else:
                            self.q_read = t
                            c2.close()
                    return f

                fills_of = {}

                def kv_out(i, b):
                    v = VE.do([b.tok], ve.tensor_copy, KV[:, i, :], b.t[:, :])
                    give(b, v)
                    cs = [x[:, i, :].unsqueeze(1).broadcast_to([128, 2, 8]) for x in (cos, sin)]
                    for c in (0, 256):
                        k4 = KV[:, i, c:c + 128].rearrange("p (g c) -> p g c", c=64)
                        t = [tm[:, u, 0:16].rearrange("p (h c) -> p h c", c=8) for u in range(2)]
                        v = rope(k4[:, :, 0:8], k4[:, :, 8:16], k4[:, :, 0:8], k4[:, :, 8:16], cs[0], cs[1],
                                 t[0], t[1], v, VE.last())
                    k_rot.append(v)
                    return v

                def keys():
                    for c in range(2):
                        b = take()
                        t = transposes([(KV[:, i, 256 * c:256 * c + 128], 128 * i) for i in range(NT)], b, k_rot)
                        e = VE.do([t], ve.tensor_copy, KS[c][:, :], b.t[:, :])
                        give(b, e)
                        self.k_tok.append(e)

                def g_out(i, b):
                    e = AC.do([b.tok], act.activation, self.GN[:, i, :], b.t[:, 0:24], ACT.Tanh, scale=0.5)
                    give(b, e)
                    return VE.do([e], ve.tensor_scalar, self.GN[:, i, :], self.GN[:, i, :], 0.5, 0.5, mult, add)

                def gate_job():
                    self.g_tok = [g_out(i, b) for i, b in enumerate(proj_N([(w[:, :, 1280:1304], 8)], 24, XT, ready))]

                hb, kx = {}, {}

                def blocks_in(j):
                    def f():
                        b = proj_T(w[:, :, 512 + 128 * j:640 + 128 * j], XT, ready)
                        if j == 0:
                            KX.extend([alloc(c3, "KX", [128, 560], R) for h in "hl"] for _ in range(2))
                        K = KX[j]
                        t1 = split([K[0][:, 0:512], K[1][:, 0:512]], b.t[:, :], b.tok, self.q_read)
                        give(b, t1)
                        b = take()
                        t = transposes([(PF[j][:, :], 0)], b, [kd[j]])
                        t2 = split([K[0][:, 528:560], K[1][:, 528:560]], b.t[:, 0:32], t)
                        give(b, t2)
                        kx[j] = [t1, t2, split([K[0][:, 512:528], K[1][:, 512:528]], Z[:, :], z)]
                        hb[j] = [take(), take()]
                    return f

                def blocks_mid(j, l0):
                    def f():
                        w1 = A[f"cmp_{'kv'[j]}_w1"][0].rearrange("(l d) n -> d l n", d=64)
                        wt = weight([(w1[:, l0:l0 + 8, :], 0, 0), (w1[:, l0:l0 + 8, :], 0, 64)], 128)
                        for g in range(2):
                            for l in range(8):
                                rs = slice(64 * g, 64 * g + 64)
                                rh = [KX[j][h][rs, l0 + l:l0 + l + 529:16] for h in range(2)]
                                tok = mm3(hb[j][g].t[:, 0:34], wt(l, 0, 128, 64 * g, 64 * g + 64), rh, l0 + l == 0,
                                          l0 + l == 31, [wt.ready, hb[j][g].free, kx[j]], sig=g == 1 and l == 7)
                                if tok:
                                    hb[j][g].tok = tok
                        release(wt, tok)
                        if l0 == 24:
                            kx[j] = []
                            for g in range(2):
                                x = 2 * j + g
                                v = VE.do([hb[j][g].tok], ve.tensor_copy, HB[:, x:x + 1], hb[j][g].t[:, 33:34])
                                v = VE.do([v], ve.tensor_scalar, HC[:, x, 0:31], hb[j][g].t[:, 0:31], HB[:, x:x + 1], None, add)
                                give(hb[j][g], v)
                                e = AC.do([v], act.activation, HT[:, x, 0:31], HC[:, x, 0:31], ACT.Tanh, scale=0.5)
                                kx[j].append(VE.do([e], ve.scalar_tensor_tensor, HC[:, x, 0:31], HT[:, x, 0:31], 1.0,
                                                   HC[:, x, 0:31], add, mult))
                    return f

                def blocks_out():
                    for j in range(2):
                        for g in range(2):
                            x = 2 * j + g
                            b = take()
                            if j == 0:
                                o = b.t[64 * g:64 * g + 64, 0:31]
                                t = PE.do([kx[j], kd[j], b.free], pe.matmul, o, W2[0][:, :], HC[:, x, 0:31], start=True, stop=True)
                                dst = self.KC[64 * g:64 * g + 64, 0:31]
                            else:
                                o = b.t[0:31, 0:64]
                                t = PE.do([kx[j], kd[j], b.free], pe.matmul, o, HC[:, x, 0:31], W2[1][:, :], start=True, stop=True)
                                dst = self.VC[0:31, g, :]
                            c = VE.do([t], ve.tensor_scalar, dst, o, 0.5, None, mult)
                            give(b, c)
                            self.c_tok.append(c)
                    c3.close()

                def q_all(i, b):
                    fills_of.setdefault("q", []).append(q_out(i, b))

                return (stream("q", w[:, :, 0:512], 512, XT, ready, q_all)
                        + [("qr", turned(QR, self.q_tok))]
                        + stream("kv", w[:, :, 768:1280], 512, XT, ready, kv_out)
                        + [("qt", turned(QT, self.qt_tok)), ("g", gate_job), ("kt", keys)]
                        + [("ck", blocks_in(0))] + [(f"ck{l}", blocks_mid(0, l)) for l in range(0, 32, 8)]
                        + [("cv", blocks_in(1))] + [(f"cv{l}", blocks_mid(1, l)) for l in range(0, 32, 8)]
                        + [("co", blocks_out)])

            def attend(self, OA):
                w, ready, cm, QR, QT, KV, KS, GN, KC, VC = (self.w, self.ready, self.cm, self.QR, self.QT,
                                                                self.KV, self.KS, self.GN, self.KC, self.VC)
                ready_q, c_tok, g_tok = self.q_tok + self.qt_tok + self.k_tok, self.c_tok, self.g_tok
                att = Attention(cm)
                MC = alloc(cm, "MC", [128, 2, NT, 32])
                PC = [alloc(cm, "PC", [128, NT, 32]) for _ in range(2)]
                CT = [alloc(cm, "CT", [32, T]) for _ in range(2)]
                cs_ = [alloc(cm, "cs", [128, 16]) for _ in range(2)]
                k_mc = AC.dma([], lane("l_mc"), act.dma_start, MC[:, :, :, :],
                              A["cmask"].rearrange("p (u i n) -> p u i n", u=2, i=NT))
                c_free = [None, None]

                def gate(f):
                    def run():
                        b = proj_T(w[:, :, 2856 + 128 * f:2984 + 128 * f], XT, ready)
                        self.ga[f] = AC.do([b.tok], act.activation, self.GA(f), b.t[:, :], ACT.Tanh, scale=0.5)
                        give(b, self.ga[f])
                    return (f"m{f}", run)

                def compressed(h):
                    s, g = h % 2, h // 4
                    b = take()
                    for i in range(NT):
                        t = PE.do([b.free, ready_q, c_tok], pe.matmul, b.t[:, 32 * i:32 * i + 31],
                                  QR[64 * g:64 * g + 64, h % 4, tile(i)], KC[64 * g:64 * g + 64, 0:31], start=True, stop=True)
                    p, c = PC[s], cs_[s]
                    x = b.t[:, 0:128].rearrange("p (i n) -> p i n", i=NT)[:, :, 0:31]
                    v = VE.do([t, k_mc, c_free[s]], ve.tensor_tensor, p[:, :, 0:31], x, MC[:, 0, :, 0:31], mult)
                    give(b, v)
                    v = VE.do([v], ve.tensor_tensor, p[:, :, 0:31], p[:, :, 0:31], MC[:, 1, :, 0:31], add)
                    v = VE.do([v], ve.reduce_max, c[:, 0:4], p[:, :, 0:31], AX.X, negate=True)
                    v = VE.do([v], ve.tensor_tensor, p[:, :, 0:31], p[:, :, 0:31],
                              c[:, 0:4].unsqueeze(2).broadcast_to([128, NT, 31]), add)
                    return s, h, AC.do([v], act.activation, p[:, :, 0:31], p[:, :, 0:31], ACT.Exp)

                def c_norm(cp):
                    s, h, a = cp
                    p, c = PC[s], cs_[s]
                    v = VE.do([a], ve.reduce_sum, c[:, 4:8], p[:, :, 0:31], AX.X)
                    v = VE.do([v], ve.reciprocal, c[:, 8:12], c[:, 4:8])
                    v = VE.do([v, g_tok], ve.tensor_tensor, c[:, 8:12], c[:, 8:12], GN[:, :, 3 * h], mult)
                    v = VE.do([a], ve.tensor_tensor, p[:, :, 0:31], p[:, :, 0:31], MC[:, 0, :, 0:31], mult)
                    v = VE.do([v], ve.tensor_tensor, p[:, :, 0:31], p[:, :, 0:31],
                              c[:, 8:12].unsqueeze(2).broadcast_to([128, NT, 31]), mult)
                    return s, v

                def c_turn(cp):
                    s, v = cp
                    b = take()
                    t = transposes([(PC[s][:, i, 0:31], 128 * i) for i in range(NT)], b, [v])
                    c_free[s] = t
                    e = AC.do([t, ct_free[s]], act.copy, CT[s][0:31, :], b.t[0:31, :])
                    give(b, e)
                    return e

                ct_free = [None, None]
                jobs = [(h, c) for h in range(8) for c in range(2)]
                done, cp, ob = [], {}, [None]

                def score(x):
                    h, c = jobs[x]
                    if c == 0:
                        cp[h] = compressed(h)
                    else:
                        cp[h] = c_norm(cp[h])
                    r = slice(64 * (h // 4), 64 * (h // 4) + 64)
                    return att.scores(lambda i: QT[r, h % 4, tile(i)], lambda n: KS[c][r, 0:n], [ready_q],
                                      gate=GN[:, :, 3 * h + 1 + c])

                def value(x, turned):
                    h, c = jobs[x]
                    g, s = h // 4, h % 2
                    if c == 0 and h % 2 == 0:
                        ob[0] = take()
                    o = ob[0].t[half(h), :]
                    if c == 0:
                        e = c_turn(cp[h])
                    tk = att.values(turned, lambda j: KV[:, j, 256 * c + 128 + 64 * g:256 * c + 192 + 64 * g], o,
                                    [ob[0].free], start=c == 0, stop=c == 1)
                    if c == 0:
                        ct_free[s] = PE.do([e], pe.matmul, o, VC[0:31, g, :], CT[s][0:31, :], start=False, stop=False)
                    if c == 1 and h % 2:
                        d = split(pair(OA, ALL, h // 2, ALL), ob[0].t[:, :], tk)
                        give(ob[0], d)
                        done.append(d)

                fills = Fills(*[gate(f) for f in range(8)])
                heads(16, att, score, value, fills)
                return done

        def gla(w, ready, OB, nsa):
            with ExitStack() as cm:
                def new(name, shape):
                    return alloc(cm, name, shape, side="right")

                GQ, GK = new("GQ", [128, 2, T]), new("GK", [128, 2, T])
                LR, W2, BC = new("LR", [16, T]), new("W2", [16, 256]), new("BC", [128, 2])
                MK = new("MK", [128, 8, 128])
                GG = new("GG", [128, 128])
                OD = new("OD", [128, 2, 6, 128])
                ss = new("ss", [128, 32])
                GV = [X[:, i // 2, 512 * (i % 2):512 * (i % 2) + 512] for i in range(NT)]
                GR = [X[:, 2 + i // 2, 512 * (i % 2):512 * (i % 2) + 512] for i in range(NT)]
                C, S, Z, EX, T1 = (new(n, [128, T])[:, :] for n in ("C", "S", "Z", "EX", "T1"))
                DG = new("DG", [128, 2, NT, 128])[:, :, :, :]
                E = [GB[:, 0, 0:512], GB[:, 0, 512:1024]]
                ON = GB[:, 1, :]
                bs = first_N(cut(w[:, :, 2344:2856], 512), 512, XT, ready)
                lz = [lane(f"l_gl{j}") for j in range(4)]
                kw = [AC.dma([], lz[0], act.dma_start, W2[:, :], A["gla_gate_w2"][0]),
                      [AC.dma([], lz[1], act.dma_start, BC[:, c:c + 1], A["gla_gate_b"][0, tile(c)].rearrange("(p o) -> p o", o=1))
                       for c in range(2)],
                      AC.dma([], lz[2], act.dma_start, GG[:, :], A["gla_norm"].broadcast_to([128, 128])),
                      AC.dma([], lz[3], act.dma_start, MK[:, :, :], A["cst"][:, C_GLA:C_END].rearrange("p (m n) -> p m n", m=8))]
                gg = VE.do([kw], ve.tensor_scalar, GG[:, :], GG[:, :], 0.5, None, mult)
                gr_tok = []
                for i, b in enumerate(bs):
                    a = AC.do([b.tok], act.activation, GR[i], b.t[:, :], ACT.Tanh, scale=0.5)
                    v = VE.do([a], ve.scalar_tensor_tensor, GR[i], GR[i], 1.0, b.t[:, :], add, mult)
                    give(b, v)
                    g4 = GR[i].rearrange("p (h v) -> p h v", h=4)
                    gr_tok.append(VE.do([v, gg], ve.tensor_tensor, g4, g4, GG[:, :].unsqueeze(1).broadcast_to([128, 4, 128]), mult))
                logs()
                toks = []
                b = proj_T(w[:, :, 2328:2456], XT, ready)
                e = AC.do([b.tok], act.copy, LR[:, :], b.t[0:16, :])
                give(b, e)
                v = None
                for dp in range(2):
                    b = take()
                    t = PE.do([b.free, kw, e], pe.matmul, b.t[:, :], W2[:, tile(dp)], LR[:, :], start=True, stop=True)
                    v = VE.do([t, v], ve.tensor_scalar, Z, b.t[:, :], BC[:, dp:dp + 1], None, add)
                    give(b, v)
                    v = log_sigmoid(E[dp], Z, T1, 1.0 / 16, [v])
                one = VE.do([v], ve.memset, T1, 1.0)
                for c in range(2):
                    b = proj_T(w[:, :, 1304 + 128 * c:1432 + 128 * c], XT, ready)
                    e = AC.do([b.tok], act.mul, GQ[:, c, :], b.t[:, :], 0.125)
                    give(b, e)
                    toks.append(e)
                    b = proj_T(w[:, :, 1560 + 128 * c:1688 + 128 * c], XT, ready)
                    e = AC.do([b.tok], act.copy, GK[:, c, :], b.t[:, :])
                    give(b, e)
                    toks.append(e)

                def gv_out(i, b):
                    e = AC.do([b.tok], act.copy, GV[i], b.t[:, :])
                    give(b, e)
                    return e

                fills = Fills(*stream("gv", w[:, :, 1816:2328], 512, XT, ready, gv_out), *nsa.jobs(cm))
                points, at = 2 * 12, [0]

                def fill():
                    fills.share(at[0], points)
                    at[0] += 1

                done = []
                levels = (256, 128, 64, 32, 16, 8, 4, 2, 1)
                read = []
                for dp in range(2):
                    c_ok = one
                    for c in range(8):
                        cs = slice(64 * c, 64 * c + 64)
                        c_ok = VE.do([one], ve.tensor_tensor_scan, C[:, cs], T1[:, cs], E[dp][:, cs], 0.0, mult, add)
                    z0 = VE.do([read], ve.memset, DG, 0.0)
                    q, k = GQ[:, dp, :], GK[:, dp, :]
                    st = {"e": [c_ok], "z": []}

                    def decays(m):
                        if m >= 128:
                            for c in range(T // m):
                                cs = slice(m * c, m * c + m)
                                ok = VE.do([st["e"], one], ve.tensor_tensor_scan, S[:, cs], T1[:, cs], E[dp][:, cs], 0.0, mult, add)
                            src = S
                        else:
                            src, ok = C, c_ok
                        s3 = src.rearrange("p (b u m) -> p b u m", u=2, m=m)
                        e3 = EX.rearrange("p (b u m) -> p b u m", u=2, m=m)
                        nb = T // (2 * m)
                        v1 = VE.do([ok, st["e"]], ve.tensor_tensor, e3[:, :, 0, :],
                                   s3[:, :, 0, m - 1:m].broadcast_to([128, nb, m]), s3[:, :, 0, :], sub)
                        if m >= 64:
                            v2 = VE.do([ok], ve.tensor_copy, e3[:, :, 1, :], s3[:, :, 1, :])
                        else:
                            v2 = VE.do([ok], ve.tensor_tensor, e3[:, :, 1, :], s3[:, :, 1, :],
                                       s3[:, :, 0, m - 1:m].broadcast_to([128, nb, m]), sub)
                        return AC.do([v1, v2], act.activation, EX, EX, ACT.Exp)

                    def decayed(m, a):
                        z3, e3, q3, k3 = (t.rearrange("p (b u m) -> p b u m", u=2, m=m) for t in (Z, EX, q, k))
                        v1 = VE.do([a, st["z"], toks], ve.tensor_tensor, z3[:, :, 0, :], e3[:, :, 0, :], k3[:, :, 0, :], mult)
                        v2 = VE.do([a], ve.tensor_tensor, z3[:, :, 1, :], e3[:, :, 1, :], q3[:, :, 1, :], mult)
                        st["e"] = [v1, v2]
                        return [v1, v2]

                    def into_DG(hh, b, t, mask):
                        v = VE.do([t, z0, kw], ve.copy_predicated, DG[:, hh, :, :],
                                  MK[:, mask, :].bitcast(I32).unsqueeze(1).broadcast_to([128, NT, 128]),
                                  b.t[:, :].rearrange("p (i t) -> p i t", i=NT))
                        give(b, v)
                        return v

                    ready_z = None
                    for li, m in enumerate((0,) + levels):
                        outs = []
                        for hh in range(2):
                            b = take()
                            r = slice(64 * hh, 64 * hh + 64)
                            if m == 0:
                                for i in range(NT):
                                    t = PE.do([b.free, toks], pe.matmul, b.t[:, tile(i)], GK[r, dp, tile(i)], GQ[r, dp, tile(i)],
                                              start=True, stop=True)
                            elif m == 256:
                                for s in range(2):
                                    t = PE.do([b.free, ready_z], pe.matmul, b.t[:, 256 * s:256 * s + 256], Z[r, tile(s)],
                                              Z[r, 256:512], start=True, stop=True)
                            elif m == 128:
                                for s in range(2):
                                    t = PE.do([b.free, ready_z], pe.matmul, b.t[:, tile(s)], Z[r, tile(2 * s)],
                                              Z[r, tile(2 * s + 1)], start=True, stop=True)
                            else:
                                for i in range(NT):
                                    t = PE.do([b.free, ready_z], pe.matmul, b.t[:, tile(i)], Z[r, tile(i)], Z[r, tile(i)],
                                              start=True, stop=True)
                            outs.append((hh, b, t))
                        st["z"] = [t]
                        if li < 9:
                            a = decays(levels[li])
                        for hh, b, t in outs:
                            if m in (128, 256):
                                o, n = (OD[:, hh, 0:4, :], 4) if m == 256 else (OD[:, hh, 4:6, :], 2)
                                last_v = VE.do([t, read], ve.tensor_copy, o, b.t[:, 0:128 * n].rearrange("p (i t) -> p i t", i=n))
                                give(b, last_v)
                            else:
                                last_v = into_DG(hh, b, t, 7 if m == 0 else li - 3)
                        if li < 9:
                            ready_z = decayed(levels[li], a)
                        fill()
                    gv = fills.get("gv")
                    bs, read = [take(), take()], []
                    for i in range(NT):
                        b = bs[i // 2]
                        for hh in range(2):
                            for s in range(i + 1):
                                if s == i:
                                    l = DG[:, hh, i, :]
                                elif (s, i) in ((0, 1), (2, 3)):
                                    l = OD[:, hh, 4 + s // 2, :]
                                else:
                                    l = OD[:, hh, 2 * s + i - 2, :]
                                t = PE.do([b.free, last_v, gv], pe.matmul, b.t[:, 256 * (i % 2) + 128 * hh:256 * (i % 2) + 128 * hh + 128], l,
                                          GV[s][:, 256 * dp + 128 * hh:256 * dp + 128 * hh + 128], start=s == 0, stop=s == i)
                        b.tok = t
                    read = [t]
                    fill()
                    logs()
                    v = None
                    for j, b in enumerate(bs):
                        a = AC.do([b.tok, on_free], act.activation, ON[:, 512 * j:512 * j + 512], b.t[:, :], ACT.Square) if dp else \
                            AC.do([b.tok], act.activation, ON[:, 512 * j:512 * j + 512], b.t[:, :], ACT.Square)
                        v = VE.do([a], ve.reduce_sum, ss[:, 4 * j:4 * j + 4],
                                  ON[:, 512 * j:512 * j + 512].rearrange("p (h v) -> p h v", h=4), AX.X)
                    r = rsqrt(ss[:, 8:16], ss[:, 0:8], 1.0 / 128, 1e-6, ss[:, 16:24], ss[:, 24:32], v)
                    vs = []
                    for j, b in enumerate(bs):
                        on = ON[:, 512 * j:512 * j + 512].rearrange("p (h v) -> p h v", h=4)
                        v = VE.do([r], ve.tensor_tensor, on, b.t[:, :].rearrange("p (h v) -> p h v", h=4),
                                  ss[:, 8 + 4 * j:12 + 4 * j].unsqueeze(2).broadcast_to([128, 4, 128]), mult)
                        give(b, v)
                        for i in (2 * j, 2 * j + 1):
                            o = ON[:, 256 * i:256 * i + 256]
                            vs.append(VE.do([v, gr_tok], ve.tensor_tensor, o, o, GR[i][:, 256 * dp:256 * dp + 256], mult))
                    fill()
                    for hh in range(2):
                        b = take()
                        t = transposes([(ON[:, 256 * i + 128 * hh:256 * i + 128 * hh + 128], 128 * i) for i in range(NT)], b, vs)
                        d = split(pair(OB, ALL, 2 * dp + hh, ALL), b.t[:, :], t)
                        give(b, d)
                        done.append(d)
                    on_free = t
                while fills.jobs:
                    fills.one()
                gb_free[0] = [PE.last(), VE.last(), AC.last()]
                return done

        def passed(norm, src):
            for i in range(NT):
                norm.compute(i, src[i])
                if i > 0:
                    norm.finish(i - 1)
            norm.finish(NT - 1)
            return norm.toks

        ready = None
        logs()
        if "mix" in stages:
            with ExitStack() as cm:
                ready = passed(RmsNorm(A["norm_mix"][0], cm), k_x)
            with ExitStack() as cm:
                ready = mix(ready, cm, lambda c: RmsNorm(A["norm_ffn"][0], c))
        if "ffn" in stages:
            if ready is None:
                with ExitStack() as cm:
                    ready = passed(RmsNorm(A["norm_ffn"][0], cm), k_x)
            with ExitStack() as cm:
                ready = ffn(ready, cm, RmsNorm(A["norm_final"], cm, to_x=True))
        for n, (name, f) in enumerate((("mla0", lambda *a: mla(0, *a)), ("swa", swa), ("fox", fox),
                                       ("mla1", lambda *a: mla(1, *a)))):
            if name not in stages:
                continue
            if ready is None:
                ready = [to_XT(X[:, i, :], i, [k_x[i]] * 2) for i in range(NT)]
            norm = LayerNorm(A["ln_g_2"][n], A["ln_b_2"][n], transposed=name != stages[-1])
            with ExitStack() as cm:
                ready = f(ready, cm, norm)
        settle()
        done = ready
        o_tok = []
        o_v = out.rearrange("o (i p) d -> p (o i) d", p=128)
        l_o = [lane(f"l_o{i}") for i in range(NT)]
        for i in range(NT):
            o_tok.append(SP.dma([done[i]], l_o[i], nc.sync.dma_start, o_v[:, i, :], X[:, i, :]))
        SP.wait(*o_tok)

        block = top.enter_context(nc.Block())

        @block.sync
        def _(e):
            SP.play(e)

        @block.scalar
        def _(e):
            AC.play(e)

        @block.vector
        def _(e):
            VE.play(e)

        @block.gpsimd
        def _(e):
            PO.play(e)

        @block.tensor
        def _(e):
            PE.play(e)


def constants():
    c = np.zeros((128, C_END), np.float32)
    p = np.arange(128)
    c[:, C_ID:C_ID + 128] = np.eye(128)
    c[:, C_MASK:C_MASK + 128] = np.where(p[None, :] > p[:, None], -1e30, 0.0)
    dist = p[:, None] + 128 - np.arange(256)[None, :]
    c[:, C_DIST:C_DIST + 256] = np.where((dist >= 0) & (dist < 128), dist, 3e35)
    t = (np.arange(4)[None, :] * 128 + p[:, None]).astype(np.float32)
    inv = (np.float32(500000.0) ** (-np.arange(8, dtype=np.float32) / np.float32(8))).astype(np.float32)
    ang = (t[:, :, None] * inv).astype(np.float32)
    c[:, C_NROPE:C_NROPE + 32] = np.cos(ang).reshape(128, 32)
    c[:, C_NROPE + 32:C_NROPE + 64] = np.sin(ang).reshape(128, 32)
    inv = (np.float32(10000.0) ** (-np.arange(0, 32, 2, dtype=np.float32) / np.float32(32))).astype(np.float32)
    ang = (t[:, :, None] * inv).astype(np.float32)
    c[:, C_MROPE:C_MROPE + 64] = np.cos(ang).reshape(128, 64)
    c[:, C_MROPE + 64:C_MROPE + 128] = np.sin(ang).reshape(128, 64)
    for h in range(16):
        c[[h, 32 + h, 64 + h], C_SEL + h] = 1.0
    s, q = p[:, None], p[None, :]
    for i, m in enumerate((64, 32, 16, 8, 4, 2, 1)):
        c[:, C_GLA + 128 * i:C_GLA + 128 * i + 128] = (s // (2 * m) == q // (2 * m)) & (s // m % 2 == 0) & (q // m % 2 == 1)
    c[:, C_GLA + 896:C_GLA + 1024] = np.eye(128)
    seen = (16 * np.arange(32)[None, None, :] + 31 <= t[:, :, None]).astype(np.float32)
    m = np.stack([seen, (seen - 1) * np.float32(1e30)], 1).reshape(128, 256)
    return c, m


_OUT = (1, T, D)
_INS = ["x", "norm_mix", "w_in", "cmp_pe_k", "cmp_pe_v", "cmp_k_w1", "cmp_k_w2", "cmp_v_w1", "cmp_v_w2", "gla_gate_w2",
        "gla_gate_b", "gla_norm", "w_up_nsa", "w_up_gla", "w_out", "norm_ffn", "w_ffn_gate", "w_ffn_up", "w_ffn_down",
        "norm_final", "ln_g_2", "ln_b_2", "mla_w_in_2", "mla_q_norm_2", "mla_w_q_up_2", "mla_kv_norm_2",
        "mla_w_kv_up_2", "mla_w_out_2", "swa_w_in_2", "swa_sinks_2", "swa_w_out_2", "fox_w_in_2", "fox_b_f_2",
        "fox_w_out_2"]


def kernel(**inputs):
    import concourse.bacc as bacc
    from concourse.bass_utils import run_bass_kernel_spmd

    nc = bacc.Bacc("TRN2", target_bir_lowering=False, num_devices=1)
    cst, cmask = constants()
    arrays = {n: np.ascontiguousarray(inputs[n]) for n in _INS}
    arrays["cst"], arrays["cmask"] = cst, cmask
    aps = {n: nc.dram_tensor(f"in_{n}", a.shape, mybir.dt.from_np(a.dtype), kind="ExternalInput").ap()
           for n, a in arrays.items()}
    out = nc.dram_tensor("out_x", _OUT, F, kind="ExternalOutput").ap()
    program(nc, aps, out)
    r = run_bass_kernel_spmd(nc, [{f"in_{n}": a for n, a in arrays.items()}], core_ids=[0])
    return r.results[0]["out_x"]
```

```python
import numpy as np
from concourse import mybir
from contextlib import ExitStack

F = mybir.dt.float32
R = mybir.dt.float32r
B16 = mybir.dt.bfloat16
I32 = mybir.dt.int32
ALU = mybir.AluOpType
ACT = mybir.ActivationFunctionType
AX = mybir.AxisListType

T = 512
D = 1024
NT = 4
RAW_SLOTS = 3
W_SLOTS = 5
LOOK = 3
PIECE = 1024
OFF = (0, 128, 384, 768)
ALPHA = 8.0 ** 0.25
C_ID, C_MASK, C_DIST, C_NROPE, C_MROPE, C_SEL, C_FOX, C_GLA, C_END = 0, 128, 256, 512, 576, 704, 720, 724, 1748


class Queue:

    def __init__(self, sem):
        self.sem, self.n, self.items = sem, 0, []

    def do(self, after, f, *a, **k):
        self.n += 1
        self.items.append((after, f, a, k, (self.sem, 1)))
        return (self.sem, self.n)

    def quiet(self, after, f, *a, **k):
        self.items.append((after, f, a, k, None))

    def wait(self, *after):
        self.items.append((list(after), None, (), {}, None))

    def dma(self, after, lane, f, *a):
        lane[1] += 16
        self.items.append((after, f, a, {}, (lane[0], 16)))
        return (lane[0], lane[1])

    def slot(self):
        own = []
        self.items.append(own)
        return own

    def last(self):
        return (self.sem, self.n)

    def play(self, eng):
        seen, flat = {}, []
        for it in self.items:
            flat += it if isinstance(it, list) else [it]
        for after, f, a, k, inc in flat:
            stack = [after]
            while stack:
                t = stack.pop(0)
                if t is None:
                    continue
                if isinstance(t, list):
                    stack = t + stack
                    continue
                sem, v = t
                if v > seen.get(sem.name, 0):
                    eng.wait_ge(sem, v)
                    seen[sem.name] = v
            if f is not None:
                ins = f(*a, **k)
                if inc is not None:
                    ins.then_inc(inc[0], inc[1])


class Bank:

    def __init__(self, t):
        self.t, self.free, self.tok = t, None, None


def program(nc, A, out):
    top = ExitStack()
    with top:
        names = {}

        def sem(name):
            return top.enter_context(nc.semaphore(name))

        def alloc(cm, name, shape, dt=F, side="left"):
            names[name] = names.get(name, 0) + 1
            return cm.enter_context(nc.sbuf_tensor(f"{name}_{names[name]}", shape, dt, side=side))

        PE, AC, VE, PO = (Queue(sem(n)) for n in ("s_pe", "s_act", "s_dve", "s_pool"))
        SP = Queue(None)
        pe, act, ve, po = nc.tensor, nc.scalar, nc.vector, nc.gpsimd
        mult, add, sub = ALU.mult, ALU.add, ALU.subtract

        X = alloc(top, "X", [128, NT, D])
        XT = (alloc(top, "XTh", [128, 8, T], R), alloc(top, "XTl", [128, 8, T], R))
        Wr = [alloc(top, "Wr", [128, PIECE]) for i in range(RAW_SLOTS)]
        Wh = [alloc(top, "Wh", [128, PIECE], R) for i in range(W_SLOTS)]
        Wl = [alloc(top, "Wl", [128, PIECE], R) for i in range(W_SLOTS)]
        CST = alloc(top, "CST", [128, C_GLA])
        IDB = alloc(top, "IDB", [128, 128], B16)
        MKB = alloc(top, "MKB", [128, 128], B16)
        GB = alloc(top, "GB", [128, 2, D])
        ST = alloc(top, "ST", [128, NT, 24])

        all_banks = [Bank(top.enter_context(nc.psum_tensor(f"PS{i}", [128, 512], F))) for i in range(8)]
        idle = list(all_banks)

        def take():
            return idle.pop(0)

        def give(b, *toks):
            b.free = list(toks)
            idle.append(b)

        IDN = CST[:, C_ID:C_ID + 128]

        def logs():
            AC.quiet([], act.preload_act_table_set, "natural_log_exp_and_others")

        def lane(name):
            return [sem(name), 0]

        def tile(i):
            return slice(128 * i, 128 * i + 128)

        x_in = A["x"].rearrange("o (i p) d -> p (o i) d", p=128)
        l_x = [lane(f"l_x{i}") for i in range(NT)]
        k_x = [AC.dma([], l_x[0], act.dma_start, X[:, 0, :], x_in[:, 0, :])]
        l_g = [lane("l_g0"), lane("l_g1")]
        gb_free = [None]

        def gains(*rs):
            return [AC.dma([gb_free[0]], l_g[j], act.dma_start, GB[:, j, :],
                           r.rearrange("(o n) -> o n", o=1).broadcast_to([128, D])) for j, r in enumerate(rs)]

        k_g = gains(A["norm_mix"][0])
        k_x += [AC.dma([], l_x[i], act.dma_start, X[:, i, :], x_in[:, i, :]) for i in range(1, NT)]
        k_cst = SP.dma([], lane("l_cst"), nc.sync.dma_start, CST[:, :], A["cst"][:, 0:C_GLA])
        VE.do([k_cst], ve.tensor_copy, IDB[:, :], IDN)
        k_idb = VE.do([k_cst], ve.tensor_copy, MKB[:, :], CST[:, C_MASK:C_MASK + 128])

        l_raw = [lane(f"l_raw{i}") for i in range(RAW_SLOTS)]
        s_hi, s_lo = sem("s_hi"), sem("s_lo")
        released, places, at, slots, where, ahead = {}, [], [], {}, {}, []

        class Piece:
            def __init__(self, i, n):
                self.ready, self.i, self.n = (s_lo, i + 1), i, n
                self.t = (Wh[i % W_SLOTS], Wl[i % W_SLOTS])

            def __call__(self, a, c0, c1, p0=0, p1=128):
                return [t[p0:p1, a * self.n + c0:a * self.n + c1] for t in self.t]

        def weight(srcs, n):
            i = len(places)
            places.append(AC.slot())
            at.append(len(AC.items))
            raw, lan = Wr[i % RAW_SLOTS], l_raw[i % RAW_SLOTS]
            a = srcs[0][0].shape[1]
            for src, c, p0 in srcs:
                pp, m = src.shape[0], src.shape[2]
                dst = raw[p0:p0 + pp, 0:a * n].rearrange("p (a n) -> p a n", n=n)[:, :, c:c + m]
                tok = SP.dma([(s_lo, i - RAW_SLOTS + 1)] if i >= RAW_SLOTS else [], lan, nc.sync.dma_start, dst, src)
            used = a * n
            free = [released[i - W_SLOTS]] if i >= W_SLOTS else []
            h, l = Wh[i % W_SLOTS], Wl[i % W_SLOTS]
            j = max(i - LOOK, 0)
            later = i >= W_SLOTS and where[i - W_SLOTS] > at[j]
            place = slots[i - W_SLOTS] if later else ahead[i] if i < len(ahead) else places[j]
            place.append(([tok] + free, act.copy, (h[:, 0:used], raw[:, 0:used]), {}, (s_hi, 1)))
            PO.items.append(([tok, (s_hi, i + 1)] + free, po.tensor_tensor,
                             (l[:, 0:used], raw[:, 0:used], h[:, 0:used].bitcast(F), sub), {}, (s_lo, 1)))
            return Piece(i, n)

        def release(w, tok):
            released[w.i] = tok
            slots[w.i] = AC.slot()
            where[w.i] = len(AC.items)

        def mm3(o, l, r, start, stop, after, sig=False):
            PE.quiet(after, pe.matmul, o, l[0], r[1], start=start, stop=False)
            PE.quiet([], pe.matmul, o, l[1], r[0], start=False, stop=False)
            f = PE.do if stop or sig else PE.quiet
            return f([], pe.matmul, o, l[0], r[0], start=False, stop=stop)

        def pair(p, *ix):
            return [t[ix] for t in p]

        def by_rows(w):
            return w.rearrange("(a p) n -> p a n", p=128)

        ALL = slice(None)

        def feature_tile(src):
            srcs = src if isinstance(src, list) else [(src, 0, 0)]
            return weight(srcs, max(c + x.shape[2] for x, c, _ in srcs)), srcs[0][0].shape[1]

        def proj_T(src, rhs, rdy):
            w, kts = feature_tile(src)
            b = take()
            for a in range(kts):
                tok = mm3(b.t[0:w.n, :], w(a, 0, w.n), pair(rhs, ALL, a, ALL), a == 0, a == kts - 1,
                          [w.ready, b.free, rdy])
            b.tok = tok
            release(w, tok)
            return b

        pending = []

        def settle():
            while pending:
                pending.pop(0)()
            f = [PE.last(), AC.last(), VE.last()]
            for q in (AC, VE):
                q.wait(*f)

        def first_T(srcs, rhs, rdy):
            ws, bs = [feature_tile(s) for s in srcs], [take() for _ in srcs]
            for i0, i1 in ((0, 2), (2, 4)):
                if i0 == 2:
                    settle()
                c = slice(128 * i0, 128 * i1)
                for (w, kts), b in zip(ws, bs):
                    for a in range(kts):
                        b.tok = mm3(b.t[0:w.n, c], w(a, 0, w.n), pair(rhs, ALL, a, c), a == 0, a == kts - 1,
                                    [w.ready, b.free, rdy[i0:i1]])
                    if i1 == NT:
                        release(w, b.tok)
            return bs

        def first_N(pieces, n, lhs, rdy):
            bs = [take() for _ in range(NT)]
            ws, a0 = [], 0
            for src, k in pieces:
                ws.append((weight([(src, 0, 0)], src.shape[2]), a0, k))
                a0 += k
            for i0 in (0, 2):
                if i0 == 2:
                    settle()
                for w, a1, k in ws:
                    for i in (i0, i0 + 1):
                        for a in range(k):
                            tok = mm3(bs[i].t[:, 0:n], pair(lhs, ALL, a1 + a, tile(i)), w(a, 0, n), a1 + a == 0,
                                      a1 + a == a0 - 1, [w.ready, bs[i].free, rdy[i]], sig=i == NT - 1 and a == k - 1)
                        if tok:
                            bs[i].tok = tok
                    if i0 == 2:
                        release(w, tok)
            return bs

        def proj_N(pieces, n, lhs, rdy):
            bs = [take() for _ in range(NT)]
            kts, a0 = sum(k for _, k in pieces), 0
            for src, k in pieces:
                w = weight([(src, 0, 0)], src.shape[2])
                for i in range(NT):
                    for a in range(k):
                        tok = mm3(bs[i].t[:, 0:n], pair(lhs, ALL, a0 + a, tile(i)), w(a, 0, n), a0 + a == 0,
                                  a0 + a == kts - 1, [w.ready, bs[i].free, rdy[i]], sig=i == NT - 1 and a == k - 1)
                        if tok:
                            bs[i].tok = tok
                release(w, tok)
                a0 += k
            return bs

        def cut(src, n):
            k, per = src.shape[1], max(1, PIECE // n)
            return [(src[:, j:min(j + per, k), :], min(per, k - j)) for j in range(0, k, per)]

        def outproj(src, lhs, rdy, alpha, norm=None):
            bs = [[take(), take()] for _ in range(NT)]
            kts = src.shape[1]
            tail = 4 if norm else 1
            done = []

            def product(w, a, i, cs=(0, 1)):
                for c in cs:
                    b = bs[i][c]
                    tok = mm3(b.t[:, :], pair(lhs, ALL, a, tile(i)), w(0, 512 * c, 512 * c + 512), a == 0, a == kts - 1,
                              [w.ready, b.free, rdy[min(a, len(rdy) - 1)]], sig=i == NT - 1 and c == 1)
                    if tok:
                        b.tok = tok
                        if i == NT - 1 and c == 1:
                            release(w, tok)

            for a in range(kts - tail):
                w = weight([(src[:, a:a + 1, :], 0, 0)], D)
                for i in range(NT):
                    product(w, a, i)
            ws = [(weight([(src[:, a:a + 1, :], 0, 0)], D), a) for a in range(kts - tail, kts)]
            for i in range(NT):
                for c in range(2):
                    for w, a in ws:
                        product(w, a, i, (c,))
                    b, xs = bs[i][c], X[:, i, 512 * c:512 * c + 512]
                    t = VE.do([b.tok, k_x[i]], ve.scalar_tensor_tensor, xs, xs, alpha, b.t[:, :], mult, add)
                    give(b, t)
                    if norm:
                        norm.part(i, c, t)
                done.append(t)
                if norm:
                    norm.compute(i)
                    if i > 0:
                        norm.finish(i - 1)
            if norm:
                pending.append(lambda: norm.finish(NT - 1))
            return norm.toks if norm else done

        def split(pr, src, *after):
            a = AC.do(list(after), act.copy, pr[0], src)
            return VE.do([a, list(after)], ve.tensor_tensor, pr[1], src, pr[0].bitcast(F), sub)

        def rsqrt(dst, src, scale, eps, v, q, *after):
            a = VE.do(list(after), ve.tensor_scalar, v, src, scale, eps, mult, add)
            a = AC.do([a], act.activation, q, v, ACT.Ln)
            a = AC.do([a], act.activation, dst, q, ACT.Exp, scale=-0.5)
            a = VE.do([a], ve.tensor_tensor, q, dst, dst, mult)
            a = VE.do([a], ve.tensor_tensor, q, q, v, mult)
            a = VE.do([a], ve.tensor_scalar, q, q, -0.5, 1.5, mult, add)
            return VE.do([a], ve.tensor_tensor, dst, dst, q, mult)

        def transposes(blocks, b, after):
            after = [after, b.free, k_cst]
            for s, c in blocks:
                p, m = s.shape[0], int(np.prod(s.shape[1:]))
                f = PE.do if c == blocks[-1][1] else PE.quiet
                tok = f(after, pe.transpose, b.t[0:m, c:c + p], s, IDN[0:p, 0:p])
            return tok

        def to_XT(src, i, after):
            toks = []
            for c in range(2):
                b = take()
                t = transposes([(src[:, tile(4 * c + j)], 128 * j) for j in range(4)], b, [after[c]])
                ps = b.t[:, :].rearrange("p (j t) -> p j t", j=4)
                v = split(pair(XT, ALL, slice(4 * c, 4 * c + 4), tile(i)), ps, t)
                give(b, v)
                toks.append(v)
            return toks

        class RmsNorm:

            def __init__(self, row, cm, to_x=False, gt=None):
                self.gt, self.H, self.to_x = gt or gains(row), alloc(cm, "H", [128, 2, D]), to_x
                self.toks, self.used, self.v = [], [None, None], [None] * NT

            def part(self, i, c, ready):
                cs, st = slice(512 * c, 512 * c + 512), ST[:, i, :]
                self.a = AC.do([ready, self.used[i % 2]], act.activation, self.H[:, i % 2, cs], X[:, i, cs], ACT.Square,
                               accum_out=st[:, 4 + c:5 + c])

            def compute(self, i):
                st, h = ST[:, i, :], self.H[:, i % 2, :]
                a = VE.do([self.a], ve.tensor_tensor, st[:, 0:1], st[:, 4:5], st[:, 5:6], add)
                r = rsqrt(st[:, 1:2], st[:, 0:1], 1.0 / D, 1e-6, st[:, 2:3], st[:, 3:4], a)
                o = X[:, i, :] if self.to_x else h
                self.o = [(X[:, j, :] if self.to_x else self.H[:, j % 2, :]) for j in range(NT)]
                self.v[i] = [VE.do([r, a, self.gt], ve.scalar_tensor_tensor, o[:, c], X[:, i, c], st[:, 1:2],
                                   GB[:, 0, c], mult, mult) for c in (slice(0, 512), slice(512, D))]
                gb_free[0] = VE.last()

            def finish(self, i):
                self.toks.append(to_XT(self.o[i], i, self.v[i]))
                self.used[i % 2] = PE.last()

        class LayerNorm:

            def __init__(self, g, b, transposed=True):
                self.gt, self.transposed, self.toks, self.v = gains(g, b), transposed, [], [None] * NT

            def part(self, i, c, ready):
                self.b = VE.do([ready], ve.bn_stats, ST[:, i, 6 * c:6 * c + 6], X[:, i, 512 * c:512 * c + 512])

            def compute(self, i):
                st, x = ST[:, i, :], X[:, i, :]
                cs = (slice(0, 512), slice(512, D))
                v = VE.do([self.b], ve.bn_aggr, st[:, 12:14], st[:, 0:12])
                w = [VE.do([v, self.gt], ve.scalar_tensor_tensor, x[:, c], x[:, c], st[:, 12:13], GB[:, 0, c], sub, mult)
                     for c in cs]
                r = rsqrt(st[:, 14:15], st[:, 13:14], 1.0, 1e-5, st[:, 15:16], st[:, 16:17], v)
                self.v[i] = [VE.do([w[n], r], ve.scalar_tensor_tensor, x[:, c], x[:, c], st[:, 14:15], GB[:, 1, c],
                                   mult, add) for n, c in enumerate(cs)]
                gb_free[0] = VE.last()

            def finish(self, i):
                self.toks.append(to_XT(X[:, i, :], i, self.v[i]) if self.transposed else self.v[i])

        def rope(x1, x2, o1, o2, cos, sin, t1, t2, *after):
            VE.do([list(after), k_cst], ve.tensor_tensor, t1, x2, sin, mult)
            a = VE.do([], ve.tensor_tensor, t2, x1, sin, mult)
            VE.do([a], ve.tensor_tensor, o1, x1, cos, mult)
            a = VE.do([a], ve.tensor_tensor, o2, x2, cos, mult)
            VE.do([a], ve.tensor_tensor, o1, o1, t1, sub)
            return VE.do([a], ve.tensor_tensor, o2, o2, t2, add)

        class Attention:
            def __init__(self, cm):
                self.P = [alloc(cm, "P", [128, 1280]) for i in range(2)]
                self.PT = [alloc(cm, "PT", [128, 1280]) for i in range(2)]
                self.sm = [alloc(cm, "sm", [128, 20]) for i in range(2)]
                self.p_free, self.t_free, self.n, self.m, self.flip = [None, None], [None, None], 0, 0, 0

            def scores(self, q, k, rdy, extra=(), gate=None):
                s = self.n % 2
                self.n += 1
                P, sm = self.P[s], self.sm[s]
                toks = []
                for i in range(NT):
                    n = (i + 1) * 128
                    b = take()
                    PE.quiet([b.free, rdy], pe.matmul, b.t[:, 0:n], q(i), k(n), start=True, stop=False)
                    for l, r in extra:
                        PE.quiet([], pe.matmul, b.t[:, 0:n], l(i), r(n), start=False, stop=False)
                    t = PE.do([k_idb], pe.matmul, b.t[:, n - 128:n], IDB[:, :], MKB[:, :], start=False, stop=True)
                    v = VE.do([t, self.p_free[s]], ve.reduce_max, sm[:, i:i + 1], b.t[:, 0:n], AX.X, negate=True)
                    a = AC.do([v, self.p_free[s]], act.activation, P[:, OFF[i]:OFF[i] + n], b.t[:, 0:n], ACT.Exp,
                              bias=sm[:, i:i + 1], accum_out=sm[:, 4 + i:5 + i])
                    give(b, a)
                    toks.append(a)
                return s, toks, gate

            def normalise(self, sc):
                s, toks, gate = sc
                P, sm = self.P[s], self.sm[s]
                v = VE.do([toks], ve.reciprocal, sm[:, 8:12], sm[:, 4:8])
                if gate is not None:
                    v = VE.do([v], ve.tensor_tensor, sm[:, 8:12], sm[:, 8:12], gate, mult)
                for i in range(NT):
                    n = (i + 1) * 128
                    p = P[:, OFF[i]:OFF[i] + n]
                    v2 = VE.do([v], ve.tensor_scalar, p, p, sm[:, 8 + i:9 + i], None, mult)
                return s, v2

            def evacuate(self, dst, src, after):
                self.flip ^= 1
                if self.flip:
                    return AC.do(after, act.copy, dst, src)
                return VE.do(after, ve.tensor_copy, dst, src)

            def turn(self, ps):
                s, done = ps
                m = self.m % 2
                self.m += 1
                P, PT = self.P[s], self.PT[m]
                evs = []
                for js, base in (((0,), 0), ((1, 3), 512), ((2,), 1024)):
                    b = take()
                    cols = [(i, j) for j in js for i in range(j, NT)]
                    n = 128 * len(cols)
                    t = transposes([(P[:, OFF[i] + 128 * j:OFF[i] + 128 * j + 128], 128 * c)
                                    for c, (i, j) in enumerate(cols)], b, done)
                    e = self.evacuate(PT[:, base:base + n], b.t[:, 0:n], [t, self.t_free[m]])
                    give(b, e)
                    evs.append(e)
                self.p_free[s] = PE.last()
                return m, evs

            def values(self, turned, v, o, rdy, start=True, stop=True):
                m, evs = turned
                PT = self.PT[m]
                src = (0, 512, 1024, 896)
                for j in range(NT):
                    f = PE.quiet if j < NT - 1 else PE.do
                    tok = f([evs, rdy], pe.matmul, o[:, 128 * j:512], v(j), PT[:, src[j]:src[j] + 512 - 128 * j],
                            start=start and j == 0, stop=stop and j == NT - 1)
                self.t_free[m] = tok
                return tok

        def heads(n, normalise, turn, score, value, fills, last):
            first, new = score(0), score(1)
            ps = normalise(first)
            if fills.jobs:
                fills.one()
            for h in range(n):
                turned = turn(ps)
                if h + 1 < n:
                    ps = normalise(new)
                if h + 2 < n:
                    new = score(h + 2)
                value(h, turned)
                fills.share(h, n - last)

        class Fills:

            def __init__(self, *jobs):
                self.jobs, self.all, self.done = list(jobs), len(jobs), {}

            def one(self):
                name, f = self.jobs.pop(0)
                self.done[name] = f()

            def start(self, n):
                for _ in range(n):
                    self.one()
                self.all = len(self.jobs)

            def get(self, name):
                while name not in self.done:
                    self.one()
                return self.done[name]

            def share(self, h, n):
                while self.jobs and (self.all - len(self.jobs)) * n < self.all * (h + 1):
                    self.one()

        class Gates:

            def __init__(self, src, rdy, GT):
                self.src, self.rdy, self.GT, self.toks, self.wait, self.out = src, rdy, GT, [None] * 8, [], [None] * 8

            def job(self, f):
                def run():
                    b = proj_T(self.src[:, :, tile(f)], XT, self.rdy)
                    a = AC.do([b.tok], act.activation, self.GT[:, f, :], b.t[:, :], ACT.Tanh, scale=0.5)
                    v = VE.do([a], ve.scalar_tensor_tensor, self.GT[:, f, :], self.GT[:, f, :], 1.0, b.t[:, :], add, mult)
                    give(b, v)
                    self.toks[f] = v
                    self.last_read = b.tok
                    return v
                return (f"g{f}", run)

            def output(self, f, ob, tok, fills):
                fills.get(f"g{f}")
                G = self.GT[:, f, :]
                v = VE.do([tok, self.toks[f]], ve.scalar_tensor_tensor, G, G, 0.5, ob.t[:, :], mult, mult)
                give(ob, v)
                self.wait.append((f, v))
                for _ in range(8 if f == 7 else 1):
                    if self.wait and not fills.jobs:
                        f, v = self.wait.pop(0)
                        self.out[f] = split(pair(XT, ALL, f, ALL), self.GT[:, f, :], v, self.last_read)

        def half(h):
            return slice(64 * (h % 2), 64 * (h % 2) + 64)

        def ffn(ready, cm, norm):
            wg, wu, wd = by_rows(A["w_ffn_gate"][0]), by_rows(A["w_ffn_up"][0]), by_rows(A["w_ffn_down"][0])
            HT = [(alloc(cm, "HTh", [128, 8, T], R), alloc(cm, "HTl", [128, 8, T], R)) for _ in range(2)]
            sg = [alloc(cm, "sg", [128, T]) for _ in range(2)]
            hf = [alloc(cm, "hf", [128, T]) for _ in range(2)]
            f0, n, used = 0, 0, [None, None]
            free = [None, None]
            early = first_T([m[:, :, tile(f)] for f in range(2) for m in (wg, wu)], XT, ready)
            for g, cnt in enumerate((8, 7, 7)):
                H, toks = HT[g % 2], []
                for f in range(cnt):
                    c = slice(128 * (f0 + f), 128 * (f0 + f) + 128)
                    bg = early.pop(0) if early else proj_T(wg[:, :, c], XT, ready)
                    bu = early.pop(0) if early else proj_T(wu[:, :, c], XT, ready)
                    s = n % 2
                    n += 1
                    a = AC.do([bg.tok, used[s]], act.activation, sg[s][:, :], bg.t[:, :], ACT.Silu)
                    give(bg, a)
                    v = VE.do([a, bu.tok, used[s]], ve.tensor_tensor, hf[s][:, :], sg[s][:, :], bu.t[:, :], mult)
                    give(bu, v)
                    toks.append(split(pair(H, ALL, f, ALL), hf[s][:, :], v, free[g % 2]))
                    used[s] = toks[-1]
                done = outproj(wd[:, f0:f0 + cnt, :], H, toks, 1.0, norm if g == 2 else None)
                free[g % 2] = PE.last()
                f0 += cnt
            return done

        def mla(li, ready, cm, norm):
            w_in = by_rows(A["mla_w_in_2"][li])
            CQ = [alloc(cm, "CQ", [128, 3, T], R) for h in "hl"]
            CK = [alloc(cm, "CK", [128, 2, T], R) for h in "hl"]
            GT = alloc(cm, "GT", [128, 8, T])
            QT = [alloc(cm, "QT", [96, T]) for i in range(3)]
            KT = [alloc(cm, "KT", [96, T]) for i in range(3)]
            QRT = alloc(cm, "QRT", [128, NT, T])
            V = alloc(cm, "V", [128, NT, D])
            cos = lambda i: CST[:, C_MROPE + 16 * i:C_MROPE + 16 * i + 16]
            sin = lambda i: CST[:, C_MROPE + 64 + 16 * i:C_MROPE + 64 + 16 * i + 16]
            scale = 96.0 ** -0.5
            gates = Gates(w_in[:, :, 672:1696], ready, GT)
            fills = Fills(*[gates.job(f) for f in range(3)], ("v0", lambda: vals(0)), gates.job(3), ("v1", lambda: vals(1)),
                          *[gates.job(f) for f in range(4, 8)])
            with ExitStack() as c1:
                QN, KN = alloc(c1, "QN", [128, 384]), alloc(c1, "KN", [128, 256])
                CN = alloc(c1, "CN", [128, NT, 704])
                scr = alloc(c1, "scr", [128, 384])
                tm, sq = alloc(c1, "tm", [128, 2, 64]), alloc(c1, "sq", [128, 32])
                ln = lane(f"l_n{li}"), lane(f"l_m{li}")
                bs = first_N(cut(w_in[:, :, 0:336], 336), 336, XT, ready)
                k_n = [AC.dma([], ln[0], act.dma_start, QN[:, :], A["mla_q_norm_2"][li:li + 1, :].broadcast_to([128, 384])),
                       AC.dma([], ln[1], act.dma_start, KN[:, :], A["mla_kv_norm_2"][li:li + 1, :].broadcast_to([128, 256]))]
                got = [[] for _ in range(NT)]
                for c0, n in ((0, 336), (336, 336)):
                    if c0:
                        bs = proj_N(cut(w_in[:, :, c0:c0 + n], n), n, XT, ready)
                    for i, b in enumerate(bs):
                        got[i].append(VE.do([b.tok], ve.tensor_copy, CN[:, i, c0:c0 + n], b.t[:, 0:n]))
                        give(b, got[i][-1])
                for i in range(NT):
                    for c0, n, j in ((0, 384, 0), (384, 256, 4)):
                        a = AC.do([got[i], AC.last()], act.activation, scr[:, 0:n], CN[:, i, c0:c0 + n], ACT.Square,
                                  accum_out=sq[:, j + i:j + i + 1])
                v = [VE.do([a], ve.tensor_scalar, sq[:, j:j + 4], sq[:, j:j + 4], 1.0 / n, None, mult) for j, n in ((0, 384), (4, 256))]
                r = rsqrt(sq[:, 8:16], sq[:, 0:8], 1.0, 1e-6, sq[:, 16:24], sq[:, 24:32], v)
                tr = [[VE.do([r, k_n], ve.scalar_tensor_tensor, CN[:, i, c0:c0 + n], CN[:, i, c0:c0 + n],
                             sq[:, j + i:j + i + 1], g[:, :], mult, mult) for c0, n, j, g in ((0, 384, 8, QN), (384, 256, 12, KN))]
                      for i in range(NT)]
                t2 = [tm[:, u, :].rearrange("p (i c) -> p i c", i=NT) for u in range(2)]
                kr = rope(CN[:, :, 640:656], CN[:, :, 656:672], CN[:, :, 672:688], CN[:, :, 688:704],
                          *[CST[:, C_MROPE + 64 * u:C_MROPE + 64 * u + 64].rearrange("p (i c) -> p i c", c=16) for u in range(2)],
                          t2[0], t2[1], got)
                tr[NT - 1].append(kr)
                fills.start(3)
                tok_c = []
                for i in range(NT):
                    b = take()
                    t = transposes([(CN[:, i, tile(j)], 128 * j) for j in range(4)], b, tr[i])
                    ps = b.t[:, :].rearrange("p (j t) -> p j t", j=4)
                    u = split(pair(CQ, ALL, ALL, tile(i)), ps[:, 0:3, :], t)
                    w = split(pair(CK, ALL, 0, tile(i)), ps[:, 3, :], t, u)
                    give(b, u, w)
                    b = take()
                    t = transposes([(CN[:, i, 512:640], 0), (CN[:, i, 672:704], 128)], b, [tr[i], kr])
                    w2 = split(pair(CK, ALL, 1, tile(i)), b.t[:, 0:128], t)
                    e = [VE.do([t, w2], ve.tensor_copy, KT[n][64:96, tile(i)], b.t[0:32, 128:256]) for n in range(3)]
                    give(b, e)
                    tok_c.append([u, w, w2, e])
            w_q = A["mla_w_q_up_2"][li].rearrange("(a p) (h c) -> p a h c", p=128, c=96)
            w_kv = A["mla_w_kv_up_2"][li].rearrange("(a p) (h c) -> p a h c", p=128, c=128)

            def vals(c):
                toks = []
                bs = proj_N([(w_kv[:, a, 8 * c:8 * c + 8, 64:128], 1) for a in range(2)], 512, CK, tok_c)
                for i, b in enumerate(bs):
                    toks.append(VE.do([b.tok], ve.tensor_copy, V[:, i, 512 * c:512 * c + 512], b.t[:, :]))
                    give(b, toks[-1])
                return toks

            with ExitStack() as c2:
                QRn = alloc(c2, "QRn", [128, NT, T])
                RT = alloc(c2, "RT", [128, 2, 16, 16])
                bs = proj_N([(w_q[:, a, :, 64:96], 1) for a in range(3)], 512, CQ, tok_c)
                qn = []
                for i, b in enumerate(bs):
                    v = AC.do([b.tok], act.mul, QRn[:, i, :], b.t[:, :], scale)
                    give(b, v)
                    q4 = QRn[:, i, :].rearrange("p (h c) -> p h c", c=32)
                    x1, x2 = q4[:, :, 0:16], q4[:, :, 16:32]
                    cs = [x.unsqueeze(1).broadcast_to([128, 16, 16]) for x in (cos(i), sin(i))]
                    qn.append(rope(x1, x2, x1, x2, cs[0], cs[1], RT[:, 0], RT[:, 1], v, VE.last()))
                fills.start(2)
                qrt = []
                for c in range(4):
                    b = take()
                    t = transposes([(QRn[:, i, tile(c)], 128 * i) for i in range(NT)], b, qn)
                    a = AC.do([t], act.copy, QRT[:, c, :], b.t[:, :])
                    give(b, a)
                    qrt.append(a)
            att = Attention(cm)
            free, prep, ob = [None] * 3, {}, [None]

            def prepare(p):
                hs = (2 * p, 2 * p + 1)
                bq = proj_T([(w_q[:, :, h, 0:64], 64 * j, 0) for j, h in enumerate(hs)], CQ, tok_c)
                bk = proj_T([(w_kv[:, :, h, 0:64], 64 * j, 0) for j, h in enumerate(hs)], CK, tok_c)
                for j, h in enumerate(hs):
                    s, r = h % 3, slice(64 * j, 64 * j + 64)
                    prep[h] = [AC.do([bq.tok, free[s]], act.mul, QT[s][0:64, :], bq.t[r, :], scale),
                               VE.do([bk.tok, free[s]], ve.tensor_copy, KT[s][0:64, :], bk.t[r, :]),
                               VE.do([qrt, free[s]], ve.tensor_copy, QT[s][64:96, :], QRT[32 * (h % 4):32 * (h % 4) + 32, h // 4, :])]
                give(bq, prep[hs[0]][0], prep[hs[1]][0])
                give(bk, prep[hs[0]][1], prep[hs[1]][1])

            def score(h):
                if h == 0:
                    prepare(0)
                s = h % 3
                sc = att.scores(lambda i: QT[s][:, tile(i)], lambda n: KT[s][:, 0:n], [prep[h], tok_c])
                free[s] = PE.last()
                if h == 1:
                    prepare(1)
                return sc

            def value(h, turned):
                if h % 2 and h < 13:
                    prepare((h + 3) // 2)
                if h % 2 == 0:
                    ob[0] = take()
                vt = fills.get(f"v{h // 8}")
                tk = att.values(turned, lambda j: V[:, j, 64 * h:64 * h + 64], ob[0].t[half(h), :], [vt, ob[0].free])
                if h % 2:
                    gates.output(h // 2, ob[0], tk, fills)

            heads(16, att.normalise, att.turn, score, value, fills, 5)
            logs()
            return outproj(by_rows(A["mla_w_out_2"][li]), XT, gates.out, ALPHA, norm)

        def swa(ready, cm, norm):
            w = by_rows(A["swa_w_in_2"][0])
            QT, KT = alloc(cm, "QT", [128, 8, T]), alloc(cm, "KT", [128, 2, T])
            V, GT = alloc(cm, "V", [128, NT, 256]), alloc(cm, "GT", [128, 8, T])
            SB = [alloc(cm, "SB", [128, 2, T]) for _ in range(2)]
            P = [alloc(cm, "P", [128, 2, T]) for _ in range(2)]
            PT = [alloc(cm, "PT", [128, 7, 128]) for _ in range(2)]
            sm = [alloc(cm, "sm", [128, 20]) for _ in range(2)]
            SK = alloc(cm, "SK", [128, 16])
            def q_cols(c, a):
                return [(w[:, :, 64 * (8 * c + a):64 * (8 * c + a) + 64], 0, 0),
                        (w[:, :, 64 * (8 * c + 4 + a):64 * (8 * c + 4 + a) + 64], 64, 0)]

            early = dict(zip(("k0", "q00", "q01", "q02"),
                             first_T([w[:, :, 1024:1152]] + [q_cols(0, a) for a in range(3)], XT, ready)))
            k_s = AC.dma([], lane("l_sk"), act.dma_start, SK[:, :], A["swa_sinks_2"].broadcast_to([128, 16]))
            inits = [VE.do([], ve.memset, SB[s][:, 0, 0:128], -1e30) for s in range(2)]
            def queries(c, a):
                def run():
                    b = early.pop(f"q{c}{a}", None) or proj_T(q_cols(c, a), XT, ready)
                    e = AC.do([b.tok], act.mul, QT[:, 4 * c + a, :], b.t[:, :], 0.125)
                    give(b, e)
                    return e
                return (f"q{c}{a}", run)

            def keys(c):
                def run():
                    b = early.pop(f"k{c}", None) or proj_T(w[:, :, 1024 + 128 * c:1152 + 128 * c], XT, ready)
                    e = VE.do([b.tok], ve.tensor_copy, KT[:, c, :], b.t[:, :])
                    give(b, e)
                    return e
                return (f"k{c}", run)

            def vals():
                toks = []
                bs = proj_N(cut(w[:, :, 1280:1536], 256), 256, XT, ready)
                for i, b in enumerate(bs):
                    toks.append(VE.do([b.tok], ve.tensor_copy, V[:, i, :], b.t[:, 0:256]))
                    give(b, toks[-1])
                return toks

            gates = Gates(w[:, :, 1536:2560], ready, GT)
            fills = Fills(keys(0), queries(0, 0), queries(0, 1), queries(0, 2), ("v", vals), queries(0, 3), gates.job(0),
                          gates.job(1), keys(1), queries(1, 0), gates.job(2), queries(1, 1), gates.job(3), queries(1, 2),
                          gates.job(4), queries(1, 3), gates.job(5), gates.job(6), gates.job(7))
            fills.start(4)
            DIST = CST[:, C_DIST:C_DIST + 256].unsqueeze(1)
            p_free, t_free = [None, None], [None, None]

            def scores(h):
                s, g = h % 2, h // 4
                c, r = g // 2, half(g)
                q_tok = [fills.get(f"k{c}"), fills.get(f"q{c}{h % 4}")]
                S, p, m = SB[s], P[s], sm[s]
                slope = 2.0 ** (-0.5 * (h + 1))
                for u in range(2):
                    b = take()
                    for i in (2 * u, 2 * u + 1):
                        lo = max(0, i - 1)
                        o = b.t[:, (256 * (i % 2) + 128 if i == 0 else 256 * (i % 2)):256 * (i % 2) + 256]
                        t = PE.do([b.free, q_tok], pe.matmul, o, QT[r, 4 * c + h % 4, tile(i)],
                                  KT[r, c, 128 * lo:128 * i + 128], start=True, stop=True)
                    if u == 0:
                        v = VE.do([t, p_free[s]], ve.scalar_tensor_tensor, S[:, 0, 128:256], CST[:, C_DIST + 128:C_DIST + 256],
                                  -slope, b.t[:, 128:256], mult, add)
                        v = VE.do([t], ve.scalar_tensor_tensor, S[:, 0, 256:512], CST[:, C_DIST:C_DIST + 256],
                                  -slope, b.t[:, 256:512], mult, add)
                    else:
                        v = VE.do([t], ve.scalar_tensor_tensor, S[:, 1, :].rearrange("p (i k) -> p i k", i=2),
                                  DIST.broadcast_to([128, 2, 256]), -slope,
                                  b.t[:, :].rearrange("p (i k) -> p i k", i=2), mult, add)
                    give(b, v)
                    v = VE.do([v, inits], ve.reduce_max, m[:, 2 * u:2 * u + 2], S[:, u, :].rearrange("p (i k) -> p i k", i=2), AX.X)
                v = VE.do([v, k_s], ve.tensor_scalar, m[:, 0:4], m[:, 0:4], SK[:, h:h + 1], -1.0, ALU.max, mult)
                for i in range(NT):
                    a = AC.do([v, p_free[s]], act.activation, p[:, i // 2, 256 * (i % 2):256 * (i % 2) + 256],
                              S[:, i // 2, 256 * (i % 2):256 * (i % 2) + 256], ACT.Exp, bias=m[:, i:i + 1],
                              accum_out=m[:, 4 + i:5 + i])
                return s, AC.do([v], act.activation, m[:, 8:12], m[:, 0:4], ACT.Exp, bias=SK[:, h:h + 1])

            def normalise(sc):
                s, a = sc
                p, m = P[s], sm[s]
                v = VE.do([a], ve.tensor_tensor, m[:, 4:8], m[:, 4:8], m[:, 8:12], add)
                v = VE.do([v], ve.reciprocal, m[:, 12:16], m[:, 4:8])
                for i in range(NT):
                    x = p[:, i // 2, 256 * (i % 2):256 * (i % 2) + 256]
                    v2 = VE.do([v], ve.tensor_scalar, x, x, m[:, 12 + i:13 + i], None, mult)
                return s, v2

            def turn(sc):
                s, done = sc
                p, pt = P[s], PT[s]
                evs = []
                for part in (blocks[0:4], blocks[4:7]):
                    b = take()
                    n0 = 0 if part[0] == blocks[0] else 4
                    t = transposes([(p[:, i // 2, 256 * (i % 2) + (128 if i == j else 0):256 * (i % 2) + (256 if i == j else 128)],
                                     128 * x) for x, (j, i) in enumerate(part)], b, done)
                    dst, src = pt[:, n0:n0 + len(part), :].rearrange("p a b -> p (a b)"), b.t[:, 0:128 * len(part)]
                    e = (VE.do([t, t_free[s]], ve.tensor_copy, dst, src) if n0 else AC.do([t, t_free[s]], act.copy, dst, src))
                    give(b, e)
                    evs.append(e)
                p_free[s] = PE.last()
                return s, evs

            blocks = [(j, i) for j in range(NT) for i in (j, j + 1) if i < NT]

            def values(h, turned, o, rdy):
                s, evs = turned
                pt = PT[s]
                for i in range(NT):
                    js = [j for j in (i - 1, i) if j >= 0]
                    for j in js:
                        f = PE.do if (i, j) == (NT - 1, NT - 1) else PE.quiet
                        tok = f([evs, rdy], pe.matmul, o[:, tile(i)], V[:, j, 64 * (h // 4):64 * (h // 4) + 64],
                                pt[:, blocks.index((j, i)), :], start=j == js[0], stop=j == i)
                t_free[s] = tok
                return tok

            ob = [None]

            def value(h, turned):
                if h % 2 == 0:
                    ob[0] = take()
                tk = values(h, turned, ob[0].t[half(h), :], [ob[0].free, fills.get("v")])
                if h % 2:
                    gates.output(h // 2, ob[0], tk, fills)

            heads(16, normalise, turn, scores, value, fills, 4)
            logs()
            return outproj(by_rows(A["swa_w_out_2"][0]), XT, gates.out, ALPHA, norm)

        def log_sigmoid(dst, z, t, scale, after):
            a = AC.do(after, act.activation, t, z, ACT.Abs)
            a = AC.do([a], act.activation, t, t, ACT.Exp, scale=-1.0)
            a = AC.do([a], act.activation, t, t, ACT.Ln, bias=1.0)
            v = VE.do([after, a], ve.tensor_scalar, z, z, 0.0, scale, ALU.min, mult)
            return VE.do([v, a], ve.scalar_tensor_tensor, dst, t, -scale, z, mult, add)

        def fox(ready, cm, norm):
            w = by_rows(A["fox_w_in_2"][0])
            QT, KT = alloc(cm, "QT", [128, 8, T]), alloc(cm, "KT", [128, 8, T])
            V, GT = alloc(cm, "V", [128, NT, D]), alloc(cm, "GT", [128, 8, T])
            CB = [alloc(cm, "CB", [96, T], B16) for _ in range(2)]
            MB = [alloc(cm, "MB", [96, T], B16) for _ in range(2)]
            bf, *bs = first_T([[(w[:, :, 3072:3088], 0, 0), (w[:, :, 3072:3184], 16, 0)], w[:, :, 0:128], w[:, :, 1024:1152]], XT, ready)
            early = dict(zip(("q0", "k0"), bs))
            with ExitStack() as c1:
                FZ, FT, FC = (alloc(c1, n, [32, T]) for n in ("FZ", "FT", "FC"))
                FB, FP = alloc(c1, "FB", [32, 1]), alloc(c1, "FP", [32, T], B16)
                l_fb = lane("l_fb")
                k_f = [AC.dma([], l_fb, act.dma_start, FB[16 * j:16 * j + 16, :], A["fox_b_f_2"].rearrange("o h -> h o"))
                       for j in range(2)][-1]
                v = VE.do([bf.tok, k_f], ve.tensor_scalar, FZ[:, :], bf.t[0:32, :], FB[:, 0:1], None, add)
                give(bf, v)
                v = log_sigmoid(FC[:, :], FZ[:, :], FT[:, :], 1.0, [v])
                one = VE.do([v], ve.memset, FT[:, :], 1.0)
                v = VE.do([v, one], ve.tensor_tensor_scan, FZ[:, :], FT[:, :], FC[:, :], 0.0, mult, add)
                for k in range(3):
                    v = VE.do([v], ve.tensor_copy, FP[:, :], FZ[:, :])
                    for j in range(2):
                        cb = VE.do([v], ve.tensor_scalar, CB[j][32 * k:32 * k + 32, :], FP[:, :],
                                   CST[0:32, C_FOX + 2 * j:C_FOX + 2 * j + 1], CST[0:32, C_FOX + 2 * j + 1:C_FOX + 2 * j + 2], mult, add)
                    if k < 2:
                        v = VE.do([v], ve.tensor_copy, FT[:, :], FP[:, :])
                        v = VE.do([v], ve.tensor_tensor, FZ[:, :], FZ[:, :], FT[:, :], sub)
            def queries(f):
                def run():
                    b = early.pop(f"q{f}", None) or proj_T(w[:, :, tile(f)], XT, ready)
                    e = AC.do([b.tok], act.mul, QT[:, f, :], b.t[:, :], 0.125)
                    give(b, e)
                    return e
                return (f"q{f}", run)

            def keys(f):
                def run():
                    b = early.pop(f"k{f}", None) or proj_T(w[:, :, 1024 + 128 * f:1152 + 128 * f], XT, ready)
                    e = VE.do([b.tok], ve.tensor_copy, KT[:, f, :], b.t[:, :])
                    give(b, e)
                    return e
                return (f"k{f}", run)

            def vals(c):
                def run():
                    toks = []
                    bs = proj_N(cut(w[:, :, 2048 + 512 * c:2560 + 512 * c], 512), 512, XT, ready)
                    for i, b in enumerate(bs):
                        toks.append(VE.do([b.tok], ve.tensor_copy, V[:, i, 512 * c:512 * c + 512], b.t[:, :]))
                        give(b, toks[-1])
                    return toks
                return (f"v{c}", run)

            gates = Gates(w[:, :, 3088:4112], ready, GT)
            jobs = [queries(0), keys(0), vals(0), gates.job(0)]
            for f in range(1, 8):
                jobs += [queries(f), keys(f)] + ([vals(1)] if f == 3 else []) + [gates.job(f)]
            fills = Fills(*jobs)
            fills.start(3)
            att, ob, mb_free, own = Attention(cm), [None], [None, None], {}

            def select(h):
                return VE.do([cb, mb_free[h % 2]], ve.tensor_scalar, MB[h % 2][:, :], CB[1][:, :],
                             CST[0:96, C_SEL + h:C_SEL + h + 1], None, mult)

            def score(h):
                s = h % 2
                m = own.pop(h) if h else select(0)
                sc = att.scores(lambda i: QT[half(h), h // 2, tile(i)], lambda n: KT[half(h), h // 2, 0:n],
                                [fills.get(f"q{h // 2}"), fills.get(f"k{h // 2}"), m],
                                extra=[(lambda i: CB[0][:, tile(i)], lambda n: MB[s][:, 0:n])])
                mb_free[s] = PE.last()
                if h < 15:
                    own[h + 1] = select(h + 1)
                return sc

            def value(h, turned):
                if h % 2 == 0:
                    ob[0] = take()
                tk = att.values(turned, lambda j: V[:, j, 64 * h:64 * h + 64], ob[0].t[half(h), :],
                                [fills.get(f"v{h // 8}"), ob[0].free])
                if h % 2:
                    gates.output(h // 2, ob[0], tk, fills)

            heads(16, att.normalise, att.turn, score, value, fills, 6)
            logs()
            return outproj(by_rows(A["fox_w_out_2"][0]), XT, gates.out, ALPHA, norm)

        def stream(name, src, n, lhs, rdy, post):
            pieces = cut(src, n)
            kts, st = src.shape[1], {}

            def run(j):
                def f():
                    if j == 0:
                        st["b"] = [take() for _ in range(NT)]
                    a0 = sum(k for _, k in pieces[:j])
                    w, k = weight([(pieces[j][0], 0, 0)], n), pieces[j][1]
                    for i, b in enumerate(st["b"]):
                        for a in range(k):
                            tok = mm3(b.t[:, 0:n], pair(lhs, ALL, a0 + a, tile(i)), w(a, 0, n), a0 + a == 0,
                                      a0 + a == kts - 1, [w.ready, b.free, rdy[i]], sig=i == NT - 1 and a == k - 1)
                        b.tok = tok
                    release(w, tok)
                    if j == len(pieces) - 1:
                        return [post(i, b) for i, b in enumerate(st["b"])]
                return f
            return [(name if j == len(pieces) - 1 else f"{name}.{j}", run(j)) for j in range(len(pieces))]

        def mix(ready, cm, make_norm):
            w = by_rows(A["w_in"][0])
            OB = [alloc(cm, "OB", [128, 4, T], R) for h in "hl"]
            with ExitStack() as c1:
                n = Nsa(w, ready, c1)
                done_b, tail_b = gla(w, ready, OB, n)
                settle()
                OA = [alloc(cm, "OA", [128, 4, T], R, side="right") for h in "hl"]
                done_a = n.attend(OA, tail_b)
            settle()
            with ExitStack() as c1:
                MT = (alloc(c1, "MTh", [128, 8, T], R), alloc(c1, "MTl", [128, 8, T], R))
                sg = [alloc(c1, "sg", [128, T]) for _ in range(4)]
                wa, wb = by_rows(A["w_up_nsa"][0]), by_rows(A["w_up_gla"][0])
                used, toks = [None, None], []
                for f in range(8):
                    s = f % 2
                    ga, gb = sg[2 * s], sg[2 * s + 1]
                    b2 = proj_T(w[:, :, 3880 + 128 * f:4008 + 128 * f], XT, ready)
                    a2 = AC.do([b2.tok, used[s]], act.activation, gb[:, :], b2.t[:, :], ACT.Tanh, scale=0.5)
                    give(b2, a2)
                    b3 = proj_T(wa[:, :, tile(f)], OA, done_a)
                    v1 = VE.do([n.ga[f], b3.tok, used[s]], ve.scalar_tensor_tensor, ga[:, :], n.GA(f), 1.0, b3.t[:, :], add, mult)
                    give(b3, v1)
                    b4 = proj_T(wb[:, :, tile(f)], OB, done_b)
                    v2 = VE.do([a2, b4.tok], ve.scalar_tensor_tensor, gb[:, :], gb[:, :], 1.0, b4.t[:, :], add, mult)
                    give(b4, v2)
                    v = VE.do([v2], ve.tensor_tensor, ga[:, :], ga[:, :], gb[:, :], add)
                    a = AC.do([v], act.mul, MT[0][:, f, :], ga[:, :], 0.5)
                    used[s] = VE.do([a], ve.scalar_tensor_tensor, MT[1][:, f, :], ga[:, :], 0.5, MT[0][:, f, :].bitcast(F), mult, sub)
                    toks.append(used[s])
                    if f % 2:
                        k_x[f // 2] = AC.dma([v1], l_x[f // 2], act.dma_start, X[:, f // 2, :], x_in[:, f // 2, :])
                norm = make_norm(c1)
                logs()
                return outproj(by_rows(A["w_out"][0]), MT, toks, 1.0, norm)

        class Nsa:

            def __init__(self, w, ready, cm):
                self.w, self.ready, self.cm = w, ready, cm
                self.QR, self.QT = alloc(cm, "QR", [128, 4, T]), alloc(cm, "QT", [128, 4, T])
                self.KV = alloc(cm, "KV", [128, NT, T])
                self.KS = [alloc(cm, "KS", [128, T]) for _ in range(2)]
                self.GN = alloc(cm, "GN", [128, NT, 24])
                self.KC, self.VC = alloc(cm, "KC", [128, 32]), alloc(cm, "VC", [32, 2, 64])
                self.ga, self.c_tok = [None] * 8, []

            def GA(self, f):
                return X[:, f // 2, 512 * (f % 2):512 * (f % 2) + 512]

            def jobs(self, c1):
                w, ready, QR, QT, KV, KS = self.w, self.ready, self.QR, self.QT, self.KV, self.KS
                cos = CST[:, C_NROPE:C_NROPE + 32].rearrange("p (i c) -> p i c", c=8)
                sin = CST[:, C_NROPE + 32:C_NROPE + 64].rearrange("p (i c) -> p i c", c=8)
                KX, c2, c3 = [], ExitStack(), ExitStack()
                PF = [alloc(c1, "PF", [32, 128]) for _ in range(2)]
                W2 = [alloc(c1, "W2", [128, 64]) for _ in range(2)]
                HR, tn = [alloc(c1, "HR", [128, 128]) for _ in range(2)], alloc(c1, "tn", [128, 2, 64])
                HB, HC, HT = alloc(c1, "HB", [128, 4]), alloc(c1, "HC", [128, 4, 32]), alloc(c1, "HT", [128, 4, 32])
                Q4 = alloc(c2, "qn", [128, NT, T])
                qn = [Q4[:, i, :] for i in range(NT)]
                tm = alloc(c2, "tm", [128, 2, 256])
                lz = [lane(f"l_c{j}") for j in range(2)]
                kd = {}
                for j, nm in enumerate(("k", "v")):
                    for g in range(2):
                        AC.dma([], lz[j], act.dma_start, PF[j][:, 64 * g:64 * g + 64], A[f"cmp_pe_{nm}"][0])
                    kd[j] = AC.dma([], lz[j], act.dma_start, W2[j][:, :], A[f"cmp_{nm}_w2"][0])
                self.q_tok, self.qt_tok, self.k_tok, k_rot, q_read = [], [], [], [], []

                def q_out(i, b):
                    e = AC.do([b.tok], act.mul, qn[i].rearrange("p (a g d) -> p g a d", a=4, g=2),
                              b.t[:, :].rearrange("p (g a d) -> p g a d", a=4, g=2), 0.125)
                    give(b, e)
                    q_read.append(e)

                def turned(dst, out):
                    def f():
                        src = q_read if dst is QR else self.rot
                        for a in range(4):
                            b = take()
                            t = transposes([(qn[i][:, tile(a)], 128 * i) for i in range(NT)], b, src)
                            e = AC.do([t], act.copy, dst[:, a, :], b.t[:, :])
                            give(b, e)
                            out.append(e)
                        if dst is QR:
                            self.rot = turn_rows(Q4[:, :, :], 8, t)
                        else:
                            self.q_read = t
                            c2.close()
                    return f

                def turn_rows(x, h, after):
                    x = x.rearrange("p i (h c) -> p i h c", c=64)
                    cs = [y.unsqueeze(2).broadcast_to([128, NT, h, 8]) for y in (cos, sin)]
                    t2 = [(tm if h == 8 else tn)[:, u, :].rearrange("p (i h c) -> p i h c", i=NT, c=8) for u in range(2)]
                    x1, x2 = x[:, :, :, 0:8], x[:, :, :, 8:16]
                    return rope(x1, x2, x1, x2, cs[0], cs[1], t2[0], t2[1], after, VE.last())

                def kv_out(i, b):
                    v = VE.do([b.tok], ve.tensor_copy, KV[:, i, :], b.t[:, :])
                    give(b, v)
                    if i == NT - 1:
                        k_rot.extend(turn_rows(KV[:, :, c:c + 128], 2, v) for c in (0, 256))

                def keys():
                    for c in range(2):
                        b = take()
                        t = transposes([(KV[:, i, 256 * c:256 * c + 128], 128 * i) for i in range(NT)], b, k_rot)
                        e = VE.do([t], ve.tensor_copy, KS[c][:, :], b.t[:, :])
                        give(b, e)
                        self.k_tok.append(e)

                hb, kx = {}, {}

                def blocks_in(j):
                    def f():
                        b = proj_T(w[:, :, 512 + 128 * j:640 + 128 * j], XT, ready)
                        if j == 0:
                            KX.extend([alloc(c3, "KX", [128, 560], R) for h in "hl"] for _ in range(2))
                            KX.append(alloc(c3, "KF", [128, 560]))
                        KF = KX[2]
                        v = VE.do([self.q_read, kx.get("free")], ve.memset, KF[:, :], 0.0)
                        toks = []
                        for g in range(2):
                            for u in range(2):
                                o, i = KF[64 * u:64 * u + 64, 280 * g:280 * g + 256], b.t[64 * g:64 * g + 64, u:512:2]
                                toks.append(AC.do([b.tok, v], act.copy, o, i) if g else VE.do([b.tok, v], ve.tensor_copy, o, i))
                        give(b, toks)
                        b = take()
                        t = transposes([(PF[j][:, :], 0)], b, [kd[j]])
                        for g in range(2):
                            for u in range(2):
                                toks.append(VE.do([t, v], ve.tensor_copy, KF[64 * u:64 * u + 64, 280 * g + 264:280 * g + 280],
                                                  b.t[64 * g:64 * g + 64, u:32:2]))
                        give(b, toks)
                        kx["free"] = kx[j] = split([KX[j][0][:, :], KX[j][1][:, :]], KF[:, :], toks)
                        hb[j] = take()
                    return f

                def blocks_mid(j, l0):
                    def f():
                        w1 = A[f"cmp_{'kv'[j]}_w1"][0].rearrange("(l p) n -> p l n", p=128)
                        wt = weight([(w1[:, l0:l0 + 8, :], 0, 0)], 128)
                        b = hb[j]
                        for l in range(8):
                            lhs = [KX[j][h][:, l0 + l:l0 + l + 545:8] for h in range(2)]
                            tok = mm3(b.t[0:69, 0:128], lhs, wt(l, 0, 128), l0 + l == 0, l0 + l == 15,
                                      [wt.ready, b.free, kx[j]], sig=l == 7)
                        release(wt, tok)
                        if l0 == 8:
                            c = AC.do([tok], act.copy, HR[j][0:69, :], b.t[0:69, 0:128])
                            give(b, c)
                            hb[j] = c
                    return f

                def blocks_act(j):
                    def f():
                        b = take()
                        t = transposes([(HR[j][0:69, :], 0)], b, [hb[j]])
                        kx[j] = []
                        for g in range(2):
                            x = 2 * j + g
                            v = VE.do([t], ve.tensor_copy, HB[:, x:x + 1], b.t[:, 35 * g + 33:35 * g + 34])
                            v = VE.do([v], ve.tensor_scalar, HC[:, x, 0:31], b.t[:, 35 * g:35 * g + 31], HB[:, x:x + 1], None, add)
                            e = AC.do([v], act.activation, HT[:, x, 0:31], HC[:, x, 0:31], ACT.Tanh, scale=0.5)
                            kx[j].append(VE.do([e], ve.scalar_tensor_tensor, HC[:, x, 0:31], HT[:, x, 0:31], 1.0,
                                               HC[:, x, 0:31], add, mult))
                        give(b, kx[j])
                    return f

                def blocks_out():
                    for j in range(2):
                        for g in range(2):
                            x = 2 * j + g
                            b = take()
                            if j == 0:
                                o = b.t[64 * g:64 * g + 64, 0:31]
                                t = PE.do([kx[j], kd[j], b.free], pe.matmul, o, W2[0][:, :], HC[:, x, 0:31], start=True, stop=True)
                                dst = self.KC[64 * g:64 * g + 64, 0:31]
                            else:
                                o = b.t[0:31, 0:64]
                                t = PE.do([kx[j], kd[j], b.free], pe.matmul, o, HC[:, x, 0:31], W2[1][:, :], start=True, stop=True)
                                dst = self.VC[0:31, g, :]
                            c = VE.do([t], ve.tensor_scalar, dst, o, 0.5, None, mult)
                            give(b, c)
                            self.c_tok.append(c)
                    c3.close()

                return (stream("q", w[:, :, 0:512], 512, XT, ready, q_out)
                        + [("qr", turned(QR, self.q_tok))] + stream("kv", w[:, :, 768:1280], 512, XT, ready, kv_out)
                        + [("qt", turned(QT, self.qt_tok)), ("kt", keys), ("ck", blocks_in(0)), ("cv", blocks_in(1)),
                           ("ck0", blocks_mid(0, 0)), ("ck8", blocks_mid(0, 8)), ("cv0", blocks_mid(1, 0)),
                           ("cv8", blocks_mid(1, 8)), ("ca", blocks_act(0)), ("cb", blocks_act(1)), ("co", blocks_out)])

            def attend(self, OA, tail):
                w, ready, cm, QR, QT, KV, KS, GN, KC, VC = (self.w, self.ready, self.cm, self.QR, self.QT,
                                                                self.KV, self.KS, self.GN, self.KC, self.VC)
                ready_q, c_tok, g_tok = self.q_tok + self.qt_tok + self.k_tok, self.c_tok, self.g_tok
                att = Attention(cm)
                MC = alloc(cm, "MC", [128, 2, NT, 32])
                PC = [alloc(cm, "PC", [128, NT, 32]) for _ in range(2)]
                CT = [alloc(cm, "CT", [32, T]) for _ in range(2)]
                cs_ = [alloc(cm, "cs", [128, 16]) for _ in range(2)]
                k_mc = AC.dma([], lane("l_mc"), act.dma_start, MC[:, :, :, :],
                              A["cmask"].rearrange("p (u i n) -> p u i n", u=2, i=NT))
                c_free = [None, None]

                def gate(f):
                    def run():
                        b = proj_T(w[:, :, 2856 + 128 * f:2984 + 128 * f], XT, ready)
                        self.ga[f] = AC.do([b.tok], act.activation, self.GA(f), b.t[:, :], ACT.Tanh, scale=0.5)
                        give(b, self.ga[f])
                    return (f"m{f}", run)

                def compressed(h):
                    s, g = h % 2, h // 4
                    b = take()
                    for i in range(NT):
                        t = PE.do([b.free, ready_q, c_tok], pe.matmul, b.t[:, 32 * i:32 * i + 31],
                                  QR[64 * g:64 * g + 64, h % 4, tile(i)], KC[64 * g:64 * g + 64, 0:31], start=True, stop=True)
                    p, c = PC[s], cs_[s]
                    x = b.t[:, 0:128].rearrange("p (i n) -> p i n", i=NT)[:, :, 0:31]
                    v = VE.do([t, k_mc, c_free[s]], ve.tensor_tensor, p[:, :, 0:31], x, MC[:, 0, :, 0:31], mult)
                    give(b, v)
                    v = VE.do([v], ve.tensor_tensor, p[:, :, 0:31], p[:, :, 0:31], MC[:, 1, :, 0:31], add)
                    v = VE.do([v], ve.reduce_max, c[:, 0:4], p[:, :, 0:31], AX.X, negate=True)
                    v = VE.do([v], ve.tensor_tensor, p[:, :, 0:31], p[:, :, 0:31],
                              c[:, 0:4].unsqueeze(2).broadcast_to([128, NT, 31]), add)
                    return s, h, AC.do([v], act.activation, p[:, :, 0:31], p[:, :, 0:31], ACT.Exp)

                def c_norm(cp):
                    s, h, a = cp
                    p, c = PC[s], cs_[s]
                    v = VE.do([a], ve.reduce_sum, c[:, 4:8], p[:, :, 0:31], AX.X)
                    v = VE.do([v], ve.reciprocal, c[:, 8:12], c[:, 4:8])
                    v = VE.do([v, g_tok], ve.tensor_tensor, c[:, 8:12], c[:, 8:12], GN[:, :, 3 * h], mult)
                    v = VE.do([a], ve.tensor_tensor, p[:, :, 0:31], p[:, :, 0:31], MC[:, 0, :, 0:31], mult)
                    v = VE.do([v], ve.tensor_tensor, p[:, :, 0:31], p[:, :, 0:31],
                              c[:, 8:12].unsqueeze(2).broadcast_to([128, NT, 31]), mult)
                    return s, v

                def c_turn(cp):
                    s, v = cp
                    b = take()
                    t = transposes([(PC[s][:, i, 0:31], 128 * i) for i in range(NT)], b, [v])
                    c_free[s] = t
                    e = AC.do([t, ct_free[s]], act.copy, CT[s][0:31, :], b.t[0:31, :])
                    give(b, e)
                    return e

                ct_free = [None, None]
                jobs = [(h, c) for h in range(8) for c in range(2)]
                done, cp, ct, ob = [], {}, {}, [None]

                def score(x):
                    h, c = jobs[x]
                    if c == 0:
                        if h:
                            ct[h - 1] = c_turn(cp[h - 1])
                        cp[h] = compressed(h)
                    else:
                        cp[h] = c_norm(cp[h])
                    r = slice(64 * (h // 4), 64 * (h // 4) + 64)
                    return att.scores(lambda i: QT[r, h % 4, tile(i)], lambda n: KS[c][r, 0:n], [ready_q],
                                      gate=GN[:, :, 3 * h + 1 + c])

                def value(x, turned):
                    h, c = jobs[x]
                    g, s = h // 4, h % 2
                    if c == 0 and h % 2 == 0:
                        ob[0] = take()
                    o = ob[0].t[half(h), :]
                    if c == 0:
                        e = ct[h] if h in ct else c_turn(cp[h])
                    tk = att.values(turned, lambda j: KV[:, j, 256 * c + 128 + 64 * g:256 * c + 192 + 64 * g], o,
                                    [ob[0].free], start=c == 0, stop=c == 1)
                    if c == 0:
                        ct_free[s] = PE.do([e], pe.matmul, o, VC[0:31, g, :], CT[s][0:31, :], start=False, stop=False)
                    if c == 1 and h % 2:
                        d = split(pair(OA, ALL, h // 2, ALL), ob[0].t[:, :], tk)
                        give(ob[0], d)
                        done.append(d)

                fills = Fills(("tail", tail), *[gate(f) for f in range(8)])
                heads(16, att.normalise, att.turn, score, value, fills, 2)
                return done

        def gla(w, ready, OB, nsa):
            with ExitStack() as cm:
                def new(name, shape):
                    return alloc(cm, name, shape, side="right")

                GQ, GK = new("GQ", [128, 2, T]), new("GK", [128, 2, T])
                LR, W2, BC = new("LR", [16, T]), new("W2", [16, 256]), new("BC", [128, 2])
                MK = new("MK", [128, 8, 128])
                GG = new("GG", [128, 128])
                OD = new("OD", [128, 2, 6, 128])
                ss = new("ss", [128, 32])
                GV = [X[:, i // 2, 512 * (i % 2):512 * (i % 2) + 512] for i in range(NT)]
                GR = [X[:, 2 + i // 2, 512 * (i % 2):512 * (i % 2) + 512] for i in range(NT)]
                C, S, Z, EX, T1 = (new(n, [128, T])[:, :] for n in ("C", "S", "Z", "EX", "T1"))
                DG = new("DG", [128, 2, NT, 128])[:, :, :, :]
                E = [GB[:, 0, 0:512], GB[:, 0, 512:1024]]
                ON = GB[:, 1, :]
                bs = first_N(cut(w[:, :, 2344:2856], 512), 512, XT, ready)
                lz = [lane(f"l_gl{j}") for j in range(4)]
                kw = [AC.dma([], lz[0], act.dma_start, W2[:, :], A["gla_gate_w2"][0]),
                      [AC.dma([], lz[1], act.dma_start, BC[:, c:c + 1], A["gla_gate_b"][0, tile(c)].rearrange("(p o) -> p o", o=1))
                       for c in range(2)],
                      AC.dma([], lz[2], act.dma_start, GG[:, :], A["gla_norm"].broadcast_to([128, 128])),
                      AC.dma([], lz[3], act.dma_start, MK[:, :, :], A["cst"][:, C_GLA:C_END].rearrange("p (m n) -> p m n", m=8))]
                gg = VE.do([kw], ve.tensor_scalar, GG[:, :], GG[:, :], 0.5, None, mult)
                gr_tok = []
                for i, b in enumerate(bs):
                    a = AC.do([b.tok], act.activation, GR[i], b.t[:, :], ACT.Tanh, scale=0.5)
                    v = VE.do([a], ve.scalar_tensor_tensor, GR[i], GR[i], 1.0, b.t[:, :], add, mult)
                    give(b, v)
                    g4 = GR[i].rearrange("p (h v) -> p h v", h=4)
                    gr_tok.append(VE.do([v, gg], ve.tensor_tensor, g4, g4, GG[:, :].unsqueeze(1).broadcast_to([128, 4, 128]), mult))
                toks = []
                b = proj_T([(w[:, :, 1280:1312], 0, 0), (w[:, :, 2328:2424], 32, 0)], XT, ready)
                g = AC.do([b.tok], act.activation, S[0:24, :], b.t[0:24, :], ACT.Tanh, scale=0.5)
                e = AC.do([b.tok], act.copy, LR[:, :], b.t[32:48, :])
                give(b, e)
                g = VE.do([g], ve.tensor_scalar, S[0:24, :], S[0:24, :], 0.5, 0.5, mult, add)
                logs()
                v = None
                for dp in range(2):
                    b = take()
                    t = PE.do([b.free, kw, e], pe.matmul, b.t[:, :], W2[:, tile(dp)], LR[:, :], start=True, stop=True)
                    v = VE.do([t, v], ve.tensor_scalar, Z, b.t[:, :], BC[:, dp:dp + 1], None, add)
                    give(b, v)
                    v = log_sigmoid(E[dp], Z, T1, 1.0 / 16, [v])
                one = VE.do([v], ve.memset, T1, 1.0)
                for c in range(2):
                    b = proj_T(w[:, :, 1304 + 128 * c:1432 + 128 * c], XT, ready)
                    e = AC.do([b.tok], act.mul, GQ[:, c, :], b.t[:, :], 0.125)
                    give(b, e)
                    toks.append(e)
                    b = proj_T(w[:, :, 1560 + 128 * c:1688 + 128 * c], XT, ready)
                    e = AC.do([b.tok], act.copy, GK[:, c, :], b.t[:, :])
                    give(b, e)
                    toks.append(e)

                def gv_out(i, b):
                    e = AC.do([b.tok], act.copy, GV[i], b.t[:, :])
                    give(b, e)
                    return e

                b = take()
                t = transposes([(S[0:24, tile(i)], 128 * i) for i in range(NT)], b, [g])
                nsa.g_tok = VE.do([t], ve.tensor_copy, nsa.GN[:, :, :], b.t[:, :].rearrange("p (i c) -> p i c", c=128)[:, :, 0:24])
                give(b, nsa.g_tok)

                fills = Fills(*stream("gv", w[:, :, 1816:2328], 512, XT, ready, gv_out), *nsa.jobs(cm))
                points, at = 22, [0]

                def fill():
                    fills.share(at[0], points)
                    at[0] += 1

                done = []
                levels = (256, 128, 64, 32, 16, 8, 4, 2, 1)
                read = []
                for dp in range(2):
                    c_ok = one
                    for c in range(8):
                        cs = slice(64 * c, 64 * c + 64)
                        c_ok = VE.do([one], ve.tensor_tensor_scan, C[:, cs], T1[:, cs], E[dp][:, cs], 0.0, mult, add)
                    z0 = VE.do([read], ve.memset, DG, 0.0)
                    q, k = GQ[:, dp, :], GK[:, dp, :]
                    st = {"e": [c_ok, nsa.g_tok], "z": []}

                    def decays(m):
                        if m >= 128:
                            for c in range(T // m):
                                cs = slice(m * c, m * c + m)
                                ok = VE.do([st["e"], one], ve.tensor_tensor_scan, S[:, cs], T1[:, cs], E[dp][:, cs], 0.0, mult, add)
                            src = S
                        else:
                            src, ok = C, c_ok
                        s3 = src.rearrange("p (b u m) -> p b u m", u=2, m=m)
                        e3 = EX.rearrange("p (b u m) -> p b u m", u=2, m=m)
                        nb = T // (2 * m)
                        v1 = VE.do([ok, st["e"]], ve.tensor_tensor, e3[:, :, 0, :],
                                   s3[:, :, 0, m - 1:m].broadcast_to([128, nb, m]), s3[:, :, 0, :], sub)
                        if m >= 64:
                            v2 = VE.do([ok], ve.tensor_copy, e3[:, :, 1, :], s3[:, :, 1, :])
                        else:
                            v2 = VE.do([ok], ve.tensor_tensor, e3[:, :, 1, :], s3[:, :, 1, :],
                                       s3[:, :, 0, m - 1:m].broadcast_to([128, nb, m]), sub)
                        return AC.do([v1, v2], act.activation, EX, EX, ACT.Exp)

                    def decayed(m, a):
                        z3, e3, q3, k3 = (t.rearrange("p (b u m) -> p b u m", u=2, m=m) for t in (Z, EX, q, k))
                        v1 = VE.do([a, st["z"], toks], ve.tensor_tensor, z3[:, :, 0, :], e3[:, :, 0, :], k3[:, :, 0, :], mult)
                        v2 = VE.do([a], ve.tensor_tensor, z3[:, :, 1, :], e3[:, :, 1, :], q3[:, :, 1, :], mult)
                        st["e"] = [v1, v2]
                        return [v1, v2]

                    def into_DG(hh, b, t, mask):
                        v = VE.do([t, z0, kw], ve.copy_predicated, DG[:, hh, :, :],
                                  MK[:, mask, :].bitcast(I32).unsqueeze(1).broadcast_to([128, NT, 128]),
                                  b.t[:, :].rearrange("p (i t) -> p i t", i=NT))
                        give(b, v)
                        return v

                    ready_z = None
                    for li, m in enumerate((0,) + levels):
                        banks = [take(), take()]
                        if m == 0:
                            ps = [(slice(128 * i, 128 * i + 128), GK[:, dp, tile(i)], GQ[:, dp, tile(i)]) for i in range(NT)]
                        elif m == 256:
                            ps = [(slice(256 * s, 256 * s + 256), Z[:, tile(s)], Z[:, 256:512]) for s in range(2)]
                        elif m == 128:
                            ps = [(tile(s), Z[:, tile(2 * s)], Z[:, tile(2 * s + 1)]) for s in range(2)]
                        else:
                            ps = [(tile(i), Z[:, tile(i)], Z[:, tile(i)]) for i in range(NT)]
                        for o, l, r in ps:
                            for hh, b in enumerate(banks):
                                rs = slice(64 * hh, 64 * hh + 64)
                                b.tok = PE.do([b.free, ready_z if m else toks], pe.matmul, b.t[:, o], l[rs, :], r[rs, :],
                                              start=True, stop=True)
                        outs = [(hh, b, b.tok) for hh, b in enumerate(banks)]
                        t = b.tok
                        st["z"] = [t]
                        if li < 9:
                            a = decays(levels[li])
                        for hh, b, t in outs:
                            if m in (128, 256):
                                o, n = (OD[:, hh, 0:4, :], 4) if m == 256 else (OD[:, hh, 4:6, :], 2)
                                last_v = VE.do([t, read], ve.tensor_copy, o, b.t[:, 0:128 * n].rearrange("p (i t) -> p i t", i=n))
                                give(b, last_v)
                            else:
                                last_v = into_DG(hh, b, t, 7 if m == 0 else li - 3)
                        if li < 9:
                            ready_z = decayed(levels[li], a)
                        fill()
                    gv = fills.get("gv")
                    bs, read = [take(), take()], []
                    for i in range(NT):
                        b = bs[i // 2]
                        for hh in range(2):
                            for s in range(i + 1):
                                if s == i:
                                    l = DG[:, hh, i, :]
                                elif (s, i) in ((0, 1), (2, 3)):
                                    l = OD[:, hh, 4 + s // 2, :]
                                else:
                                    l = OD[:, hh, 2 * s + i - 2, :]
                                t = PE.do([b.free, last_v, gv], pe.matmul, b.t[:, 256 * (i % 2) + 128 * hh:256 * (i % 2) + 128 * hh + 128], l,
                                          GV[s][:, 256 * dp + 128 * hh:256 * dp + 128 * hh + 128], start=s == 0, stop=s == i)
                        b.tok = t
                    read = [t]
                    fill()
                    while dp and fills.jobs:
                        fills.one()
                    logs()
                    v = None
                    for j, b in enumerate(bs):
                        a = AC.do([b.tok, gb_free[0]], act.activation, ON[:, 512 * j:512 * j + 512], b.t[:, :], ACT.Square)
                        v = VE.do([a], ve.reduce_sum, ss[:, 4 * j:4 * j + 4],
                                  ON[:, 512 * j:512 * j + 512].rearrange("p (h v) -> p h v", h=4), AX.X)
                    r = rsqrt(ss[:, 8:16], ss[:, 0:8], 1.0 / 128, 1e-6, ss[:, 16:24], ss[:, 24:32], v)
                    vs = []
                    for j, b in enumerate(bs):
                        on = ON[:, 512 * j:512 * j + 512].rearrange("p (h v) -> p h v", h=4)
                        v = VE.do([r], ve.tensor_tensor, on, b.t[:, :].rearrange("p (h v) -> p h v", h=4),
                                  ss[:, 8 + 4 * j:12 + 4 * j].unsqueeze(2).broadcast_to([128, 4, 128]), mult)
                        give(b, v)
                        for i in (2 * j, 2 * j + 1):
                            o = ON[:, 256 * i:256 * i + 256]
                            vs.append(VE.do([v, gr_tok], ve.tensor_tensor, o, o, GR[i][:, 256 * dp:256 * dp + 256], mult))
                    fill()

                    def out(dp):
                        for hh in range(2):
                            b = take()
                            t = transposes([(ON[:, 256 * i + 128 * hh:256 * i + 128 * hh + 128], 128 * i) for i in range(NT)], b, vs)
                            d = split(pair(OB, ALL, 2 * dp + hh, ALL), b.t[:, :], t)
                            give(b, d)
                            done.append(d)
                        gb_free[0] = t
                    if dp == 0:
                        out(0)
                return done, lambda: out(1)

        def passed(norm, src):
            for i in range(NT):
                for c in range(2):
                    norm.part(i, c, src[i])
                norm.compute(i)
                if i > 0:
                    norm.finish(i - 1)
                    ahead.append(AC.slot())
            pending.append(lambda: norm.finish(NT - 1))
            return norm.toks

        logs()
        with ExitStack() as cm:
            ready = passed(RmsNorm(A["norm_mix"][0], cm, gt=k_g), k_x)
        with ExitStack() as cm:
            ready = mix(ready, cm, lambda c: RmsNorm(A["norm_ffn"][0], c))
        with ExitStack() as cm:
            ready = ffn(ready, cm, RmsNorm(A["norm_final"], cm, to_x=True))
        for n, f in enumerate((lambda *a: mla(0, *a), swa, fox, lambda *a: mla(1, *a))):
            with ExitStack() as cm:
                ready = f(ready, cm, LayerNorm(A["ln_g_2"][n], A["ln_b_2"][n], transposed=n < 3))
        settle()
        o_tok = []
        o_v = out.rearrange("o (i p) d -> p (o i) d", p=128)
        for i in range(NT):
            l_o = lane(f"l_o{i}")
            for c in range(2):
                cs = slice(512 * c, 512 * c + 512)
                tok = SP.dma([ready[i][c]], l_o, nc.sync.dma_start, o_v[:, i, cs], X[:, i, cs])
            o_tok.append(tok)
        SP.wait(*o_tok)

        block = top.enter_context(nc.Block())

        @block.sync
        def _(e):
            SP.play(e)

        @block.scalar
        def _(e):
            AC.play(e)

        @block.vector
        def _(e):
            VE.play(e)

        @block.gpsimd
        def _(e):
            PO.play(e)

        @block.tensor
        def _(e):
            PE.play(e)


def constants():
    c = np.zeros((128, C_END), np.float32)
    p = np.arange(128)
    c[:, C_ID:C_ID + 128] = np.eye(128)
    c[:, C_MASK:C_MASK + 128] = np.where(p[None, :] > p[:, None], -1e30, 0.0)
    dist = p[:, None] + 128 - np.arange(256)[None, :]
    c[:, C_DIST:C_DIST + 256] = np.where((dist >= 0) & (dist < 128), dist, 3e35)
    t = (np.arange(4)[None, :] * 128 + p[:, None]).astype(np.float32)
    inv = (np.float32(500000.0) ** (-np.arange(8, dtype=np.float32) / np.float32(8))).astype(np.float32)
    ang = (t[:, :, None] * inv).astype(np.float32)
    c[:, C_NROPE:C_NROPE + 32] = np.cos(ang).reshape(128, 32)
    c[:, C_NROPE + 32:C_NROPE + 64] = np.sin(ang).reshape(128, 32)
    inv = (np.float32(10000.0) ** (-np.arange(0, 32, 2, dtype=np.float32) / np.float32(32))).astype(np.float32)
    ang = (t[:, :, None] * inv).astype(np.float32)
    c[:, C_MROPE:C_MROPE + 64] = np.cos(ang).reshape(128, 64)
    c[:, C_MROPE + 64:C_MROPE + 128] = np.sin(ang).reshape(128, 64)
    for h in range(16):
        c[[16 * k + h for k in range(6)], C_SEL + h] = 1.0
    c[0:16, C_FOX:C_FOX + 4] = (1, 0, 0, 1)
    c[16:32, C_FOX:C_FOX + 4] = (0, 1, -1, 0)
    s, q = p[:, None], p[None, :]
    for i, m in enumerate((64, 32, 16, 8, 4, 2, 1)):
        c[:, C_GLA + 128 * i:C_GLA + 128 * i + 128] = (s // (2 * m) == q // (2 * m)) & (s // m % 2 == 0) & (q // m % 2 == 1)
    c[:, C_GLA + 896:C_GLA + 1024] = np.eye(128)
    seen = (16 * np.arange(32)[None, None, :] + 31 <= t[:, :, None]).astype(np.float32)
    m = np.stack([seen, (seen - 1) * np.float32(1e30)], 1).reshape(128, 256)
    return c, m


_OUT = (1, T, D)
_INS = ["x", "norm_mix", "w_in", "cmp_pe_k", "cmp_pe_v", "cmp_k_w1", "cmp_k_w2", "cmp_v_w1", "cmp_v_w2", "gla_gate_w2",
        "gla_gate_b", "gla_norm", "w_up_nsa", "w_up_gla", "w_out", "norm_ffn", "w_ffn_gate", "w_ffn_up", "w_ffn_down",
        "norm_final", "ln_g_2", "ln_b_2", "mla_w_in_2", "mla_q_norm_2", "mla_w_q_up_2", "mla_kv_norm_2",
        "mla_w_kv_up_2", "mla_w_out_2", "swa_w_in_2", "swa_sinks_2", "swa_w_out_2", "fox_w_in_2", "fox_b_f_2",
        "fox_w_out_2"]


def kernel(**inputs):
    import concourse.bacc as bacc
    from concourse.bass_utils import run_bass_kernel_spmd

    nc = bacc.Bacc("TRN2", target_bir_lowering=False, num_devices=1)
    cst, cmask = constants()
    arrays = {n: np.ascontiguousarray(inputs[n]) for n in _INS}
    arrays["cst"], arrays["cmask"] = cst, cmask
    aps = {n: nc.dram_tensor(f"in_{n}", a.shape, mybir.dt.from_np(a.dtype), kind="ExternalInput").ap()
           for n, a in arrays.items()}
    out = nc.dram_tensor("out_x", _OUT, F, kind="ExternalOutput").ap()
    program(nc, aps, out)
    r = run_bass_kernel_spmd(nc, [{f"in_{n}": a for n, a in arrays.items()}], core_ids=[0])
    return r.results[0]["out_x"]
```
